# Optimizing a Trainium2 kernel written in Bass

```python
import math
import jax, jax.numpy as jnp
from jax import lax
import numpy as np

D_MODEL = 1024
BATCH = 1
SEQ = 256
DEPTH = 1

GRID_W = 64
ATT_HEADS = 8
ATT_KV_HEADS = 2
ATT_HEAD_DIM = 64
ATT_WIDTH = ATT_HEADS * ATT_HEAD_DIM
ATT_KV_WIDTH = ATT_KV_HEADS * ATT_HEAD_DIM
ROPE_AXIS_DIM = ATT_HEAD_DIM // 2
ROPE_THETA = 10000.0
Q_BLOCK = 128
HG_HEADS = 4
HG_F_DIM = 128
HG_I_DIM = 128
HG_F_WIDTH = HG_HEADS * HG_F_DIM
HG_WIDTH = HG_HEADS * HG_I_DIM
HG_CHUNK = 64
MIN_FORGET = 1e-6
N_BRANCHES = 2
N_EXPERTS = 16
EC_CAPACITY_FACTOR = 2
EXPERT_FF = 2048
NORM_EPS = 1e-6

IN_SPLITS = (ATT_WIDTH, ATT_KV_WIDTH, ATT_KV_WIDTH,
             HG_F_WIDTH, HG_F_WIDTH, HG_F_WIDTH,
             HG_WIDTH, HG_WIDTH,
             N_BRANCHES * D_MODEL)
IN_WIDTH = sum(IN_SPLITS)


def rms_norm(x, w):
    xf = x.astype(jnp.float32)
    y = xf * lax.rsqrt(jnp.mean(xf * xf, axis=-1, keepdims=True) + NORM_EPS)
    return (y * w.astype(jnp.float32)).astype(x.dtype)

def axial_rope_tables(seq_len):
    rows = seq_len // GRID_W
    row_id = jnp.repeat(jnp.arange(rows, dtype=jnp.float32), GRID_W)
    col_id = jnp.tile(jnp.arange(GRID_W, dtype=jnp.float32), rows)
    inv_freq = ROPE_THETA ** (-jnp.arange(0, ROPE_AXIS_DIM, 2, dtype=jnp.float32) / ROPE_AXIS_DIM)
    ang = jnp.stack([row_id[:, None] * inv_freq, col_id[:, None] * inv_freq], axis=1)
    return jnp.cos(ang), jnp.sin(ang)

def apply_axial_rope(x, cos, sin):
    B, S, H, hd = x.shape
    xr = x.reshape(B, S, H, 2, 2, ROPE_AXIS_DIM // 2)
    x1, x2 = xr[..., 0, :], xr[..., 1, :]
    cs, sn = cos[None, :, None], sin[None, :, None]
    out = jnp.stack([x1 * cs - x2 * sn, x2 * cs + x1 * sn], axis=-2)
    return out.reshape(B, S, H, hd)

def blocked_bidirectional_gqa(q, k, v):
    B, S, _, _ = q.shape
    G = ATT_HEADS // ATT_KV_HEADS
    n_blk = S // Q_BLOCK
    qb = q.reshape(B, n_blk, Q_BLOCK, ATT_KV_HEADS, G, ATT_HEAD_DIM).transpose(1, 0, 3, 4, 2, 5)
    kt = k.transpose(0, 2, 1, 3)
    vt = v.transpose(0, 2, 1, 3)
    scale = ATT_HEAD_DIM ** -0.5

    def one_block(qblk):
        s = jnp.einsum('bhgqd,bhkd->bhgqk', qblk, kt) * scale
        p = jax.nn.softmax(s, axis=-1)
        return jnp.einsum('bhgqk,bhkd->bhgqd', p, vt)

    o = lax.map(one_block, qb)
    return o.transpose(1, 0, 4, 2, 3, 5).reshape(B, S, ATT_WIDTH)

def gla_chunk_scan(q, k, v, log_f):
    B, S, H, Dk = q.shape
    Dv = v.shape[-1]
    n = S // HG_CHUNK

    def to_chunks(a):
        return a.reshape(B, n, HG_CHUNK, H, a.shape[-1]).transpose(1, 0, 3, 2, 4)

    qc, kc, vc, gc = to_chunks(q), to_chunks(k), to_chunks(v), to_chunks(log_f)
    lower = jnp.tril(jnp.ones((HG_CHUNK, HG_CHUNK), dtype=bool))[:, :, None]
    lower_f = lower.astype(jnp.float32)

    def step(state, inp):
        qi, ki, vi, gi = inp
        b = jnp.cumsum(gi, axis=-2)
        o_inter = jnp.einsum('bhcd,bhde->bhce', qi * jnp.exp(b), state)
        diff = b[:, :, :, None, :] - b[:, :, None, :, :]
        decay = jnp.exp(jnp.where(lower, diff, 0.0)) * lower_f
        scores = jnp.einsum('bhid,bhjd,bhijd->bhij', qi, ki, decay)
        o_intra = jnp.einsum('bhij,bhje->bhie', scores, vi)
        b_last = b[:, :, -1:, :]
        new_state = (jnp.exp(b_last[:, :, 0, :])[..., None] * state
                     + jnp.einsum('bhcd,bhce->bhde', ki * jnp.exp(b_last - b), vi))
        return new_state, o_inter + o_intra

    init = jnp.zeros((B, H, Dk, Dv), jnp.float32)
    _, o = lax.scan(step, init, (qc, kc, vc, gc))
    return o.transpose(1, 0, 3, 2, 4).reshape(B, S, H, Dv)

def hgrn2_forget(z, lb):
    f = lb + (1.0 - lb) * jax.nn.sigmoid(z)
    log_f = jnp.log(jnp.maximum(f, MIN_FORGET))
    one_minus_f = (1.0 - lb) * jax.nn.sigmoid(-z)
    return log_f, one_minus_f

def token_mixer(h, lb, w_in, q_norm_w, k_norm_w, hg_norm_w, w_branch_att, w_branch_hg, w_out,
                rope_cos, rope_sin):
    B, S, D = h.shape
    f32 = jnp.float32
    split_idx = np.cumsum(IN_SPLITS)[:-1].tolist()
    proj = jnp.einsum('bsd,de->bse', h, w_in)
    aq, ak, av, hq, hz_f, hz_b, hi, hgate, gate_logits = jnp.split(proj, split_idx, axis=-1)

    q = aq.astype(f32).reshape(B, S, ATT_HEADS, ATT_HEAD_DIM)
    k = ak.astype(f32).reshape(B, S, ATT_KV_HEADS, ATT_HEAD_DIM)
    v = av.astype(f32).reshape(B, S, ATT_KV_HEADS, ATT_HEAD_DIM)
    q = apply_axial_rope(rms_norm(q, q_norm_w), rope_cos, rope_sin)
    k = apply_axial_rope(rms_norm(k, k_norm_w), rope_cos, rope_sin)
    o_att = blocked_bidirectional_gqa(q, k, v)

    lb = lb.astype(f32)
    hqh = jax.nn.silu(hq.astype(f32)).reshape(B, S, HG_HEADS, HG_F_DIM)
    hv = hi.astype(f32).reshape(B, S, HG_HEADS, HG_I_DIM)
    logf_f, kf = hgrn2_forget(hz_f.astype(f32), lb[0])
    logf_b, kb = hgrn2_forget(hz_b.astype(f32), lb[1])
    shp = (B, S, HG_HEADS, HG_F_DIM)
    o_fwd = gla_chunk_scan(hqh, kf.reshape(shp), hv, logf_f.reshape(shp))
    flip = lambda a: jnp.flip(a, axis=1)
    o_bwd = flip(gla_chunk_scan(flip(hqh), flip(kb.reshape(shp)), flip(hv), flip(logf_b.reshape(shp))))
    o_h = rms_norm(o_fwd + o_bwd, hg_norm_w) * jax.nn.silu(
        hgate.astype(f32).reshape(B, S, HG_HEADS, HG_I_DIM))
    o_hg = o_h.reshape(B, S, HG_WIDTH)

    ya = jnp.einsum('bsw,wd->bsd', o_att.astype(h.dtype), w_branch_att)
    yh = jnp.einsum('bsw,wd->bsd', o_hg.astype(h.dtype), w_branch_hg)
    g = jax.nn.sigmoid(gate_logits.astype(f32)).reshape(B, S, N_BRANCHES, D)
    merged = (g[:, :, 0] * ya.astype(f32) + g[:, :, 1] * yh.astype(f32)).astype(h.dtype)
    return jnp.einsum('bsd,de->bse', merged, w_out)

def expert_choice_ffn(h, w_router, w_gate, w_up, w_down):
    B, S, D = h.shape
    cap = EC_CAPACITY_FACTOR * S // N_EXPERTS
    logits = jnp.einsum('bsd,de->bse', h.astype(jnp.float32), w_router.astype(jnp.float32))
    affinity = jax.nn.softmax(logits, axis=-1)
    top_w, top_idx = lax.top_k(affinity.transpose(0, 2, 1), cap)
    xe = jax.vmap(lambda hb, ib: hb[ib])(h, top_idx)
    hid = jax.nn.silu(jnp.einsum('becd,edf->becf', xe, w_gate)) * jnp.einsum('becd,edf->becf', xe, w_up)
    ye = jnp.einsum('becf,efd->becd', hid, w_down) * top_w[..., None].astype(h.dtype)
    combine = lambda yb, ib: jnp.zeros((S, D), h.dtype).at[ib.reshape(-1)].add(yb.reshape(-1, D))
    return jax.vmap(combine)(ye, top_idx)

def first_inputs(seed: int = 0) -> dict:
    key = jax.random.key(seed)
    ks = jax.random.split(key, 20)
    L, D = DEPTH, D_MODEL
    f32 = jnp.float32

    def nrm(k, shape, fan_in, scale=1.0):
        return jax.random.normal(k, shape, f32) * (scale * fan_in ** -0.5)

    def gain(k, shape):
        return 1.0 + 0.02 * jax.random.normal(k, shape, f32)

    return {
        "x": jax.random.normal(ks[0], (BATCH, SEQ, D), f32),
        "c": jax.random.normal(ks[1], (BATCH, D), f32),
        "ada_w": nrm(ks[2], (L, D, 6 * D), D, 0.5),
        "ada_b": 0.02 * jax.random.normal(ks[3], (L, 6 * D), f32),
        "norm_mix_w": gain(ks[4], (L, D)),
        "norm_ffn_w": gain(ks[5], (L, D)),
        "w_in": nrm(ks[6], (L, D, IN_WIDTH), D),
        "q_norm_w": gain(ks[7], (L, ATT_HEAD_DIM)),
        "k_norm_w": gain(ks[8], (L, ATT_HEAD_DIM)),
        "hg_lower_bounds": jax.random.normal(ks[9], (L, 2, HG_F_WIDTH), f32),
        "hg_norm_w": gain(ks[10], (L, HG_I_DIM)),
        "w_branch_att": nrm(ks[11], (L, ATT_WIDTH, D), ATT_WIDTH),
        "w_branch_hg": nrm(ks[12], (L, HG_WIDTH, D), HG_WIDTH),
        "w_out": nrm(ks[13], (L, D, D), D),
        "w_router": nrm(ks[14], (L, D, N_EXPERTS), D),
        "w_exp_gate": nrm(ks[15], (L, N_EXPERTS, D, EXPERT_FF), D),
        "w_exp_up": nrm(ks[16], (L, N_EXPERTS, D, EXPERT_FF), D),
        "w_exp_down": nrm(ks[17], (L, N_EXPERTS, EXPERT_FF, D), EXPERT_FF),
    }

def first_block(x, c, ada_w, ada_b, norm_mix_w, norm_ffn_w, w_in, q_norm_w, k_norm_w,
              hg_lower_bounds, hg_norm_w, w_branch_att, w_branch_hg, w_out, w_router,
              w_exp_gate, w_exp_up, w_exp_down):
    rope_cos, rope_sin = axial_rope_tables(x.shape[1])
    lb_soft = jax.nn.softmax(hg_lower_bounds.astype(jnp.float32), axis=0)
    lb_all = jnp.cumsum(lb_soft, axis=0) - lb_soft[0]
    c_act = jax.nn.silu(c)
    for l in range(DEPTH):
        mod = (jnp.einsum('bd,de->be', c_act, ada_w[l]) + ada_b[l])[:, None, :]
        shift1, scale1, gate1, shift2, scale2, gate2 = jnp.split(mod, 6, axis=-1)
        h = rms_norm(x, norm_mix_w[l]) * (1.0 + scale1) + shift1
        x = x + gate1 * token_mixer(h, lb_all[l], w_in[l], q_norm_w[l], k_norm_w[l], hg_norm_w[l],
                                    w_branch_att[l], w_branch_hg[l], w_out[l], rope_cos, rope_sin)
        h = rms_norm(x, norm_ffn_w[l]) * (1.0 + scale2) + shift2
        x = x + gate2 * expert_choice_ffn(h, w_router[l], w_exp_gate[l], w_exp_up[l], w_exp_down[l])
    return x


DEPTH_2 = 2

CHUNK = 64
N_A_LAYERS = DEPTH_2 // 2
N_B_LAYERS = DEPTH_2 - N_A_LAYERS
GMLP_BLOCK = 128
GMLP_WIDTH = D_MODEL
GMLP_GROUPS = 8
GMLP_GROUP_DIM = GMLP_WIDTH // GMLP_GROUPS
ATTN_HEADS = 16
HEAD_DIM = D_MODEL // ATTN_HEADS
LEFT_CHUNKS = 8
BAND_CHUNKS = LEFT_CHUNKS + 1
BAND = BAND_CHUNKS * CHUNK
REL_CLIP = 256
FFN_HIDDEN = 4 * D_MODEL
RMS_EPS = 1e-6
LN_EPS = 1e-5
NEG_INF = -1e30


def rms_norm_2(x, g):
    xf = x.astype(jnp.float32)
    y = xf * lax.rsqrt(jnp.mean(xf * xf, axis=-1, keepdims=True) + RMS_EPS)
    return (y * g.astype(jnp.float32)).astype(x.dtype)

def layer_norm(x, g, b):
    xf = x.astype(jnp.float32)
    mu = jnp.mean(xf, axis=-1, keepdims=True)
    xc = xf - mu
    var = jnp.mean(xc * xc, axis=-1, keepdims=True)
    y = xc * lax.rsqrt(var + LN_EPS) * g.astype(jnp.float32) + b.astype(jnp.float32)
    return y.astype(x.dtype)

def gmlp_spatial_gating(h, w_in, ln_g, ln_b, w_s, b_s, w_out):
    bsz, seq, _ = h.shape
    nblk = seq // GMLP_BLOCK
    uv = jax.nn.gelu(h @ w_in)
    u, v = jnp.split(uv, 2, axis=-1)
    v = layer_norm(v, ln_g, ln_b)
    v = v.reshape(bsz, nblk, GMLP_BLOCK, GMLP_GROUPS, GMLP_GROUP_DIM)
    chunk_id = jnp.arange(GMLP_BLOCK) // CHUNK
    mask = chunk_id[:, None] >= chunk_id[None, :]
    w_masked = jnp.where(mask[None], w_s, jnp.zeros((), w_s.dtype))
    sv = jnp.einsum('gij,bnjgd->bnigd', w_masked, v)
    sv = sv + jnp.transpose(b_s)[None, None, :, :, None]
    gate = sv.reshape(bsz, seq, GMLP_WIDTH)
    return (u * gate) @ w_out

def shared_kv_band(h, kv_norm_g, w_k, w_v):
    bsz, seq, _ = h.shape
    nc = seq // CHUNK
    hn = rms_norm_2(h, kv_norm_g)
    k = (hn @ w_k).reshape(bsz, nc, CHUNK, ATTN_HEADS, HEAD_DIM)
    v = (hn @ w_v).reshape(bsz, nc, CHUNK, ATTN_HEADS, HEAD_DIM)

    def band(t):
        tp = jnp.pad(t, ((0, 0), (LEFT_CHUNKS, 0), (0, 0), (0, 0), (0, 0)))
        tb = jnp.stack([tp[:, o:o + nc] for o in range(BAND_CHUNKS)], axis=2)
        return tb.reshape(bsz, nc, BAND, ATTN_HEADS, HEAD_DIM)

    key_chunk = jnp.arange(nc)[:, None] + jnp.arange(BAND_CHUNKS)[None, :] - LEFT_CHUNKS
    valid = jnp.repeat(key_chunk >= 0, CHUNK, axis=1)
    return band(k), band(v), valid

def relative_bias(table):
    q_pos = jnp.arange(CHUNK)[:, None] + LEFT_CHUNKS * CHUNK
    k_pos = jnp.arange(BAND)[None, :]
    idx = jnp.clip(q_pos - k_pos, -REL_CLIP, REL_CLIP) + REL_CLIP
    return table[:, idx]

def chunk_band_attention(h, w_q, rel_table, w_o, k_band, v_band, valid):
    bsz, seq, _ = h.shape
    nc = seq // CHUNK
    q = (h @ w_q).reshape(bsz, nc, CHUNK, ATTN_HEADS, HEAD_DIM)
    s = jnp.einsum('bcqhd,bckhd->bchqk', q, k_band).astype(jnp.float32)
    s = s * (HEAD_DIM ** -0.5) + relative_bias(rel_table).astype(jnp.float32)[None, None]
    s = jnp.where(valid[None, :, None, None, :], s, NEG_INF)
    p = jax.nn.softmax(s, axis=-1).astype(h.dtype)
    o = jnp.einsum('bchqk,bckhd->bcqhd', p, v_band).reshape(bsz, seq, D_MODEL)
    return o @ w_o

def sq_relu_mlp(h, w_up, w_down):
    return jnp.square(jax.nn.relu(h @ w_up)) @ w_down

def second_inputs(seed: int = 0) -> dict:
    key = jax.random.key(seed)
    ks = jax.random.split(key, 16)
    nrm = jax.random.normal
    D, W, G, H = D_MODEL, GMLP_WIDTH, GMLP_GROUPS, ATTN_HEADS
    return {
        "x": nrm(ks[0], (BATCH, SEQ, D), jnp.float32),
        "norm_g": 1.0 + 0.1 * nrm(ks[1], (DEPTH_2, 4, D), jnp.float32),
        "a_w_in": nrm(ks[2], (N_A_LAYERS, D, 2 * W), jnp.float32) * D ** -0.5,
        "a_ln_g": 1.0 + 0.1 * nrm(ks[3], (N_A_LAYERS, W), jnp.float32),
        "a_ln_b": 0.02 * nrm(ks[4], (N_A_LAYERS, W), jnp.float32),
        "a_w_s": nrm(ks[5], (N_A_LAYERS, G, GMLP_BLOCK, GMLP_BLOCK), jnp.float32) * GMLP_BLOCK ** -0.5,
        "a_b_s": 1.0 + 0.1 * nrm(ks[6], (N_A_LAYERS, G, GMLP_BLOCK), jnp.float32),
        "a_w_out": nrm(ks[7], (N_A_LAYERS, W, D), jnp.float32) * W ** -0.5,
        "kv_norm_g": 1.0 + 0.1 * nrm(ks[8], (D,), jnp.float32),
        "w_k": nrm(ks[9], (D, D), jnp.float32) * D ** -0.5,
        "w_v": nrm(ks[10], (D, D), jnp.float32) * D ** -0.5,
        "b_w_q": nrm(ks[11], (N_B_LAYERS, D, D), jnp.float32) * D ** -0.5,
        "b_rel_bias": 0.5 * nrm(ks[12], (N_B_LAYERS, H, 2 * REL_CLIP + 1), jnp.float32),
        "b_w_o": nrm(ks[13], (N_B_LAYERS, D, D), jnp.float32) * D ** -0.5,
        "w_up": nrm(ks[14], (DEPTH_2, D, FFN_HIDDEN), jnp.float32) * D ** -0.5,
        "w_down": nrm(ks[15], (DEPTH_2, FFN_HIDDEN, D), jnp.float32) * FFN_HIDDEN ** -0.5,
    }

def second_block(x, norm_g, a_w_in, a_ln_g, a_ln_b, a_w_s, a_b_s, a_w_out,
              kv_norm_g, w_k, w_v, b_w_q, b_rel_bias, b_w_o, w_up, w_down):
    h = x
    k_band = v_band = valid = None
    for layer in range(DEPTH_2):
        g = norm_g[layer]
        if layer < N_A_LAYERS:
            m = gmlp_spatial_gating(rms_norm_2(h, g[0]), a_w_in[layer], a_ln_g[layer],
                                    a_ln_b[layer], a_w_s[layer], a_b_s[layer], a_w_out[layer])
        else:
            if layer == N_A_LAYERS:
                k_band, v_band, valid = shared_kv_band(h, kv_norm_g, w_k, w_v)
            j = layer - N_A_LAYERS
            m = chunk_band_attention(rms_norm_2(h, g[0]), b_w_q[j], b_rel_bias[j], b_w_o[j],
                                     k_band, v_band, valid)
        h = h + rms_norm_2(m, g[1])
        f = sq_relu_mlp(rms_norm_2(h, g[2]), w_up[layer], w_down[layer])
        h = h + rms_norm_2(f, g[3])
    return h


def setup_inputs(seed=0):
    out = dict(first_inputs(seed))
    for name, value in second_inputs(seed + 1).items():
        if name != "x":
            out[name + "_2"] = value
    return out


def reference(
    x, c, ada_w, ada_b, norm_mix_w, norm_ffn_w, w_in, q_norm_w, k_norm_w, hg_lower_bounds,
    hg_norm_w, w_branch_att, w_branch_hg, w_out, w_router, w_exp_gate, w_exp_up, w_exp_down,
    norm_g_2, a_w_in_2, a_ln_g_2, a_ln_b_2, a_w_s_2, a_b_s_2, a_w_out_2, kv_norm_g_2, w_k_2,
    w_v_2, b_w_q_2, b_rel_bias_2, b_w_o_2, w_up_2, w_down_2,
):
    x = first_block(
        x, c, ada_w, ada_b, norm_mix_w, norm_ffn_w, w_in, q_norm_w, k_norm_w, hg_lower_bounds,
        hg_norm_w, w_branch_att, w_branch_hg, w_out, w_router, w_exp_gate, w_exp_up, w_exp_down,
    )
    return second_block(
        x, norm_g_2, a_w_in_2, a_ln_g_2, a_ln_b_2, a_w_s_2, a_b_s_2, a_w_out_2, kv_norm_g_2,
        w_k_2, w_v_2, b_w_q_2, b_rel_bias_2, b_w_o_2, w_up_2, w_down_2,
    )


_drawn_inputs = setup_inputs


def setup_inputs(seed=0):
    import zlib

    import numpy as np

    out = dict(_drawn_inputs(seed))
    spreads = {}
    factors = {'ada_b': 3.686,
     'norm_mix_w': 8.0,
     'norm_ffn_w': 7.706,
     'q_norm_w': 8.0,
     'k_norm_w': 8.0,
     'hg_norm_w': 8.0,
     'a_ln_b_2': 133.734,
     'norm_g_2': 2.909,
     'a_ln_g_2': 27.558,
     'a_b_s_2': 24.627,
     'kv_norm_g_2': 6.173,
     'b_rel_bias_2': 2.816}
    for name, (base, spread) in spreads.items():
        noise = np.random.default_rng([zlib.crc32(name.encode()), seed]).standard_normal(out[name].shape)
        drawn = base * np.exp(spread * noise) if base else spread * noise
        out[name] = __import__('jax').numpy.asarray(drawn.astype(out[name].dtype))
    for name, factor in factors.items():
        out[name] = (out[name] * factor).astype(out[name].dtype)
    return out
```

```python
from contextlib import ExitStack

import concourse.bass as bass
from concourse import mybir

F32 = mybir.dt.float32
BF16 = mybir.dt.bfloat16
I32 = mybir.dt.int32
U32 = mybir.dt.uint32
ALU = mybir.AluOpType
ACT = mybir.ActivationFunctionType
AX = mybir.AxisListType.X

P = 128
S = 256
T = S // P
D = 1024
KD = D // P
NB = 512
SLOT = KD * NB
R = 6

AH, AHD = 8, 64
HG, HGD = 4, 128
LEVELS = 9
NE, CAP, FF = 16, 32, 2048
PER_EXPERT = 12
FFH = 4096
FJ = FFH // NB
BHEADS, BHD = 16, 64
EPS, LN_EPS, MIN_F = 1e-6, 1e-5, 1e-6
NEG = -1e30

C_ID, C_MASK, C_IOTA, C_TOK, C_ROPE, C_BD = 0, 128, 1024, 1280, 1282, 1410
C_END = 1922
V_C, V_NM, V_NF, V_GA0, V_GA2, V_GB0, V_GB2, V_KV, V_BS, V_LB, V_AB = (8 * i for i in range(11))

JOBS = (
    [("vecT", 1)]
    + [(j, 1) for j in ("ada0", "ada1", "adc0", "ada2", "adc1", "ada3", "adc2", "adc3")]
    + [("nT0a", 2), ("nT0b", 2)]
    + [("W0", 2), ("W1", 2), ("W2", 2), ("W3", 2), ("W4", 2), ("lv0", 2), ("W5", 2), ("lv1", 2), ("W6", 2)]
    + [("lv2", 2), ("qT", 2), ("kT", 1), ("lv3", 2), ("sc00", 2), ("sc01", 2), ("lv4", 2)]
    + [("PT00", 2), ("pv00", 1), ("PT01", 2), ("pv01", 1), ("sc10", 2), ("sc11", 2), ("lv5", 2)]
    + [("PT10", 2), ("pv10", 1), ("PT11", 2), ("pv11", 1), ("lv6", 2), ("lv7", 2), ("lv8", 2)]
    + [("ada4", 1), ("ada5", 1), ("og", 2), ("adr4", 1), ("adr5", 1)]
    + [("W7", 2), ("W8", 2), ("ohgT", 2), ("W9", 2), ("W10", 2)]
    + [("ada6", 1), ("ada7", 1), ("adc6", 1), ("adc7", 1), ("ya0", 2), ("ya1", 2), ("yh0", 2), ("yh1", 2)]
    + [("ada8", 1), ("ada9", 1), ("adc8", 1), ("adc9", 1), ("mTa", 2), ("mTb", 2), ("mo0", 2), ("mo1", 2)]
    + [("ada10", 1), ("ada11", 1), ("adr10", 1), ("adr11", 1)]
    + [("nT1a", 2), ("nT1b", 2), ("rt", 1), ("aT", 1), ("ic", 1), ("ib", 1)]
    + [("ga0", 2), ("ga1", 2), ("ga2", 2), ("ga3", 2)]
    + [("wsT", 2), ("nT2a", 2), ("nT2b", 2), ("v0", 2), ("v1", 2), ("u0", 2), ("u1", 2)]
    + [("sv0", 2), ("sv1", 2), ("pTa", 2), ("pTb", 2), ("am0", 2), ("am1", 2), ("nT3a", 2), ("nT3b", 2)]
    + [("nT4a", 2), ("nT4b", 2), ("bk0", 2), ("bk1", 2), ("bq0", 2), ("bq1", 2), ("bv0", 2), ("bv1", 2)]
    + [("bs0", 2), ("bs1", 2), ("bT0", 2), ("bo0", 1), ("bs2", 2), ("bT1", 2), ("bo1", 1), ("bs3", 2)]
    + [("bT2", 2), ("bo2", 1), ("bs4", 2), ("bT3", 2), ("bo3", 1), ("bs5", 2), ("bT4", 2), ("bo4", 1)]
    + [("bT5", 2), ("bo5", 1), ("bm0", 2), ("bm1", 2), ("nT5a", 2), ("nT5b", 2)]
)
JOB_AT = {name: i for i, (name, _) in enumerate(JOBS)}
DRAINED = [sum(n for j, (_, n) in enumerate(JOBS) if j % 4 == i % 4 and j <= i) for i in range(len(JOBS))]

FIRST_SLABS = (
    [(f"ada{i}", f"ada{i}") for i in range(4)]
    + [(f"W{i}", f"W{i}") for i in range(7)]
    + [("ada4", "ada4"), ("ada5", "ada5")]
    + [(f"W{i}", f"W{i}") for i in range(7, 11)]
    + [("ada6", "ada6"), ("ada7", "ada7"), ("att", "ya1"), ("hg", "yh1"), ("ada8", "ada8"), ("ada9", "ada9")]
    + [("out0", "mo0"), ("out1", "mo1"), ("ada10", "ada10"), ("ada11", "ada11")]
)
A_SLABS = [("v0", "v0"), ("v1", "v1"), ("u0", "u0"), ("u1", "u1"), ("am0", "am0"), ("am1", "am1")]
B_SLABS = [(j, j) for j in ("bk0", "bk1", "bq0", "bq1", "bv0", "bv1", "bm0", "bm1")]
N_FIRST = len(FIRST_SLABS)
N_EXPERT = NE * PER_EXPERT
AT_EXPERT = N_FIRST
AT_A = AT_EXPERT + N_EXPERT
AT_FFN = [AT_A + len(A_SLABS), AT_A + len(A_SLABS) + 2 * FJ + len(B_SLABS)]
AT_B = AT_FFN[0] + 2 * FJ
SLAB_AT = {name: i for i, (name, _) in enumerate(FIRST_SLABS)}
SLAB_AT |= {name: AT_A + i for i, (name, _) in enumerate(A_SLABS)}
SLAB_AT |= {name: AT_B + i for i, (name, _) in enumerate(B_SLABS)}
READER = {i: job for i, (_, job) in enumerate(FIRST_SLABS)}
READER |= {AT_A + i: job for i, (_, job) in enumerate(A_SLABS)}
READER |= {AT_B + i: job for i, (_, job) in enumerate(B_SLABS)}
W_COLS = {"W0": 768, "W1": 1280, "W2": 1792, "W3": 2304, "W4": 0, "W5": 512, "W6": 2816,
          "W7": 3328, "W8": 3840, "W9": 4352, "W10": 4864}
FFN_ORDER = [("up", 0)] + [x for j in range(1, FJ) for x in (("up", j), ("down", j - 1))] + [("down", FJ - 1)]


def build(nc, A, out):
    with ExitStack() as ctx:
        def sb(name, shape, dt=F32):
            return ctx.enter_context(nc.sbuf_tensor(name, shape, dt))

        def sem(name):
            return ctx.enter_context(nc.semaphore(name))

        PS = ctx.enter_context(nc.psum_tensor("PS", [P, 8, NB], F32))

        ring = sb("ring", [P, R, SLOT])
        x = sb("x", [P, T, D])
        xn = sb("xn", [P, T, D])
        hT = sb("hT", [P, KD, S])
        consts = sb("consts", [P, C_END])
        vrow = sb("vrow", [P, P])
        vcol = sb("vcol", [P, P])
        modc = sb("modc", [P, 48])
        aff1 = sb("aff1", [P, KD])
        aff2 = sb("aff2", [P, KD])
        crep = sb("crep", [P, KD, 32])
        csil = sb("csil", [P, KD])
        wrt = sb("wrt", [P, KD, NE])
        mean32 = sb("mean32", [P, P])
        ones16 = sb("ones16", [16, P])
        zrow = sb("zrow", [1, P + NB], BF16)
        junk = sb("junk", [P, D], BF16)
        tmp = sb("tmp", [P, D])
        gate2 = sb("gate2", [P, D])
        ssq = sb("ssq", [P, 6, T])
        std = sb("std", [P, 6, T])
        rstd = sb("rstd", [P, 6, T])
        small = sb("small", [P, 256])
        arena = sb("arena", [P, 16 * 1024])

        def at(kb, cols):
            return arena[:, kb * 256:kb * 256 + cols]

        ident = consts[:, C_ID:C_ID + P]
        masks = consts[:, C_MASK:C_MASK + 7 * P].bitcast(I32)
        iota = consts[:, C_IOTA:C_IOTA + S]
        rope = consts[:, C_ROPE:C_ROPE + 128].rearrange("p (t f a i) -> p t f a i", t=T, f=2, a=2)
        blockdiag = consts[0:16, C_BD:C_BD + NE * CAP].rearrange("p (e c) -> p e c", e=NE)

        part = at(32, 2 * NB).rearrange("p (b n) -> p b n", b=2)
        gq = at(0, 1024).rearrange("p (h s) -> p h s", h=HG)
        gkf = at(4, 1024).rearrange("p (h s) -> p h s", h=HG)
        gkb = at(8, 1024).rearrange("p (h s) -> p h s", h=HG)
        PF = at(12, 1024).rearrange("p (h s) -> p h s", h=HG)
        XF = at(16, 1024).rearrange("p (h s) -> p h s", h=HG)
        PB = at(20, 1024).rearrange("p (h s) -> p h s", h=HG)
        XB = at(24, 1024).rearrange("p (h s) -> p h s", h=HG)
        EK = at(28, 1024).rearrange("p (h s) -> p h s", h=HG)
        EQ = at(32, 1024).rearrange("p (h s) -> p h s", h=HG)
        AT = at(36, 2048).rearrange("p (j i h s) -> p j i h s", j=T, i=T, h=HG)
        gv = at(44, 1024).rearrange("p (t n) -> p t n", t=T)
        hgate = at(48, 1024).rearrange("p (t n) -> p t n", t=T)
        qk = at(52, 1280).rearrange("p (t n) -> p t n", t=T)
        va = at(57, 256).rearrange("p (t n) -> p t n", t=T)
        aqT = at(58, 1024).rearrange("p (i s) -> p i s", i=4)
        akT = at(62, 256)
        wqk = at(63, 128)
        hgw = at(63, 256)[:, P:2 * P]
        oattT = at(52, 1024).rearrange("p (i s) -> p i s", i=4)
        prob = [xn[:, b, :].rearrange("p (i s) -> p i s", i=4) for b in range(2)]
        ptr = tmp[:, :].rearrange("p (k i s) -> p k i s", k=2, i=4)
        ohg = at(0, 1024).rearrange("p (t n) -> p t n", t=T)
        ohgT = at(4, 1024).rearrange("p (i s) -> p i s", i=4)
        gate1 = at(8, 1024)
        gsig = at(12, 4096).rearrange("p (b t n) -> p b t n", b=2, t=T)
        merged = xn

        xeT = at(0, 4096).rearrange("p (k c) -> p k c", k=KD)
        onehot = at(16, 1024).rearrange("p (t c) -> p t c", t=T)
        xe = at(20, 256).rearrange("p (k c) -> p k c", k=KD)
        sg = at(21, 512)
        hid = at(23, 512)
        hidT = at(25, 512).rearrange("p (i m) -> p i m", i=4)
        ye = at(27, 1024).rearrange("p (n m) -> p n m", n=2)
        comb = at(31, 256)
        eprob = at(40, 32).rearrange("p (t e) -> p t e", t=T)
        etop = at(41, 256)
        eidx = at(42, 64)
        etop2 = at(43, 256)
        erep = at(44, 256).rearrange("p (a j c) -> p a j c", a=2, j=4)
        ebd = at(45, 512)
        ecol = at(47, 32).rearrange("p (a e) -> p a e", a=2)

        V = at(0, 2048).rearrange("p (t n) -> p t n", t=T)
        U = at(8, 2048).rearrange("p (t n) -> p t n", t=T)
        ws = at(16, 1024).rearrange("p (g j) -> p g j", g=8)
        wsT = at(20, 1024).rearrange("p (g i) -> p g i", g=8)
        lng = at(32, 1024)
        lnb = at(36, 1024)
        grow = at(28, 1024)
        rl = at(0, 1024)
        hidden = at(4, 3072).rearrange("p (b i s) -> p b i s", b=3, i=4)
        bias = at(48, 4096).rearrange("p (h m) -> p h m", h=BHEADS)
        hR = at(0, 2048).rearrange("p (k s) -> p k s", k=KD)
        bqT = at(8, 2048).rearrange("p (k s) -> p k s", k=KD)
        bkT = at(16, 2048).rearrange("p (k s) -> p k s", k=KD)
        vR = at(32, 2048).rearrange("p (t n) -> p t n", t=T)
        oT = at(0, 2048).rearrange("p (k s) -> p k s", k=KD)
        bp = [at(40, 1024), at(44, 1024)]
        bpt = at(24, 1024)

        psum_full = [sem(f"psum_full{i}") for i in range(4)]
        psum_drained = [sem(f"psum_drained{i}") for i in range(4)]
        slab_in = [sem(f"slab_in{i}") for i in range(R)]
        slot_passed = sem("slot_passed")
        slab_done = sem("slab_done")
        consts_in, vrow_in, x_in, rows_in, wrt_in = (sem(n) for n in ("consts_in", "vrow_in", "x_in", "rows_in", "wrt_in"))
        bias1_in, grow_in, ln_in, ws_in, bias_in, out_written = (
            sem(n) for n in ("bias1_in", "grow_in", "ln_in", "ws_in", "bias_in", "out_written"))
        filled = sem("filled")
        norm_ssq, norm_var, norm_std, xn_ready = (sem(n) for n in ("norm_ssq", "norm_var", "norm_std", "xn_ready"))
        x_ready = sem("x_ready")
        crep_ready, c_silu, lb_in, lb_exp, lb_ready, aff_ready = (
            sem(n) for n in ("crep_ready", "c_silu", "lb_in", "lb_exp", "lb_ready", "aff_ready"))
        sig_ready, forget_ready, log_in, log_ready, k_ready, q_ready = (
            sem(n) for n in ("sig_ready", "forget_ready", "log_in", "log_ready", "k_ready", "q_ready"))
        exp_ready, sums_ready, factors_ready = (sem(n) for n in ("exp_ready", "sums_ready", "factors_ready"))
        qk_copied, qk_var, qk_std, qk_rstd, qk_ready = (sem(n) for n in ("qk_copied", "qk_var", "qk_std", "qk_rstd", "qk_ready"))
        row_max, row_exp, prob_ready = (sem(n) for n in ("row_max", "row_exp", "prob_ready"))
        gate_silu, hgate_ready, o_ssq, o_var, o_std, ohg_ready = (
            sem(n) for n in ("gate_silu", "hgate_ready", "o_ssq", "o_var", "o_std", "ohg_ready"))
        merged_ready = sem("merged_ready")
        r_max, r_exp, r_ready, top_ready, pick_ready = (sem(n) for n in ("r_max", "r_exp", "r_ready", "top_ready", "pick_ready"))
        xe_ready, silu_ready, hid_ready, hid_turned, hidT_ready, ye_ready, comb_done = (
            sem(n) for n in ("xe_ready", "silu_ready", "hid_ready", "hid_turned", "hidT_ready", "ye_ready", "comb_done"))
        gelu_ready, ln_var, ln_std, ln_ready, prod_ready = (sem(n) for n in ("gelu_ready", "ln_var", "ln_std", "ln_ready", "prod_ready"))
        post_ssq, post_var, post_std = (sem(n) for n in ("post_ssq", "post_var", "post_std"))
        relu_ready, hidden_ready, mlp_done = (sem(n) for n in ("relu_ready", "hidden_ready", "mlp_done"))
        dve_step, act_step, pool_step = sem("dve_step"), sem("act_step"), sem("pool_step")
        grow_free, bias_masked = sem("grow_free"), sem("bias_masked")

        X_MIX, X_EXP, X_GM, X_F0, X_AT, X_LAST = (2 * i for i in range(1, 7))

        def pair(job):
            return JOB_AT[job] % 4

        def banks(job):
            p = 2 * pair(job)
            return PS[:, p:p + 2, :]

        def bank(job, b):
            return PS[:, 2 * pair(job) + b, :]

        def wait_full(eng, job):
            eng.wait_ge(psum_full[pair(job)], JOB_AT[job] // 4 + 1)

        def wait_drained(eng, job):
            eng.wait_ge(psum_drained[pair(job)], DRAINED[JOB_AT[job]])

        def wait_slab(eng, n):
            before = sum(2 if m == SLAB_AT["att"] else 1 for m in range(n % R, n + 1, R))
            eng.wait_ge(slab_in[n % R], 16 * before)

        def slot_in(n):
            return 16 * sum(2 if m == SLAB_AT["att"] else 1 for m in range(n % R, n + 1, R))

        def slot(n):
            return ring[:, n % R, :]

        def kn(n, k=KD):
            return slot(n).rearrange("p (k n) -> p k n", k=k)

        def done_count(n):
            if n < AT_A:
                return n - AT_EXPERT + 1
            if n < AT_B:
                return N_EXPERT + n - AT_FFN[0] + 1
            return N_EXPERT + 2 * FJ + n - AT_FFN[1] + 1

        def split(ap, s):
            v = ap.rearrange("p h s -> p (h s)").rearrange("p (m a s) -> p a m s", a=2, s=s)
            return v[:, 0], v[:, 1]

        def hankel(table):
            v = table[0, :, 129:129 + S]
            return bass.AP(tensor=v.tensor, offset=v.offset, ap=[[1, P], [table.shape[2], BHEADS], [1, S]])

        block = ctx.enter_context(nc.Block())

        @block.sync
        def _(sp):
            def slab_free(n):
                if n < R:
                    return
                if n - R in READER:
                    wait_full(sp, READER[n - R])
                else:
                    sp.wait_ge(slab_done, done_count(n - R))

            def load(n, src, k=KD, dst=None):
                slab_free(n)
                sp.dma_start(kn(n, k) if dst is None else dst, src).then_inc(slab_in[n % R], 16)

            def columns(w, n0, width=NB):
                return w[:, n0:n0 + width].rearrange("(k p) n -> p k n", p=P)

            sp.dma_start(vrow[V_AB:V_AB + 48, :], A["ada_b"][0].rearrange("(k p) -> k p", p=P)).then_inc(vrow_in, 16)
            for v, src in ((V_C, A["c"][0]), (V_NM, A["norm_mix_w"][0]), (V_NF, A["norm_ffn_w"][0]),
                           (V_GA0, A["norm_g_2"][0, 0]), (V_GA2, A["norm_g_2"][0, 2]),
                           (V_GB0, A["norm_g_2"][1, 0]), (V_GB2, A["norm_g_2"][1, 2]), (V_KV, A["kv_norm_g_2"])):
                sp.dma_start(vrow[v:v + 8, :], src.rearrange("(k p) -> k p", p=P)).then_inc(vrow_in, 16)
            sp.dma_start(vrow[V_BS:V_BS + 8, :], A["a_b_s_2"][0]).then_inc(vrow_in, 16)
            sp.dma_start(vrow[V_LB:V_LB + 8, :],
                         A["hg_lower_bounds"][0].rearrange("a (h p) -> (a h) p", p=P)).then_inc(vrow_in, 16)
            for name, _ in FIRST_SLABS:
                n = SLAB_AT[name]
                if name.startswith("ada"):
                    load(n, columns(A["ada_w"][0], int(name[3:]) * NB))
                elif name == "W5":
                    load(n, columns(A["w_in"][0], W_COLS[name], 256), dst=kn(n)[:, :, 0:256])
                elif name.startswith("W"):
                    load(n, columns(A["w_in"][0], W_COLS[name]))
                elif name == "att":
                    for g in range(2):
                        src = A["w_branch_att"][0, g * 256:(g + 1) * 256, :].rearrange("(i d) n -> d i n", d=AHD)
                        load(n, src, dst=kn(n, 4)[64 * g:64 * g + 64])
                elif name == "hg":
                    load(n, A["w_branch_hg"][0].rearrange("(k p) n -> p k n", p=P), 4)
                else:
                    load(n, columns(A["w_out"][0], int(name[3:]) * NB))

            def expert_slab(e, i):
                if i < 8:
                    w = A["w_exp_gate"] if i < 4 else A["w_exp_up"]
                    return w[0, e, (i % 4) * 256:(i % 4 + 1) * 256, :].rearrange("(k p) n -> p k n", p=P), 2
                rows = A["w_exp_down"][0, e].rearrange("(j i p) n -> i p j n", j=4, p=P)
                return rows[i - 8], 4

            for i in range(R):
                load(AT_EXPERT + i, *expert_slab(0, i))
            with sp.Fori(0, NE - 1) as e:
                for i in range(PER_EXPERT):
                    ahead = R + i
                    sp.wait_ge(slab_done, e * PER_EXPERT + (i + 1))
                    sp.sem_inc(slot_passed, 1)
                    src, k = expert_slab(e + ahead // PER_EXPERT, ahead % PER_EXPERT)
                    sp.dma_start(kn(AT_EXPERT + ahead, k), src).then_inc(slab_in[(AT_EXPERT + ahead) % R], 16)
            for i in range(R, PER_EXPERT):
                load(AT_EXPERT + (NE - 1) * PER_EXPERT + i, *expert_slab(NE - 1, i))

            def mlp_slabs(layer):
                up, down = A["w_up_2"][layer], A["w_down_2"][layer]
                for i, (kind, j) in enumerate(FFN_ORDER):
                    if kind == "up":
                        load(AT_FFN[layer] + i, columns(up, j * NB))
                    else:
                        load(AT_FFN[layer] + i,
                             down[j * NB:(j + 1) * NB, :].rearrange("(k p) n -> p k n", p=P), 4)

            for name, _ in A_SLABS:
                w = A["a_w_out_2"] if name.startswith("am") else A["a_w_in_2"]
                load(SLAB_AT[name], columns(w[0], int(name[-1]) * NB + (D if name[0] == "v" else 0)))
            mlp_slabs(0)
            for name, _ in B_SLABS:
                w = {"bk": A["w_k_2"], "bv": A["w_v_2"], "bq": A["b_w_q_2"][0], "bm": A["b_w_o_2"][0]}[name[:2]]
                load(SLAB_AT[name], columns(w, int(name[-1]) * NB))
            mlp_slabs(1)
            sp.wait_ge(x_ready, X_LAST)
            sp.dma_start(out[0].rearrange("(t p) d -> p t d", p=P), x[:, :, :]).then_inc(out_written, 16)
            sp.wait_ge(out_written, 16)


        @block.gpsimd
        def _(pool):
            steps = [0]

            def link(ins):
                steps[0] += 1
                ins.then_inc(pool_step, 1)
                pool.wait_ge(pool_step, steps[0])

            pool.memset(mean32[:, :], 1.0 / 32).then_inc(filled, 1)
            pool.memset(ones16[:, :], 1.0).then_inc(filled, 1)
            pool.memset(zrow[:, :], 0.0).then_inc(filled, 1)
            pool.dma_start(wqk[:, 0:64], A["q_norm_w"][0].partition_broadcast(P)).then_inc(rows_in, 16)
            pool.dma_start(wqk[:, 64:128], A["k_norm_w"][0].partition_broadcast(P)).then_inc(rows_in, 16)
            pool.dma_start(hgw[:, :], A["hg_norm_w"][0].partition_broadcast(P)).then_inc(rows_in, 16)
            pool.dma_start(wrt[:, :, :], A["w_router"][0].rearrange("(k p) e -> p k e", p=P)).then_inc(wrt_in, 16)
            pool.dma_start(gate2[:, :], A["ada_b"][0, 5 * D:6 * D].partition_broadcast(P)).then_inc(bias1_in, 16)

            pool.wait_ge(lb_ready, 1)
            for d, (f, k) in enumerate(((PF, gkf), (PB, gkb))):
                wait_drained(pool, f"W{d + 1}")
                for h in range(HG):
                    c = d * HG + h
                    pool.tensor_scalar(f[:, h, :], f[:, h, :], small[:, 8 + c:9 + c], small[:, c:c + 1],
                                       ALU.mult, ALU.add).then_inc(forget_ready, 1)
                for h in range(HG):
                    c = d * HG + h
                    pool.tensor_scalar(k[:, h, :], k[:, h, :], small[:, 8 + c:9 + c], 0.0,
                                       ALU.mult, ALU.add).then_inc(k_ready, 1)
            pool.memset(XF, 0.0).then_inc(filled, 1)
            pool.memset(XB, 0.0).then_inc(filled, 1)

            pool.wait_ge(rows_in, 48)
            for t in range(T):
                pool.wait_ge(qk_rstd, t + 1)
                q10 = qk[:, t, :].rearrange("p (h d) -> p h d", d=AHD)
                link(pool.tensor_tensor(q10[:, 0:8, :], q10[:, 0:8, :],
                                        wqk[:, 0:64].unsqueeze(1).broadcast_to([P, 8, 64]), ALU.mult))
                link(pool.tensor_tensor(q10[:, 8:10, :], q10[:, 8:10, :],
                                        wqk[:, 64:128].unsqueeze(1).broadcast_to([P, 2, 64]), ALU.mult))
                halves = qk[:, t, :].rearrange("p (h a f i) -> p f h a i", h=10, a=2, f=2)
                x1, x2 = halves[:, 0], halves[:, 1]
                cos = rope[:, t, 0].unsqueeze(1).broadcast_to([P, 10, 2, 16])
                sin = rope[:, t, 1].unsqueeze(1).broadcast_to([P, 10, 2, 16])
                r = [xn[:, 0, i * 320:(i + 1) * 320].rearrange("p (h a i) -> p h a i", h=10, a=2) for i in range(3)]
                r.append(xn[:, 1, 0:320].rearrange("p (h a i) -> p h a i", h=10, a=2))
                pool.tensor_tensor(r[0], x1, cos, ALU.mult)
                pool.tensor_tensor(r[1], x2, sin, ALU.mult)
                pool.tensor_tensor(r[2], x2, cos, ALU.mult)
                link(pool.tensor_tensor(r[3], x1, sin, ALU.mult))
                pool.tensor_tensor(x1, r[0], r[1], ALU.subtract)
                pool.tensor_tensor(x2, r[2], r[3], ALU.add).then_inc(qk_ready, 1)
            wait_drained(pool, "W6")
            for t in range(T):
                g4 = hgate[:, t, :].rearrange("p (h d) -> p h d", h=HG)
                pool.tensor_tensor(g4, g4, hgw[:, :].unsqueeze(1).broadcast_to([P, HG, HGD]), ALU.mult)\
                    .then_inc(hgate_ready, 1)

            wait_full(pool, "lv8")
            pool.dma_start(gate1, A["ada_b"][0, 2 * D:3 * D].partition_broadcast(P)).then_inc(bias1_in, 16)

            wait_full(pool, "yh1")
            pool.dma_start(bias[:, :, :], hankel(A["b_rel_bias_2"])).then_inc(bias_in, 16)
            pool.wait_ge(bias_in, 16)
            pool.memset(bias[0:64, :, 0:64], NEG).then_inc(bias_masked, 1)
            wait_full(pool, "adr11")
            pool.dma_start(lng, A["a_ln_g_2"][0].partition_broadcast(P)).then_inc(ln_in, 16)
            pool.dma_start(lnb, A["a_ln_b_2"][0].partition_broadcast(P)).then_inc(ln_in, 16)
            pool.wait_ge(x_ready, X_EXP)
            pool.dma_start(ws, A["a_w_s_2"][0].rearrange("g i j -> i g j")).then_inc(ws_in, 16)
            for n, row in enumerate((A["norm_g_2"][0, 1], A["norm_g_2"][0, 3],
                                     A["norm_g_2"][1, 1], A["norm_g_2"][1, 3])):
                if n:
                    pool.wait_ge(grow_free, n)
                pool.dma_start(grow, row.partition_broadcast(P)).then_inc(grow_in, 16)

        @block.scalar
        def _(act):
            act.dma_start(consts[:, :], A["consts"]).then_inc(consts_in, 16)
            act.dma_start(x[:, :, :], A["x"][0].rearrange("(t p) d -> p t d", p=P)).then_inc(x_in, 16)

            def norm(n):
                for t in range(T):
                    if t:
                        act.wait_ge(norm_ssq, T * n + t)
                    act.activation(junk[:, :], x[:, t, :], ACT.Square, accum_out=ssq[:, n, t:t + 1])\
                        .then_inc(norm_ssq, 1)
                act.wait_ge(norm_var, n + 1)
                act.activation(std[:, n, :], ssq[:, n, :], ACT.Sqrt).then_inc(norm_std, 1)

            def turn_out(jobs, scale, shift=None, dst=hT, shifts=1):
                for half, job in enumerate(jobs):
                    wait_full(act, job)
                    for kk in (2, 3):
                        k = 4 * half + kk
                        ins = act.activation(dst[:, k, :], bank(job, 1)[:, (kk - 2) * S:(kk - 1) * S], ACT.Identity,
                                             scale=scale[:, k:k + 1], bias=shift[:, k:k + 1] if shift is not None else 0.0)
                    ins.then_inc(psum_drained[pair(job)], 1)

            def copy_out(job, dst, b):
                wait_full(act, job)
                act.activation(dst, bank(job, b), ACT.Copy).then_inc(psum_drained[pair(job)], 1)

            wait_full(act, "vecT")
            act.wait_ge(lb_in, 1)
            act.activation(small[:, 24:32], small[:, 16:24], ACT.Exp).then_inc(lb_exp, 1)
            act.activation(csil[:, :], vcol[:, V_C:V_C + 8], ACT.Silu).then_inc(c_silu, 1)
            act.wait_ge(x_in, 16)
            norm(0)
            act.wait_ge(aff_ready, 1)
            turn_out(("nT0a", "nT0b"), aff1, modc)

            wait_full(act, "W0")
            for b in range(2):
                act.activation(gq[:, 2 * b:2 * b + 2, :], bank("W0", b).rearrange("p (h s) -> p h s", h=2), ACT.Silu)\
                    .then_inc(psum_drained[pair("W0")], 1)
            for job, f, k in (("W1", PF, gkf), ("W2", PB, gkb)):
                wait_full(act, job)
                for b in range(2):
                    src = bank(job, b).rearrange("p (h s) -> p h s", h=2)
                    act.activation(f[:, 2 * b:2 * b + 2, :], src, ACT.Sigmoid)
                    act.activation(k[:, 2 * b:2 * b + 2, :], src, ACT.Sigmoid, scale=-1.0)\
                        .then_inc(psum_drained[pair(job)], 1)
            for d, f in enumerate((PF, PB)):
                act.wait_ge(log_in, d + 1)
                act.activation(f, f, ACT.Ln).then_inc(log_ready, 1)

            def levels(lv):
                s = 1 << (lv - 1)
                act.wait_ge(log_ready if lv == 1 else sums_ready, 2 if lv == 1 else lv - 1)
                if lv == 1:
                    act.wait_ge(filled, 5)
                wait_full(act, f"lv{lv - 1}")
                for dst, left, right in ((EQ, PB, PF), (EK, XF, XB)):
                    act.activation(split(dst, s)[0], split(left, s)[0], ACT.Exp)
                    ins = act.activation(split(dst, s)[1], split(right, s)[1], ACT.Exp)
                ins.then_inc(exp_ready, 1)

            def values():
                for t in range(T):
                    copy_out("W3", gv[:, t, :], t)
                wait_full(act, "W4")
                for t in range(T):
                    dst = qk[:, t, 0:512].rearrange("p (i g d) -> p g i d", i=4, g=2)
                    act.activation(dst, bank("W4", t).rearrange("p (g i d) -> p g i d", g=2, i=4), ACT.Copy)\
                        .then_inc(psum_drained[pair("W4")], 1)

            values()
            levels(1)
            wait_full(act, "W5")
            for t in range(T):
                act.activation(qk[:, t, 512:640], bank("W5", t)[:, 0:128], ACT.Copy)
                act.activation(va[:, t, :], bank("W5", t)[:, 128:256], ACT.Copy).then_inc(psum_drained[pair("W5")], 1)
            act.wait_ge(qk_var, 2)
            act.activation(small[:, 80:100], small[:, 60:80], ACT.Sqrt).then_inc(qk_std, 1)
            levels(2)
            wait_full(act, "W6")
            for t in range(T):
                act.activation(hgate[:, t, :], bank("W6", t), ACT.Silu).then_inc(psum_drained[pair("W6")], 1)
            levels(3)
            copy_out("qT", aqT[:, 2:4, :].rearrange("p i s -> p (i s)"), 1)
            levels(4)

            def softmax(n, job, units, width, scale, dst):
                act.wait_ge(row_max, n + 1)
                src = banks(job).rearrange("p b n -> p (b n)").rearrange("p (u w) -> p u w", u=units)
                for u in range(units):
                    ins = act.activation(dst[:, u, :], src[:, u, :], ACT.Exp, scale=scale,
                                         bias=small[:, 100 + 8 * (n % 2) + u:101 + 8 * (n % 2) + u],
                                         accum_out=small[:, 120 + 8 * (n % 2) + u:121 + 8 * (n % 2) + u])
                    if u == units // 2 - 1 or u == units - 1:
                        ins.then_inc(psum_drained[pair(job)], 1)

            def half_of_turned(job):
                copy_out(job, tmp[:, NB:D], 1)

            softmax(0, "sc00", 4, S, 0.125, prob[0])
            softmax(1, "sc01", 4, S, 0.125, prob[1])
            levels(5)
            half_of_turned("PT00")
            wait_full(act, "pv00")
            half_of_turned("PT01")
            softmax(2, "sc10", 4, S, 0.125, prob[0])
            softmax(3, "sc11", 4, S, 0.125, prob[1])
            levels(6)
            half_of_turned("PT10")
            half_of_turned("PT11")
            levels(7)
            levels(8)
            copy_out("lv8", AT[:, 1, 0].rearrange("p h s -> p (h s)"), 1)
            wait_full(act, "og")
            for t in range(T):
                for h in range(HG):
                    i = HG * t + h
                    ins = act.activation(junk[:, i * HGD:(i + 1) * HGD], bank("og", t)[:, h * HGD:(h + 1) * HGD], ACT.Square,
                                         accum_out=small[:, 140 + 4 * t + h:141 + 4 * t + h])
            ins.then_inc(o_ssq, 1)
            act.wait_ge(o_var, 1)
            act.activation(small[:, 150:158], small[:, 140:148], ACT.Sqrt).then_inc(o_std, 1)
            for job, b, n in (("W7", 0, 0), ("W8", 0, 1), (None, 0, 0), ("W9", 1, 0), ("W10", 1, 1)):
                if job is None:
                    copy_out("ohgT", ohgT[:, 2:4, :].rearrange("p i s -> p (i s)"), 1)
                    continue
                wait_full(act, job)
                for t in range(T):
                    act.activation(gsig[:, b, t, n * NB:(n + 1) * NB], bank(job, t), ACT.Sigmoid)\
                        .then_inc(psum_drained[pair(job)], 1)
            copy_out("mTa", hT[:, 2:4, :].rearrange("p k s -> p (k s)"), 1)
            copy_out("mTb", hT[:, 6:8, :].rearrange("p k s -> p (k s)"), 1)

            act.wait_ge(x_ready, X_MIX)
            norm(1)
            act.wait_ge(aff_ready, 2)
            turn_out(("nT1a", "nT1b"), aff2, modc[:, 24:32])
            act.wait_ge(r_max, 1)
            for t in range(T):
                ins = act.activation(eprob[:, t, :], bank("rt", 0)[:, t * NE:(t + 1) * NE], ACT.Exp,
                                     bias=small[:, 160 + t:161 + t], accum_out=small[:, 162 + t:163 + t])
            ins.then_inc(r_exp, 1)
            for q in range(4):
                job = f"ga{q}"
                wait_full(act, job)
                k = 2 * q + 1
                act.activation(xeT[:, k, :], bank(job, 1), ACT.Identity, scale=aff2[:, k:k + 1],
                               bias=modc[:, 24 + k:25 + k]).then_inc(psum_drained[pair(job)], 1)

            with act.Fori(0, NE) as e:
                act.wait_ge(slab_done, e * PER_EXPERT + 4)
                act.activation(sg, PS[:, 0, :], ACT.Silu).then_inc(silu_ready, 1)
                act.wait_ge(hid_turned, e + 1)
                act.activation(hidT.rearrange("p i m -> p (i m)"), PS[:, 0, :], ACT.Copy).then_inc(hidT_ready, 1)
                act.wait_ge(slab_done, e * PER_EXPERT + 12)
                act.activation(ye[:, 0, :], PS[:, 2, :], ACT.Copy).then_inc(ye_ready, 1)

            copy_out("wsT", wsT[:, 4:8, :].rearrange("p g i -> p (g i)"), 1)
            act.wait_ge(x_ready, X_EXP)
            norm(2)
            turn_out(("nT2a", "nT2b"), vcol[:, V_GA0:V_GA0 + 8])
            for job, dst, n in (("v0", V, 0), ("v1", V, 1), ("u0", U, 0), ("u1", U, 1)):
                wait_full(act, job)
                for t in range(T):
                    act.activation(dst[:, t, n * NB:(n + 1) * NB], bank(job, t), ACT.Gelu_apprx_tanh)\
                        .then_inc(psum_drained[pair(job)], 1)
                if job == "v1":
                    act.wait_ge(ln_var, 1)
                    act.activation(small[:, 176:178], small[:, 172:174], ACT.Sqrt).then_inc(ln_std, 1)
            copy_out("pTa", hT[:, 2:4, :].rearrange("p k s -> p (k s)"), 1)
            copy_out("pTb", hT[:, 6:8, :].rearrange("p k s -> p (k s)"), 1)

            def post_norm(n, bank_of, ready):
                for half in range(2):
                    ready(half)
                    for t in range(T):
                        if half:
                            act.wait_ge(post_ssq, 4 * n + t + 1)
                        act.activation(junk[:, t * NB:(t + 1) * NB], bank_of(half, t), ACT.Square,
                                       accum_out=small[:, 180 + 2 * t + half:181 + 2 * t + half]).then_inc(post_ssq, 1)
                act.wait_ge(post_var, n + 1)
                act.activation(small[:, 188:190], small[:, 186:188], ACT.Sqrt).then_inc(post_std, 1)

            def mlp(layer):
                base = done_count(AT_FFN[layer]) - 1
                done = layer * FJ

                def relu(j, up):
                    act.wait_ge(slab_done, up)
                    if not (isinstance(j, int) and j == 0):
                        act.wait_ge(hidden_ready, j + done)
                    act.activation(rl, PS[:, 4:6, :].rearrange("p b n -> p (b n)"), ACT.Relu).then_inc(relu_ready, 1)

                relu(0, base + 1)
                with act.Fori(0, 2) as it:
                    for jj in range(1, 4):
                        relu(it * 3 + jj, it * 6 + (base + 2 * jj))
                relu(7, base + 14)

            post_norm(0, lambda h, t: bank(f"am{h}", t), lambda h: wait_full(act, f"am{h}"))
            act.wait_ge(x_ready, X_GM)
            norm(3)
            turn_out(("nT3a", "nT3b"), vcol[:, V_GA2:V_GA2 + 8])
            mlp(0)
            post_norm(1, lambda h, t: PS[:, 2 * t + h, :], lambda h: act.wait_ge(mlp_done, 1))
            act.wait_ge(x_ready, X_F0)
            norm(4)
            for half, job in enumerate(("nT4a", "nT4b")):
                wait_full(act, job)
                for kk in range(2):
                    k = 4 * half + 2 + kk
                    src = bank(job, 1)[:, kk * S:(kk + 1) * S]
                    act.activation(hT[:, k, :], src, ACT.Identity, scale=vcol[:, V_GB0 + k:V_GB0 + k + 1])
                    ins = act.activation(hR[:, k, ::-1], src, ACT.Identity, scale=vcol[:, V_KV + k:V_KV + k + 1])
                ins.then_inc(psum_drained[pair(job)], 1)
            for job, dst in (("bk0", bkT[:, 2:4]), ("bk1", bkT[:, 6:8]), ("bq0", bqT[:, 2:4]), ("bq1", bqT[:, 6:8])):
                copy_out(job, dst.rearrange("p k s -> p (k s)"), 1)
            for n in range(2):
                copy_out(f"bv{n}", vR[:, 1, n * NB:(n + 1) * NB], 1)

            def b_softmax(n):
                units = 8 if n < 2 else 4
                pr = bp[n % 2].rearrange("p (u w) -> p u w", u=units)
                act.wait_ge(row_max, 5 + n)
                for u in range(units):
                    ins = act.activation(pr[:, u, :], pr[:, u, :], ACT.Exp,
                                         bias=small[:, 100 + 8 * (n % 2) + u:101 + 8 * (n % 2) + u],
                                         accum_out=small[:, 120 + 8 * (n % 2) + u:121 + 8 * (n % 2) + u])
                ins.then_inc(row_exp, 1)

            def b_turned(n):
                copy_out(f"bT{n}", bpt[:, NB:D], 1)

            b_softmax(0)
            b_softmax(1)
            b_turned(0)
            b_softmax(2)
            b_turned(1)
            b_softmax(3)
            b_turned(2)
            b_softmax(4)
            b_turned(3)
            b_softmax(5)
            b_turned(4)
            b_turned(5)
            post_norm(2, lambda h, t: bank(f"bm{h}", t), lambda h: wait_full(act, f"bm{h}"))
            act.wait_ge(x_ready, X_AT)
            norm(5)
            turn_out(("nT5a", "nT5b"), vcol[:, V_GB2:V_GB2 + 8])
            mlp(1)
            post_norm(3, lambda h, t: PS[:, 2 * t + h, :], lambda h: act.wait_ge(mlp_done, 2))

        @block.vector
        def _(dve):
            steps = [0]

            def link(ins):
                steps[0] += 1
                ins.then_inc(dve_step, 1)
                dve.wait_ge(dve_step, steps[0])

            def norm(n):
                dve.wait_ge(norm_ssq, T * (n + 1))
                dve.tensor_scalar(ssq[:, n, :], ssq[:, n, :], 1.0 / D, EPS, ALU.mult, ALU.add).then_inc(norm_var, 1)
                dve.wait_ge(norm_std, n + 1)
                link(dve.reciprocal(rstd[:, n, :], std[:, n, :]))
                for t in range(T):
                    dve.tensor_scalar(xn[:, t, :], x[:, t, :], rstd[:, n, t:t + 1], None, ALU.mult)\
                        .then_inc(xn_ready, 1)

            def turn_out(jobs, scale, shift=None):
                for half, job in enumerate(jobs):
                    wait_full(dve, job)
                    for kk in (0, 1):
                        k = 4 * half + kk
                        src = bank(job, 0)[:, kk * S:(kk + 1) * S]
                        if shift is None:
                            ins = dve.tensor_scalar(hT[:, k, :], src, scale[:, k:k + 1], None, ALU.mult)
                        else:
                            ins = dve.tensor_scalar(hT[:, k, :], src, scale[:, k:k + 1], shift[:, k:k + 1],
                                                    ALU.mult, ALU.add)
                    ins.then_inc(psum_drained[pair(job)], 1)

            def copy_out(job, dst, b):
                wait_full(dve, job)
                dve.tensor_copy(dst, bank(job, b)).then_inc(psum_drained[pair(job)], 1)

            def ada_part(s):
                copy_out(f"ada{s}", part[:, s % 2, :], 0)

            def ada_col(s):
                job = f"adc{s}"
                wait_full(dve, job)
                dve.tensor_tensor(modc[:, 4 * s:4 * s + 4], bank(job, 0)[:, 0:4], vcol[:, V_AB + 4 * s:V_AB + 4 * s + 4],
                                  ALU.add).then_inc(psum_drained[pair(job)], 1)

            def ada_row(s, dst):
                job = f"adr{s}"
                wait_full(dve, job)
                dve.tensor_tensor(dst, dst, bank(job, 0), ALU.add).then_inc(psum_drained[pair(job)], 1)

            wait_full(dve, "vecT")
            link(dve.tensor_copy(vcol[:, :], bank("vecT", 0)[:, 0:P]))
            dve.tensor_tensor(small[:, 16:24], vcol[:, V_LB:V_LB + 8], vcol[:, V_LB:V_LB + 8], ALU.subtract)\
                .then_inc(lb_in, 1)
            dve.sem_inc(psum_drained[pair("vecT")], 1)
            dve.wait_ge(c_silu, 1)
            for k in range(KD):
                ins = dve.tensor_copy(crep[:, k, :], csil[:, k:k + 1].broadcast_to([P, 32]))
            ins.then_inc(crep_ready, 1)
            dve.wait_ge(lb_exp, 1)
            link(dve.reciprocal(small[:, 32:40], small[:, 24:32]))
            link(dve.tensor_tensor(small[:, 32:40], small[:, 24:32], small[:, 32:40], ALU.mult))
            link(dve.tensor_tensor(small[:, 0:8], small[:, 32:40], small[:, 32:40], ALU.subtract))
            dve.tensor_scalar(small[:, 8:16], small[:, 0:8], -1.0, 1.0, ALU.mult, ALU.add).then_inc(lb_ready, 1)
            norm(0)
            ada_part(0)
            ada_part(1)
            ada_col(0)
            ada_part(2)
            ada_col(1)
            ada_part(3)
            ada_col(2)
            ada_col(3)
            wait_drained(dve, "adc3")
            wait_drained(dve, "adc2")
            dve.scalar_tensor_tensor(out=aff1[:, :], in0=modc[:, 8:16], scalar=1.0, in1=vcol[:, V_NM:V_NM + 8],
                                     op0=ALU.add, op1=ALU.mult).then_inc(aff_ready, 1)
            dve.wait_ge(aff_ready, 1)
            turn_out(("nT0a", "nT0b"), aff1, modc)

            def factors(lv):
                s = 1 << (lv - 1)
                dve.wait_ge(exp_ready, lv)
                if lv == 1:
                    dve.wait_ge(k_ready, 8)
                for src, dst, side in ((gkf, EK, 0), (gkb, EK, 1)):
                    dve.tensor_tensor(split(dst, s)[side], split(dst, s)[side], split(src, s)[side], ALU.mult)
                dve.tensor_tensor(EQ, EQ, gq, ALU.mult).then_inc(factors_ready, 1)
                if lv < LEVELS - 1:
                    (pfl, pfr), (xfl, _) = split(PF, s), split(XF, s)
                    (pbl, pbr), (_, xbr) = split(PB, s), split(XB, s)
                    m = HG * S // (2 * s)
                    wide = [P, m, s]
                    dve.tensor_tensor(xfl, xfl, pfr[:, :, s - 1:s].broadcast_to(wide), ALU.add)
                    link(dve.tensor_tensor(xbr, xbr, pbl[:, :, 0:1].broadcast_to(wide), ALU.add))
                    dve.tensor_tensor(pfr, pfr, pfl[:, :, s - 1:s].broadcast_to(wide), ALU.add)
                    dve.tensor_tensor(pbl, pbl, pbr[:, :, 0:1].broadcast_to(wide), ALU.add).then_inc(sums_ready, 1)

            def scores(lv):
                job = f"lv{lv}"
                wait_full(dve, job)
                for t in range(T):
                    src = bank(job, t).rearrange("p (h s) -> p h s", h=HG)
                    if lv == 0:
                        dve.tensor_copy(AT[:, t, t], src).then_inc(psum_drained[pair(job)], 1)
                    else:
                        m = masks[:, (lv - 1) * P:lv * P].unsqueeze(1).broadcast_to([P, HG, P])
                        dve.copy_predicated(AT[:, t, t], m, src).then_inc(psum_drained[pair(job)], 1)
                    wait_drained(dve, job) if t else None

            for d, f in enumerate((PF, PB)):
                dve.wait_ge(forget_ready, 4 * d + 4)
                dve.tensor_scalar(f, f, MIN_F, None, ALU.max).then_inc(log_in, 1)
            dve.wait_ge(k_ready, 8)
            wait_drained(dve, "W0")
            dve.tensor_tensor(EK, gkf, gkb, ALU.add)
            dve.tensor_copy(EQ, gq).then_inc(factors_ready, 1)
            scores(0)
            factors(1)

            wait_drained(dve, "W4")
            wait_drained(dve, "W5")
            for t in range(T):
                sq = tmp[:, 0:640]
                link(dve.tensor_tensor(sq, qk[:, t, :], qk[:, t, :], ALU.mult))
                link(dve.tensor_reduce(small[:, 60 + 10 * t:70 + 10 * t], sq.rearrange("p (h d) -> p h d", h=10),
                                       AX, ALU.add))
                dve.tensor_scalar(small[:, 60 + 10 * t:70 + 10 * t], small[:, 60 + 10 * t:70 + 10 * t],
                                  1.0 / AHD, EPS, ALU.mult, ALU.add).then_inc(qk_var, 1)
            scores(1)
            dve.wait_ge(qk_std, 1)
            link(dve.reciprocal(small[:, 40:60], small[:, 80:100]))
            for t in range(T):
                v = qk[:, t, :].rearrange("p (h d) -> p h d", h=10)
                dve.tensor_tensor(v, v, small[:, 40 + 10 * t:50 + 10 * t].unsqueeze(2).broadcast_to([P, 10, AHD]),
                                  ALU.mult).then_inc(qk_rstd, 1)
            factors(2)
            scores(2)
            factors(3)
            copy_out("qT", aqT[:, 0:2, :].rearrange("p i s -> p (i s)"), 0)
            wait_full(dve, "kT")
            dve.tensor_copy(akT, bank("kT", 0)[:, 0:S]).then_inc(psum_drained[pair("kT")], 1)
            scores(3)
            factors(4)

            def maxima(n, job):
                wait_full(dve, job)
                m = small[:, 100 + 8 * (n % 2):104 + 8 * (n % 2)]
                src = banks(job).rearrange("p b n -> p (b n)").rearrange("p (u w) -> p u w", u=4)
                link(dve.tensor_reduce(m, src, AX, ALU.max))
                dve.tensor_scalar(m, m, -0.125, None, ALU.mult).then_inc(row_max, 1)

            def normalise(n, pr, units):
                rs = small[:, 120 + 8 * (n % 2):120 + 8 * (n % 2) + units]
                link(dve.reciprocal(rs, rs))
                shape = [P, units, D // units]
                dve.tensor_tensor(pr, pr, rs.unsqueeze(2).broadcast_to(shape), ALU.mult).then_inc(prob_ready, 1)

            def attended(job, t, g):
                wait_full(dve, job)
                dst = oattT[64 * g:64 * g + 64, :, t * P:(t + 1) * P]
                src = PS[64 * g:64 * g + 64, 2 * pair(job), :].rearrange("p (i s) -> p i s", i=4)
                dve.tensor_copy(dst, src).then_inc(psum_drained[pair(job)], 1)

            maxima(0, "sc00")
            maxima(1, "sc01")
            wait_drained(dve, "sc00")
            normalise(0, prob[0], 4)
            wait_drained(dve, "sc01")
            normalise(1, prob[1], 4)
            scores(4)
            factors(5)
            copy_out("PT00", tmp[:, 0:NB], 0)
            attended("pv00", 0, 0)
            copy_out("PT01", tmp[:, 0:NB], 0)
            attended("pv01", 0, 1)
            maxima(2, "sc10")
            maxima(3, "sc11")
            wait_drained(dve, "sc10")
            normalise(2, prob[0], 4)
            wait_drained(dve, "sc11")
            normalise(3, prob[1], 4)
            scores(5)
            factors(6)
            copy_out("PT10", tmp[:, 0:NB], 0)
            attended("pv10", 1, 0)
            copy_out("PT11", tmp[:, 0:NB], 0)
            attended("pv11", 1, 1)
            scores(6)
            factors(7)
            scores(7)
            factors(8)
            copy_out("lv8", AT[:, 0, 1].rearrange("p h s -> p (h s)"), 0)
            ada_part(4)
            ada_part(5)
            dve.wait_ge(o_ssq, 1)
            dve.tensor_scalar(small[:, 140:148], small[:, 140:148], 1.0 / HGD, EPS, ALU.mult, ALU.add).then_inc(o_var, 1)
            dve.wait_ge(o_std, 1)
            link(dve.reciprocal(small[:, 150:158], small[:, 150:158]))
            for t in range(T):
                o4 = ohg[:, t, :].rearrange("p (h d) -> p h d", h=HG)
                dve.tensor_tensor(o4, bank("og", t).rearrange("p (h d) -> p h d", h=HG),
                                  small[:, 150 + 4 * t:154 + 4 * t].unsqueeze(2).broadcast_to([P, HG, HGD]),
                                  ALU.mult).then_inc(psum_drained[pair("og")], 1)
            wait_drained(dve, "og")
            dve.wait_ge(hgate_ready, 2)
            for t in range(T):
                dve.tensor_tensor(ohg[:, t, :], ohg[:, t, :], hgate[:, t, :], ALU.mult).then_inc(ohg_ready, 1)
            dve.wait_ge(bias1_in, 32)
            ada_row(4, gate1[:, 0:NB])
            ada_row(5, gate1[:, NB:D])
            copy_out("ohgT", ohgT[:, 0:2, :].rearrange("p i s -> p (i s)"), 0)
            ada_part(6)
            ada_part(7)
            ada_col(6)
            ada_col(7)
            for job in ("W7", "W8"):
                wait_drained(dve, job)
            for n in range(2):
                job = f"ya{n}"
                wait_full(dve, job)
                for t in range(T):
                    dve.tensor_tensor(merged[:, t, n * NB:(n + 1) * NB], bank(job, t),
                                      gsig[:, 0, t, n * NB:(n + 1) * NB], ALU.mult).then_inc(psum_drained[pair(job)], 1)
            for job in ("W9", "W10"):
                wait_drained(dve, job)
            for n in range(2):
                job = f"yh{n}"
                wait_full(dve, job)
                for t in range(T):
                    g = gsig[:, 1, t, n * NB:(n + 1) * NB]
                    dve.tensor_tensor(g, bank(job, t), g, ALU.mult).then_inc(psum_drained[pair(job)], 1)
                wait_drained(dve, job)
                wait_drained(dve, f"ya{n}")
                for t in range(T):
                    m = merged[:, t, n * NB:(n + 1) * NB]
                    dve.tensor_tensor(m, m, gsig[:, 1, t, n * NB:(n + 1) * NB], ALU.add).then_inc(merged_ready, 1)
            ada_part(8)
            ada_part(9)
            ada_col(8)
            ada_col(9)
            wait_drained(dve, "adc9")
            wait_drained(dve, "adc8")
            dve.scalar_tensor_tensor(out=aff2[:, :], in0=modc[:, 32:40], scalar=1.0, in1=vcol[:, V_NF:V_NF + 8],
                                     op0=ALU.add, op1=ALU.mult).then_inc(aff_ready, 1)
            copy_out("mTa", hT[:, 0:2, :].rearrange("p k s -> p (k s)"), 0)
            copy_out("mTb", hT[:, 4:6, :].rearrange("p k s -> p (k s)"), 0)
            wait_drained(dve, "adr5")
            wait_drained(dve, "adr4")
            for n in range(2):
                job = f"mo{n}"
                wait_full(dve, job)
                for t in range(T):
                    dve.tensor_tensor(tmp[:, t * NB:(t + 1) * NB], bank(job, t), gate1[:, n * NB:(n + 1) * NB],
                                      ALU.mult).then_inc(psum_drained[pair(job)], 1)
                wait_drained(dve, job)
                for t in range(T):
                    v = x[:, t, n * NB:(n + 1) * NB]
                    link(dve.tensor_tensor(v, v, tmp[:, t * NB:(t + 1) * NB], ALU.add))
            dve.sem_inc(x_ready, T)
            ada_part(10)
            ada_part(11)
            ada_row(10, gate2[:, 0:NB])
            ada_row(11, gate2[:, NB:D])
            norm(1)
            dve.wait_ge(aff_ready, 2)
            turn_out(("nT1a", "nT1b"), aff2, modc[:, 24:32])

            wait_full(dve, "rt")
            link(dve.tensor_reduce(small[:, 160:162], bank("rt", 0)[:, 0:T * NE].rearrange("p (t e) -> p t e", t=T),
                                   AX, ALU.max))
            dve.tensor_scalar(small[:, 160:162], small[:, 160:162], -1.0, None, ALU.mult).then_inc(r_max, 1)
            dve.wait_ge(r_exp, 1)
            link(dve.reciprocal(small[:, 162:164], small[:, 162:164]))
            dve.tensor_tensor(eprob, eprob, small[:, 162:164].unsqueeze(2).broadcast_to([P, T, NE]), ALU.mult)\
                .then_inc(r_ready, 1)
            dve.sem_inc(psum_drained[pair("rt")], 1)
            wait_full(dve, "aT")
            link(dve.tensor_copy(etop[0:16, :], bank("aT", 0)[0:16, 0:S]))
            dve.sem_inc(psum_drained[pair("aT")], 1)
            cur, other = etop[0:16, :], etop2[0:16, :]
            topw = small[0:16, 208:240]
            for r8 in range(4):
                link(dve.max(topw[:, 8 * r8:8 * r8 + 8], cur))
                link(dve.max_index(eidx[0:16, 8 * r8:8 * r8 + 8].bitcast(U32), topw[:, 8 * r8:8 * r8 + 8], cur))
                if r8 < 3:
                    link(dve.match_replace(other, topw[:, 8 * r8:8 * r8 + 8], cur, -1.0))
                    cur, other = other, cur
            link(dve.tensor_copy(eidx[0:16, 32:64], eidx[0:16, 0:32].bitcast(U32)))
            dve.tensor_copy(erep[0:16, 0], eidx[0:16, 32:64].unsqueeze(1).broadcast_to([16, 4, CAP]))
            dve.tensor_copy(erep[0:16, 1], topw.unsqueeze(1).broadcast_to([16, 4, CAP]))
            dve.tensor_tensor(ebd[0:16, :].rearrange("p (e c) -> p e c", e=NE), blockdiag,
                              eidx[0:16, 32:64].unsqueeze(1).broadcast_to([16, NE, CAP]), ALU.mult).then_inc(top_ready, 1)
            wait_full(dve, "ic")
            dve.tensor_copy(ecol.rearrange("p a e -> p (a e)"), bank("ic", 0)[:, 0:32]).then_inc(psum_drained[pair("ic")], 1)
            wait_full(dve, "ib")
            for t in range(T):
                ins = dve.tensor_scalar(onehot[:, t, :], bank("ib", 0), consts[:, C_TOK + t:C_TOK + t + 1], None,
                                        ALU.is_equal)
                ins.then_inc(pick_ready if t == 0 else psum_drained[pair("ib")], 1)
            for q in range(4):
                job = f"ga{q}"
                wait_full(dve, job)
                k = 2 * q
                dve.tensor_scalar(xeT[:, k, :], bank(job, 0), aff2[:, k:k + 1], modc[:, 24 + k:25 + k],
                                  ALU.mult, ALU.add).then_inc(psum_drained[pair(job)], 1)
            for q in range(4):
                wait_drained(dve, f"ga{q}")

            with dve.Fori(0, NE) as e:
                dve.tensor_copy(xe, xeT[:, :, bass.ds(e * CAP, CAP)]).then_inc(xe_ready, 1)
                dve.wait_ge(slab_done, e * PER_EXPERT + 8)
                dve.wait_ge(silu_ready, e + 1)
                dve.tensor_tensor(hid, PS[:, 1, :], sg, ALU.mult).then_inc(hid_ready, 1)
                dve.tensor_scalar(comb, iota, ecol[:, 0, bass.ds(e, 1)], ecol[:, 1, bass.ds(e, 1)],
                                  ALU.is_equal, ALU.mult)
                dve.wait_ge(slab_done, e * PER_EXPERT + 12)
                dve.tensor_copy(ye[:, 1, :], PS[:, 3, :]).then_inc(ye_ready, 1)

            wait_drained(dve, "adr11")
            wait_drained(dve, "adr10")
            dve.wait_ge(comb_done, 1)
            for t in range(T):
                link(dve.tensor_tensor(tmp[:, :], PS[:, 4 + 2 * t:6 + 2 * t, :].rearrange("p b n -> p (b n)"),
                                       gate2[:, :], ALU.mult))
                link(dve.tensor_tensor(x[:, t, :], x[:, t, :], tmp[:, :], ALU.add))
            dve.sem_inc(x_ready, T)

            copy_out("wsT", wsT[:, 0:4, :].rearrange("p g i -> p (g i)"), 0)
            wait_drained(dve, "wsT")
            link(dve.memset(wsT[64:128, :, 0:64], 0.0))
            norm(2)
            turn_out(("nT2a", "nT2b"), vcol[:, V_GA0:V_GA0 + 8])
            stats = small[:, 204:228].rearrange("p (t n) -> p t n", t=T)
            for n in range(2):
                wait_drained(dve, f"v{n}")
                for t in range(T):
                    link(dve.bn_stats(stats[:, t, 6 * n:6 * n + 6], V[:, t, n * NB:(n + 1) * NB]))
            for t in range(T):
                link(dve.bn_aggr(small[:, 168 + 2 * t:170 + 2 * t], stats[:, t, :]))
            mv = small[:, 168:172].rearrange("p (t c) -> p t c", t=T)
            dve.tensor_scalar(small[:, 172:174], mv[:, :, 1], LN_EPS, None, ALU.add).then_inc(ln_var, 1)
            dve.wait_ge(ln_std, 1)
            link(dve.reciprocal(small[:, 174:176], small[:, 176:178]))
            for t in range(T):
                link(dve.tensor_scalar(V[:, t, :], V[:, t, :], mv[:, t, 0:1], small[:, 174 + t:175 + t],
                                       ALU.subtract, ALU.mult))
            dve.wait_ge(ln_in, 32)
            for t in range(T):
                link(dve.tensor_tensor(V[:, t, :], V[:, t, :], lng, ALU.mult))
                dve.tensor_tensor(V[:, t, :], V[:, t, :], lnb, ALU.add).then_inc(ln_ready, 1)
            for n in range(2):
                wait_drained(dve, f"u{n}")
            for t in range(T):
                job = f"sv{t}"
                wait_full(dve, job)
                for g in range(8):
                    u = U[:, t, g * P:(g + 1) * P]
                    ins = dve.scalar_tensor_tensor(out=u, in0=bank(job, g // 4)[:, (g % 4) * P:(g % 4 + 1) * P],
                                                   scalar=vcol[:, V_BS + g:V_BS + g + 1], in1=u,
                                                   op0=ALU.add, op1=ALU.mult)
                    if g % 4 == 3:
                        ins.then_inc(psum_drained[pair(job)], 1)
            copy_out("pTa", hT[:, 0:2, :].rearrange("p k s -> p (k s)"), 0)
            copy_out("pTb", hT[:, 4:6, :].rearrange("p k s -> p (k s)"), 0)

            def post_norm(n, bank_of, drained):
                dve.wait_ge(post_ssq, 4 * (n + 1))
                ss = small[:, 180:184].rearrange("p (t h) -> p t h", t=T)
                link(dve.tensor_reduce(small[:, 184:186], ss, AX, ALU.add))
                dve.tensor_scalar(small[:, 186:188], small[:, 184:186], 1.0 / D, EPS, ALU.mult, ALU.add)\
                    .then_inc(post_var, 1)
                dve.wait_ge(post_std, n + 1)
                link(dve.reciprocal(small[:, 190:192], small[:, 188:190]))
                dve.wait_ge(grow_in, 16 * (n + 1))
                for half in range(2):
                    cols = slice(half * NB, (half + 1) * NB)
                    for t in range(T):
                        link(dve.scalar_tensor_tensor(out=tmp[:, t * NB:(t + 1) * NB], in0=bank_of(half, t),
                                                      scalar=small[:, 190 + t:191 + t], in1=grow[:, cols],
                                                      op0=ALU.mult, op1=ALU.mult))
                    if drained is not None:
                        dve.sem_inc(drained(half), T)
                    if half:
                        dve.sem_inc(grow_free, 1)
                    for t in range(T):
                        link(dve.tensor_tensor(x[:, t, cols], x[:, t, cols], tmp[:, t * NB:(t + 1) * NB], ALU.add))
                dve.sem_inc(x_ready, T)

            def mlp(layer):
                done = layer * FJ

                def square(j, b):
                    dve.wait_ge(relu_ready, j + (done + 1))
                    dve.tensor_tensor(hidden[:, b].rearrange("p i s -> p (i s)"), rl, rl, ALU.mult)\
                        .then_inc(hidden_ready, 1)

                square(0, 0)
                with dve.Fori(0, 2) as it:
                    for jj in range(1, 4):
                        square(it * 3 + jj, jj % 3)
                square(7, 1)

            post_norm(0, lambda h, t: bank(f"am{h}", t), lambda h: psum_drained[pair(f"am{h}")])
            norm(3)
            turn_out(("nT3a", "nT3b"), vcol[:, V_GA2:V_GA2 + 8])
            mlp(0)
            post_norm(1, lambda h, t: PS[:, 2 * t + h, :], None)
            norm(4)
            for half, job in enumerate(("nT4a", "nT4b")):
                wait_full(dve, job)
                for kk in range(2):
                    k = 4 * half + kk
                    src = bank(job, 0)[:, kk * S:(kk + 1) * S]
                    dve.tensor_scalar(hT[:, k, :], src, vcol[:, V_GB0 + k:V_GB0 + k + 1], None, ALU.mult)
                    ins = dve.tensor_scalar(hR[:, k, ::-1], src, vcol[:, V_KV + k:V_KV + k + 1], None, ALU.mult)
                ins.then_inc(psum_drained[pair(job)], 1)
            for job, dst in (("bk0", bkT[:, 0:2]), ("bk1", bkT[:, 4:6]), ("bq0", bqT[:, 0:2]), ("bq1", bqT[:, 4:6])):
                copy_out(job, dst.rearrange("p k s -> p (k s)"), 0)
            for n in range(2):
                copy_out(f"bv{n}", vR[:, 0, n * NB:(n + 1) * NB], 0)

            def b_scores(n):
                job = f"bs{n}"
                units, width = (8, P) if n < 2 else (4, S)
                pr = bp[n % 2]
                wait_full(dve, job)
                if n == 0:
                    dve.wait_ge(bias_masked, 1)
                per = units // 2
                b0 = 4 * n if n < 2 else 2 * (n - 2)
                for g in range(2):
                    add = bias.rearrange("p (b g) m -> p g b m", g=2)[:, g, b0:b0 + per, 0:width]
                    dve.scalar_tensor_tensor(out=pr[:, g * NB:(g + 1) * NB].rearrange("p (u w) -> p u w", u=per),
                                             in0=bank(job, g).rearrange("p (u w) -> p u w", u=per), scalar=0.125,
                                             in1=add, op0=ALU.mult, op1=ALU.add).then_inc(psum_drained[pair(job)], 1)
                wait_drained(dve, job)
                m = small[:, 100 + 8 * (n % 2):100 + 8 * (n % 2) + units]
                link(dve.tensor_reduce(m, pr.rearrange("p (u w) -> p u w", u=units), AX, ALU.max))
                dve.tensor_scalar(m, m, -1.0, None, ALU.mult).then_inc(row_max, 1)

            def b_attended(n):
                job = f"bo{n}"
                wait_full(dve, job)
                if n < 2:
                    dst = oT[:, 4 * n:4 * n + 4, 0:P]
                    src = bank(job, 0).rearrange("p (b s) -> p b s", b=4)
                else:
                    dst = oT[:, 2 * (n - 2):2 * (n - 2) + 2, P:S]
                    src = bank(job, 0)[:, 0:S].rearrange("p (b s) -> p b s", b=2)
                dve.tensor_copy(dst, src).then_inc(psum_drained[pair(job)], 1)

            def b_probs(n):
                units = 8 if n < 2 else 4
                dve.wait_ge(row_exp, n + 1)
                normalise(4 + n, bp[n % 2].rearrange("p (u w) -> p u w", u=units), units)

            def b_turned(n):
                copy_out(f"bT{n}", bpt[:, 0:NB], 0)

            b_scores(0)
            b_scores(1)
            b_probs(0)
            for n in range(6):
                b_turned(n)
                if n < 5:
                    b_probs(n + 1)
                if n < 4:
                    b_scores(n + 2)
                b_attended(n)
            post_norm(2, lambda h, t: bank(f"bm{h}", t), lambda h: psum_drained[pair(f"bm{h}")])
            norm(5)
            turn_out(("nT5a", "nT5b"), vcol[:, V_GB2:V_GB2 + 8])
            mlp(1)
            post_norm(3, lambda h, t: PS[:, 2 * t + h, :], None)

        @block.tensor
        def _(pe):
            mm = nc.tensor.matmul

            def begin(job):
                i = JOB_AT[job]
                if i >= 4:
                    pe.wait_ge(psum_drained[i % 4], DRAINED[i - 4])

            def end(ins, job):
                ins.then_inc(psum_full[pair(job)], 1)

            def turn(job, blocks):
                begin(job)
                for i, src in enumerate(blocks):
                    ins = nc.tensor.transpose(bank(job, i // 4)[:, (i % 4) * P:(i % 4 + 1) * P], src, ident)
                end(ins, job)

            def turn_rows(jobs, src):
                for half, job in enumerate(jobs):
                    turn(job, [src[:, t, k * P:(k + 1) * P] for k in range(4 * half, 4 * half + 4) for t in range(T)])

            def norm(n):
                pe.wait_ge(xn_ready, 2 * n + 2)
                turn_rows((f"nT{n}a", f"nT{n}b"), xn)

            def natural(job, slab, lhs=hT, k=KD, c0=0, width=NB):
                begin(job)
                wait_slab(pe, slab)
                w = kn(slab, k)
                for t in range(T):
                    for i in range(k):
                        ins = mm(bank(job, t)[:, 0:width], lhs[:, i, t * P:(t + 1) * P], w[:, i, c0:c0 + width],
                                 start=i == 0, stop=i == k - 1)
                end(ins, job)

            def turned(job, slab, rhs=hT):
                begin(job)
                wait_slab(pe, slab)
                for b in range(4):
                    for i in range(KD):
                        ins = mm(bank(job, b // 2)[:, (b % 2) * S:(b % 2 + 1) * S], kn(slab)[:, i, b * P:(b + 1) * P],
                                 rhs[:, i, :], start=i == 0, stop=i == KD - 1)
                end(ins, job)

            def ada_part(s):
                job, n = f"ada{s}", SLAB_AT[f"ada{s}"]
                begin(job)
                wait_slab(pe, n)
                for i in range(2):
                    for j in range(4):
                        ins = mm(PS[32 * j:32 * j + 32, 2 * pair(job), :], crep[:, 2 * j + i, :], kn(n)[:, 2 * j + i, :],
                                 start=i == 0, stop=i == 1)
                end(ins, job)

            def ada_col(s):
                job = f"adc{s}"
                begin(job)
                wait_drained(pe, f"ada{s}")
                for i in range(4):
                    ins = mm(bank(job, 0)[:, i:i + 1], part[:, s % 2, i * P:(i + 1) * P], mean32[:, 0:1],
                             start=True, stop=True)
                end(ins, job)

            def ada_row(s):
                job = f"adr{s}"
                begin(job)
                wait_drained(pe, f"ada{s}")
                end(mm(bank(job, 0), mean32[:, :], part[:, s % 2, :], start=True, stop=True), job)

            pe.wait_ge(consts_in, 16)
            pe.wait_ge(vrow_in, 16 * 11)
            begin("vecT")
            end(nc.tensor.transpose(bank("vecT", 0)[:, 0:P], vrow[:, :], ident), "vecT")
            pe.wait_ge(crep_ready, 1)
            pe.wait_ge(filled, 3)
            ada_part(0)
            ada_part(1)
            ada_col(0)
            ada_part(2)
            ada_col(1)
            ada_part(3)
            ada_col(2)
            ada_col(3)
            norm(0)
            wait_drained(pe, "nT0a")
            wait_drained(pe, "nT0b")

            def W(i):
                job = f"W{i}"
                if i < 3:
                    turned(job, SLAB_AT[job])
                else:
                    natural(job, SLAB_AT[job], width=256 if i == 5 else NB)

            def level(lv):
                job = f"lv{lv}"
                begin(job)
                pe.wait_ge(factors_ready, lv + 1)
                for t in range(T):
                    for h in range(HG):
                        key = t if lv < LEVELS - 1 else t
                        qry = t if lv < LEVELS - 1 else 1 - t
                        ins = mm(bank(job, t)[:, h * P:(h + 1) * P], EK[:, h, key * P:(key + 1) * P],
                                 EQ[:, h, qry * P:(qry + 1) * P], start=True, stop=True)
                end(ins, job)

            def a_scores(t, g):
                job = f"sc{t}{g}"
                begin(job)
                rows = slice(64 * g, 64 * g + 64)
                for i in range(4):
                    ins = mm(bank(job, i // 2)[:, (i % 2) * S:(i % 2 + 1) * S], aqT[rows, i, t * P:(t + 1) * P],
                             akT[rows, :], start=True, stop=True)
                end(ins, job)

            def a_values(t, g, n):
                pe.wait_ge(prob_ready, n + 1)
                turn(f"PT{t}{g}", [prob[n % 2][:, i, k * P:(k + 1) * P] for k in range(2) for i in range(4)])
                job = f"pv{t}{g}"
                begin(job)
                wait_drained(pe, f"PT{t}{g}")
                for k in range(2):
                    ins = mm(PS[64 * g:64 * g + 64, 2 * pair(job), :], va[:, k, 64 * g:64 * g + 64],
                             ptr[:, k].rearrange("p i s -> p (i s)"), start=k == 0, stop=k == 1)
                end(ins, job)

            for i in range(5):
                W(i)
            level(0)
            W(5)
            level(1)
            W(6)
            level(2)
            pe.wait_ge(qk_ready, 2)
            turn("qT", [qk[:, t, i * P:(i + 1) * P] for i in range(4) for t in range(T)])
            turn("kT", [qk[:, t, 512:640] for t in range(T)])
            level(3)
            wait_drained(pe, "qT")
            wait_drained(pe, "kT")
            wait_drained(pe, "W5")
            a_scores(0, 0)
            a_scores(0, 1)
            level(4)
            a_values(0, 0, 0)
            a_values(0, 1, 1)
            a_scores(1, 0)
            a_scores(1, 1)
            level(5)
            a_values(1, 0, 2)
            a_values(1, 1, 3)
            level(6)
            level(7)
            level(8)
            ada_part(4)
            ada_part(5)
            begin("og")
            for lv in (7, 8):
                wait_drained(pe, f"lv{lv}")
            for t in range(T):
                for h in range(HG):
                    for j in range(T):
                        ins = mm(bank("og", t)[:, h * HGD:(h + 1) * HGD], AT[:, j, t, h, :],
                                 gv[:, j, h * HGD:(h + 1) * HGD], start=j == 0, stop=j == 1)
            end(ins, "og")
            ada_row(4)
            ada_row(5)
            W(7)
            W(8)
            pe.wait_ge(ohg_ready, 2)
            turn("ohgT", [ohg[:, t, i * P:(i + 1) * P] for i in range(4) for t in range(T)])
            W(9)
            W(10)
            ada_part(6)
            ada_part(7)
            ada_col(6)
            ada_col(7)
            for g in ("pv00", "pv01", "pv10", "pv11", "ohgT"):
                wait_drained(pe, g)
            for n in range(2):
                natural(f"ya{n}", SLAB_AT["att"], oattT, 4, n * NB)
            for n in range(2):
                natural(f"yh{n}", SLAB_AT["hg"], ohgT, 4, n * NB)
            ada_part(8)
            ada_part(9)
            ada_col(8)
            ada_col(9)
            pe.wait_ge(merged_ready, 4)
            turn_rows(("mTa", "mTb"), merged)
            wait_drained(pe, "mTa")
            wait_drained(pe, "mTb")
            for n in range(2):
                natural(f"mo{n}", SLAB_AT[f"out{n}"])
            ada_part(10)
            ada_part(11)
            ada_row(10)
            ada_row(11)
            norm(1)
            wait_drained(pe, "nT1a")
            wait_drained(pe, "nT1b")
            pe.wait_ge(wrt_in, 16)
            begin("rt")
            for t in range(T):
                for k in range(KD):
                    ins = mm(bank("rt", 0)[:, t * NE:(t + 1) * NE], hT[:, k, t * P:(t + 1) * P], wrt[:, k, :],
                             start=k == 0, stop=k == KD - 1)
            end(ins, "rt")
            begin("aT")
            pe.wait_ge(r_ready, 1)
            for t in range(T):
                ins = nc.tensor.transpose(bank("aT", 0)[0:16, t * P:(t + 1) * P], eprob[:, t, :], ident)
            end(ins, "aT")
            begin("ic")
            pe.wait_ge(top_ready, 1)
            for a in range(2):
                ins = nc.tensor.transpose(bank("ic", 0)[:, a * NE:(a + 1) * NE],
                                          erep[0:16, a].rearrange("p j c -> p (j c)"), consts[0:16, C_ID:C_ID + 16])
            end(ins, "ic")
            begin("ib")
            end(mm(bank("ib", 0), ones16[:, :], ebd[0:16, :], start=True, stop=True), "ib")
            wait_drained(pe, "ib")
            for q in range(4):
                job = f"ga{q}"
                begin(job)
                for b in range(2):
                    k = 2 * q + b
                    for t in range(T):
                        ins = mm(bank(job, b), xn[:, t, k * P:(k + 1) * P], onehot[:, t, :], start=t == 0, stop=t == 1)
                end(ins, job)

            for q in range(4):
                wait_drained(pe, f"ga{q}")
            for b in range(4):
                mm(PS[:, 4 + b, :], zrow[0:1, 0:P], zrow[0:1, P:P + NB], start=True, stop=False)

            with pe.Fori(0, NE) as e:
                def expert_slab(i):
                    n = AT_EXPERT + i
                    pe.wait_ge(slab_in[n % R], e * (16 * PER_EXPERT // R) + slot_in(n))

                pe.wait_ge(xe_ready, e + 1)
                for side in range(2):
                    for q in range(4):
                        i = 4 * side + q
                        expert_slab(i)
                        w = kn(AT_EXPERT + i, 2)
                        for kk in range(2):
                            for j in range(4):
                                ins = mm(PS[32 * j:32 * j + 32, side, :], xe[:, 2 * q + kk, :],
                                         w[:, kk, j * NB:(j + 1) * NB], start=q == 0 and kk == 0, stop=q == 3 and kk == 1)
                        ins.then_inc(slab_done, 1)
                pe.wait_ge(hid_ready, e + 1)
                for i in range(4):
                    ins = nc.tensor.transpose(PS[:, 0, i * P:(i + 1) * P], hid[:, i * P:(i + 1) * P], ident)
                ins.then_inc(hid_turned, 1)
                pe.wait_ge(hidT_ready, e + 1)
                for i in range(4):
                    expert_slab(8 + i)
                    w = kn(AT_EXPERT + 8 + i, 4)
                    for n in range(2):
                        for j in range(4):
                            ins = mm(PS[32 * j:32 * j + 32, 2 + n, :], hidT[:, i, 32 * j:32 * j + 32],
                                     w[:, j, n * NB:(n + 1) * NB], start=i == 0, stop=i == 3)
                    ins.then_inc(slab_done, 1)
                pe.wait_ge(ye_ready, 2 * e + 2)
                for t in range(T):
                    for n in range(2):
                        mm(PS[:, 4 + 2 * t + n, :], comb[:, t * P:(t + 1) * P], ye[:, n, :], start=False, stop=False)
            for b in range(4):
                ins = mm(PS[:, 4 + b, :], zrow[0:1, 0:P], zrow[0:1, P:P + NB], start=False, stop=True)
            ins.then_inc(comb_done, 1)

            pe.wait_ge(x_ready, X_EXP)
            pe.wait_ge(ws_in, 16)
            turn("wsT", [ws[:, g, :] for g in range(8)])
            norm(2)
            wait_drained(pe, "nT2a")
            wait_drained(pe, "nT2b")
            for j in ("v0", "v1", "u0", "u1"):
                natural(j, SLAB_AT[j])
            pe.wait_ge(ln_ready, 2)
            for t in range(T):
                job = f"sv{t}"
                begin(job)
                for g in range(8):
                    ins = mm(bank(job, g // 4)[:, (g % 4) * P:(g % 4 + 1) * P], wsT[:, g, :],
                             V[:, t, g * P:(g + 1) * P], start=True, stop=True)
                end(ins, job)
            wait_drained(pe, "sv0")
            wait_drained(pe, "sv1")
            turn_rows(("pTa", "pTb"), U)
            wait_drained(pe, "pTa")
            wait_drained(pe, "pTb")
            for n in range(2):
                natural(f"am{n}", SLAB_AT[f"am{n}"])

            def mlp(layer):
                at0 = AT_FFN[layer]
                squares = layer * FJ
                for b in range(4):
                    mm(PS[:, b, :], zrow[0:1, 0:P], zrow[0:1, P:P + NB], start=True, stop=False)

                def up(j, i, turns=None):
                    n = at0 + i
                    pe.wait_ge(slab_in[n % R], slot_in(n) if turns is None else turns * 16 + slot_in(n))
                    if not (isinstance(j, int) and j == 0):
                        pe.wait_ge(relu_ready, j + squares)
                    for b in range(4):
                        for k in range(KD):
                            ins = mm(PS[:, 4 + b // 2, (b % 2) * S:(b % 2 + 1) * S], kn(n)[:, k, b * P:(b + 1) * P],
                                     hT[:, k, :], start=k == 0, stop=k == KD - 1)
                    ins.then_inc(slab_done, 1)

                def down(j, i, b, turns=None):
                    n = at0 + i
                    pe.wait_ge(slab_in[n % R], slot_in(n) if turns is None else turns * 16 + slot_in(n))
                    pe.wait_ge(hidden_ready, j + (squares + 1))
                    for t in range(T):
                        for h in range(2):
                            for k in range(4):
                                ins = mm(PS[:, 2 * t + h, :], hidden[:, b, k, t * P:(t + 1) * P],
                                         kn(n, 4)[:, k, h * NB:(h + 1) * NB], start=False, stop=False)
                    ins.then_inc(slab_done, 1)

                up(0, 0)
                with pe.Fori(0, 2) as it:
                    for jj in range(1, 4):
                        up(it * 3 + jj, 2 * jj - 1, it)
                        down(it * 3 + (jj - 1), 2 * jj, (jj - 1) % 3, it)
                up(7, 13)
                down(6, 14, 0)
                down(7, 15, 1)
                for b in range(4):
                    ins = mm(PS[:, b, :], zrow[0:1, 0:P], zrow[0:1, P:P + NB], start=False, stop=True)
                ins.then_inc(mlp_done, 1)

            pe.wait_ge(x_ready, X_GM)
            norm(3)
            wait_drained(pe, "nT3a")
            wait_drained(pe, "nT3b")
            mlp(0)
            pe.wait_ge(x_ready, X_F0)
            norm(4)
            wait_drained(pe, "nT4a")
            wait_drained(pe, "nT4b")
            for j in ("bk0", "bk1"):
                turned(j, SLAB_AT[j], hR)
            for j in ("bq0", "bq1"):
                turned(j, SLAB_AT[j])
            for j in ("bv0", "bv1"):
                natural(j, SLAB_AT[j], hR)

            def b_scores(n):
                job = f"bs{n}"
                begin(job)
                t, per, k0 = (0, 4, P) if n < 2 else (1, 2, 0)
                b0 = 4 * n if n < 2 else 2 * (n - 2)
                w = S - k0
                for g in range(2):
                    rows = slice(64 * g, 64 * g + 64)
                    for i in range(per):
                        ins = mm(bank(job, g)[:, i * w:(i + 1) * w], bqT[rows, b0 + i, t * P:(t + 1) * P],
                                 bkT[rows, b0 + i, k0:S], start=True, stop=True)
                end(ins, job)

            def b_turn(n):
                pe.wait_ge(prob_ready, 5 + n)
                turn(f"bT{n}", [bp[n % 2][:, i * P:(i + 1) * P] for i in range(8)])

            def b_values(n):
                job = f"bo{n}"
                begin(job)
                wait_drained(pe, f"bT{n}")
                per = 4 if n < 2 else 2
                b0 = 4 * n if n < 2 else 2 * (n - 2)
                for g in range(2):
                    for i in range(per):
                        h = 2 * (b0 + i) + g
                        for kb in ((1,) if n < 2 else (0, 1)):
                            blk = g * 4 + (i if n < 2 else 2 * i + kb)
                            ins = mm(PS[64 * g:64 * g + 64, 2 * pair(job), i * P:(i + 1) * P],
                                     vR[:, kb, h * BHD:(h + 1) * BHD], bpt[:, blk * P:(blk + 1) * P],
                                     start=n < 2 or kb == 0, stop=n < 2 or kb == 1)
                end(ins, job)

            for j in ("bk0", "bk1", "bq0", "bq1"):
                wait_drained(pe, j)
            b_scores(0)
            b_scores(1)
            wait_drained(pe, "bv0")
            wait_drained(pe, "bv1")
            for n in range(6):
                b_turn(n)
                if n < 4:
                    pass
                b_values(n)
                if n < 4:
                    b_scores(n + 2)
            for n in range(6):
                wait_drained(pe, f"bo{n}")
            for n in range(2):
                natural(f"bm{n}", SLAB_AT[f"bm{n}"], oT)
            pe.wait_ge(x_ready, X_AT)
            norm(5)
            wait_drained(pe, "nT5a")
            wait_drained(pe, "nT5b")
            mlp(1)


_INS = ["x", "c", "ada_w", "ada_b", "norm_mix_w", "norm_ffn_w", "w_in", "q_norm_w", "k_norm_w", "hg_lower_bounds",
        "hg_norm_w", "w_branch_att", "w_branch_hg", "w_out", "w_router", "w_exp_gate", "w_exp_up", "w_exp_down",
        "norm_g_2", "a_w_in_2", "a_ln_g_2", "a_ln_b_2", "a_w_s_2", "a_b_s_2", "a_w_out_2", "kv_norm_g_2", "w_k_2",
        "w_v_2", "b_w_q_2", "b_rel_bias_2", "b_w_o_2", "w_up_2", "w_down_2"]


def constants():
    import numpy as np

    c = np.zeros((P, C_END), np.float32)
    i = np.arange(P)
    c[:, C_ID:C_ID + P] = np.eye(P)
    parted = i[:, None] ^ i[None, :]
    for lv in range(7):
        c[:, C_MASK + lv * P:C_MASK + (lv + 1) * P] = (parted >> lv) == 1
    c[:, C_IOTA:C_IOTA + S] = np.arange(S)[None, :]
    for t in range(T):
        tok = t * P + i
        c[:, C_TOK + t] = tok
        inv = np.float32(10000.0) ** (-np.arange(0, 32, 2, dtype=np.float32) / np.float32(32))
        pos = np.stack([(tok // 64), (tok % 64)], axis=1).astype(np.float32)
        ang = (pos[:, :, None] * inv.astype(np.float32)).reshape(P, 32)
        c[:, C_ROPE + 64 * t:C_ROPE + 64 * t + 32] = np.cos(ang)
        c[:, C_ROPE + 64 * t + 32:C_ROPE + 64 * t + 64] = np.sin(ang)
    for e in range(NE):
        c[e, C_BD + e * CAP:C_BD + (e + 1) * CAP] = 1.0
    return c


def kernel(**inputs):
    import numpy as _np
    import concourse.bacc as _bacc
    from concourse.bass_utils import run_bass_kernel_spmd as _run

    nc = _bacc.Bacc("TRN2", target_bir_lowering=False, num_devices=1)
    arrays, aps = {}, {}
    for name in _INS + ["consts"]:
        a = constants() if name == "consts" else _np.ascontiguousarray(inputs[name])
        arrays[f"in_{name}_dram"] = a
        aps[name] = nc.dram_tensor(f"in_{name}_dram", a.shape, mybir.dt.from_np(a.dtype), kind="ExternalInput").ap()
    out = nc.dram_tensor("out_0_dram", (1, S, D), F32, kind="ExternalOutput").ap()
    build(nc, aps, out)
    r = _run(nc, [arrays], core_ids=[0])
    return r.results[0]["out_0_dram"]
```

```python
from contextlib import ExitStack

import concourse.bass as bass
from concourse import mybir

F32 = mybir.dt.float32
F32R = mybir.dt.float32r
BF16 = mybir.dt.bfloat16
I32 = mybir.dt.int32
U32 = mybir.dt.uint32
I16 = mybir.dt.int16
ALU = mybir.AluOpType
ACT = mybir.ActivationFunctionType
AX = mybir.AxisListType.X

P = 128
S = 256
T = S // P
D = 1024
KD = D // P
NB = 512
SLOT = KD * NB
R = 6
RS = 3
NC = 3
CHUNK = SLOT // 2

AH, AHD = 8, 64
HG, HGD = 4, 128
LEVELS = 9
NE, CAP, FF = 16, 32, 2048
PER_EXPERT = 12
FFH = 4096
FJ = FFH // NB
BHEADS, BHD = 16, 64
EPS, LN_EPS, MIN_F = 1e-6, 1e-5, 1e-6
NEG = -1e30

C_ID, C_MASK, C_IOTA, C_TOK, C_ROPE = 0, 128, 576, 832, 834
C_END = 962
V_C, V_NM, V_NF, V_GA0, V_GA2, V_GB0, V_GB2, V_KV, V_BS, V_LB, V_AB = (8 * i for i in range(11))

JOBS = (
    [("vecT", 1)]
    + [(j, 1) for j in ("ada0", "ada1", "adc0", "ada2", "adc1", "ada3", "adc2", "adc3")]
    + [("nT0a", 2), ("nT0b", 2)]
    + [("W0", 2), ("W1", 2), ("W2", 2), ("lv0", 2), ("W4", 2), ("lv1", 2), ("W5", 2), ("lv2", 2), ("W3", 2)]
    + [("lv3", 2), ("qT", 2), ("kT", 1), ("sc00", 2), ("sc01", 2), ("lv4", 2), ("W6", 2)]
    + [("PT00", 2), ("pv00", 1), ("PT01", 2), ("pv01", 1), ("lv5", 2), ("sc10", 2), ("sc11", 2), ("lv6", 2)]
    + [("PT10", 2), ("pv10", 1), ("PT11", 2), ("pv11", 1), ("lv7", 2), ("lv8", 2)]
    + [("ada4", 1), ("ada5", 1), ("og", 2), ("adr4", 1), ("adr5", 1)]
    + [("W7", 2), ("W8", 2), ("ohgT", 2), ("W9", 2), ("W10", 2)]
    + [("ada6", 1), ("ada7", 1), ("adc6", 1), ("adc7", 1), ("ya0", 2), ("ya1", 2), ("yh0", 2), ("yh1", 2)]
    + [("ada8", 1), ("ada9", 1), ("adc8", 1), ("adc9", 1), ("mTa", 2), ("mTb", 2), ("mo0", 2), ("mo1", 2)]
    + [("ada10", 1), ("ada11", 1), ("adr10", 1), ("adr11", 1)]
    + [("nT1a", 2), ("nT1b", 2), ("rt", 1), ("aT", 1), ("ic", 1), ("ib", 1)]
    + [("ga0", 2), ("ga1", 2), ("ga2", 2), ("ga3", 2), ("wsT", 2)]
    + [("nT2a", 2), ("nT2b", 2), ("v0", 2), ("v1", 2), ("u0", 2), ("u1", 2)]
    + [("sv0", 2), ("sv1", 2), ("pTa", 2), ("pTb", 2), ("am0", 2), ("am1", 2), ("nT3a", 2), ("nT3b", 2)]
    + [("nT4a", 2), ("nT4b", 2), ("bk0", 2), ("bk1", 2), ("bq0", 2), ("bq1", 2), ("bv0", 2), ("bv1", 2)]
    + [("bs0", 2), ("bs1", 2), ("bs2", 2), ("bT0", 2), ("bs3", 2), ("bo0", 1), ("bT1", 2), ("bs4", 2), ("bo1", 1)]
    + [("bT2", 2), ("bs5", 2), ("bo2", 1), ("bT3", 2), ("bo3", 1), ("bT4", 2), ("bo4", 1), ("bT5", 2), ("bo5", 1)]
    + [("bm0", 2), ("bm1", 2), ("nT5a", 2), ("nT5b", 2)]
)
JOB_AT = {name: i for i, (name, _) in enumerate(JOBS)}
DRAINED = [sum(n for j, (_, n) in enumerate(JOBS) if j % 4 == i % 4 and j <= i) for i in range(len(JOBS))]

FIRST_SLABS = (
    [(f"ada{i}", f"ada{i}") for i in range(4)]
    + [(f"W{i}", f"W{i}") for i in (0, 1, 2, 4, 5, 3, 6)]
    + [("ada4", "ada4"), ("ada5", "ada5")]
    + [(f"W{i}", f"W{i}") for i in range(7, 11)]
    + [("ada6", "ada6"), ("ada7", "ada7"), ("att", "ya1"), ("hg", "yh1"), ("ada8", "ada8"), ("ada9", "ada9")]
    + [("out0", "mo0"), ("out1", "mo1"), ("ada10", "ada10"), ("ada11", "ada11")]
)
A_SLABS = [("v0", "v0"), ("v1", "v1"), ("u0", "u0"), ("u1", "u1"), ("am0", "am0"), ("am1", "am1")]
B_SLABS = [(j, j) for j in ("bk0", "bk1", "bq0", "bq1", "bv0", "bv1", "bm0", "bm1")]
N_FIRST = len(FIRST_SLABS)
N_EXPERT = NE * PER_EXPERT
AT_EXPERT = N_FIRST
AT_A = AT_EXPERT + N_EXPERT
AT_FFN = [AT_A + len(A_SLABS), AT_A + len(A_SLABS) + 2 * FJ + len(B_SLABS)]
AT_B = AT_FFN[0] + 2 * FJ
SLAB_AT = {name: i for i, (name, _) in enumerate(FIRST_SLABS)}
SLAB_AT |= {name: AT_A + i for i, (name, _) in enumerate(A_SLABS)}
SLAB_AT |= {name: AT_B + i for i, (name, _) in enumerate(B_SLABS)}

def cut_of(name):
    if name in ("W0", "W1", "W2", "bk0", "bk1", "bq0", "bq1"):
        return "n", (None, name)
    if name in ("att", "hg"):
        job = {"att": "ya", "hg": "yh"}[name]
        return "n4", (f"{job}0", f"{job}1")
    return "k", (None, {"out0": "mo0", "out1": "mo1"}.get(name, name))


CHUNKS = []
CHUNK_OF = {}


def add_chunks(slabs, at):
    for i, (name, _) in enumerate(slabs):
        if not name.startswith("ada"):
            how, jobs = cut_of(name)
            for half, job in enumerate(jobs):
                CHUNK_OF[job or jobs[1]] = min(CHUNK_OF.get(job or jobs[1], len(CHUNKS)), len(CHUNKS))
                CHUNKS.append((at + i, how, half, job))


def add_mlp_chunks(layer):
    for i, (kind, _) in enumerate(FFN_ORDER):
        CHUNKS.extend((AT_FFN[layer] + i, "n" if kind == "up" else "k", half, None) for half in range(2))


FFN_ORDER = [("up", 0)] + [x for j in range(1, FJ) for x in (("up", j), ("down", j - 1))] + [("down", FJ - 1)]
add_chunks(FIRST_SLABS, 0)
C_A = len(CHUNKS)
add_chunks(A_SLABS, AT_A)
C_FFN = [len(CHUNKS)]
add_mlp_chunks(0)
C_B = len(CHUNKS)
add_chunks(B_SLABS, AT_B)
C_FFN.append(len(CHUNKS))
add_mlp_chunks(1)


def slot_of(n):
    if n < AT_EXPERT:
        return n % RS
    return (n - AT_EXPERT) % R if n < AT_A else (n - AT_A) % RS


ARRIVED, BEFORE, _count, _last = [], [], [0] * R, [None] * R
for _n in range(AT_FFN[1] + 2 * FJ):
    _s = slot_of(_n)
    _count[_s] += 32 if _n == SLAB_AT["att"] else 16
    ARRIVED.append(_count[_s])
    BEFORE.append(_last[_s])
    _last[_s] = _n
LAST_CHUNK = {n: c for c, (n, _, _, _) in enumerate(CHUNKS)}
SPLIT_JOBS = ["nT0a", "nT0b", "ohgT", "mTa", "mTb", "nT1a", "nT1b", "nT2a", "nT2b", "pTa", "pTb", "nT3a", "nT3b",
              "nT4a", "nT4b", "nT5a", "nT5b"]
W_COLS = {"W0": 768, "W1": 1280, "W2": 1792, "W3": 2304, "W4": 0, "W5": 512, "W6": 2816,
          "W7": 3328, "W8": 3840, "W9": 4352, "W10": 4864}
def build(nc, A, out):
    with ExitStack() as ctx:
        def sb(name, shape, dt=F32):
            return ctx.enter_context(nc.sbuf_tensor(name, shape, dt))

        def sem(name):
            return ctx.enter_context(nc.semaphore(name))

        PS = ctx.enter_context(nc.psum_tensor("PS", [P, 8, NB], F32))

        ring_a = sb("ring_a", [P, RS, SLOT])
        with nc.sbuf_tensor("ring_b", [P, R - RS, SLOT], F32) as ring_b:
            pass
        parts = sb("parts", [P, NC, 2, CHUNK], F32R)
        x = sb("x", [P, T, D])
        xn = sb("xn", [P, T, D])
        hT = [sb(f"hT{i}", [P, KD, S], F32R) for i in range(2)]
        consts = sb("consts", [P, C_END])
        vcol = sb("vcol", [P, P])
        modc = sb("modc", [P, 48])
        aff1 = sb("aff1", [P, KD])
        aff2 = sb("aff2", [P, KD])
        crep = sb("crep", [P, KD, 32])
        csil = sb("csil", [P, KD])
        wr = [sb(f"wr{i}", [P, KD, NE], F32R) for i in range(2)]
        mean32 = sb("mean32", [P, P])
        zrow = sb("zrow", [1, NB], BF16)
        junk = sb("junk", [P, D], BF16)
        tmp = sb("tmp", [P, D])
        vrow = tmp[:, 0:P]
        ssq = sb("ssq", [P, 6, T, 2])
        std = sb("std", [P, 6, T])
        rstd = sb("rstd", [P, 6, T])
        small = sb("small", [P, 256])
        with nc.sbuf_tensor("arena", [P, 16 * 1024], F32) as arena:
            pass
        rounded = sb("rounded", [P, 16 * 1024], F32R)

        def at(kb, cols):
            return arena[:, kb * 256:kb * 256 + cols]

        def rat(kb, cols):
            return rounded[:, kb * 256:kb * 256 + cols]

        ident = consts[:, C_ID:C_ID + P]
        masks = consts[:, C_MASK:C_MASK + 7 * P // 2].bitcast(I16)
        iota = consts[:, C_IOTA:C_IOTA + S]
        rope = consts[:, C_ROPE:C_ROPE + 128].rearrange("p (t f a i) -> p t f a i", t=T, f=2, a=2)
        wrt = at(0, 128).rearrange("p (k e) -> p k e", k=KD)
        blockdiag = at(24, 512)[0:16, :]

        part = at(32, 2 * NB).rearrange("p (b n) -> p b n", b=2)
        gq = at(0, 1024).rearrange("p (h s) -> p h s", h=HG)
        gkf = at(4, 1024).rearrange("p (h s) -> p h s", h=HG)
        gkb = at(8, 1024).rearrange("p (h s) -> p h s", h=HG)
        PF = at(12, 1024).rearrange("p (h s) -> p h s", h=HG)
        XF = at(16, 1024).rearrange("p (h s) -> p h s", h=HG)
        PB = at(20, 1024).rearrange("p (h s) -> p h s", h=HG)
        XB = at(24, 1024).rearrange("p (h s) -> p h s", h=HG)
        EK = at(28, 1024).rearrange("p (h s) -> p h s", h=HG)
        EQ = at(32, 1024).rearrange("p (h s) -> p h s", h=HG)
        AT = at(36, 2048).rearrange("p (j i h s) -> p j i h s", j=T, i=T, h=HG)
        gv = at(44, 1024).rearrange("p (t n) -> p t n", t=T)
        hgate = at(48, 1024).rearrange("p (t n) -> p t n", t=T)
        qk = at(52, 1280).rearrange("p (t n) -> p t n", t=T)
        va = at(57, 256).rearrange("p (t n) -> p t n", t=T)
        aqT = at(58, 1024).rearrange("p (i s) -> p i s", i=4)
        akT = at(62, 256)
        wqk = at(63, 128)
        hgw = at(63, 256)[:, P:2 * P]
        oattT = at(52, 1024)
        oattR = [rat(kb, 1024).rearrange("p (i s) -> p i s", i=4) for kb in (56, 60)]
        prob = [xn[:, b, :].rearrange("p (i s) -> p i s", i=4) for b in range(2)]
        ptr = tmp[:, :].rearrange("p (k i s) -> p k i s", k=2, i=4)
        ohg = at(0, 1024).rearrange("p (t n) -> p t n", t=T)
        ohgR = [rat(kb, 1024).rearrange("p (i s) -> p i s", i=4) for kb in (4, 28)]
        gate1 = at(8, 1024)
        gsig = at(12, 4096).rearrange("p (b t n) -> p b t n", b=2, t=T)
        merged = xn

        xeT = at(0, 4096).rearrange("p (k c) -> p k c", k=KD)
        onehot = at(16, 1024).rearrange("p (t c) -> p t c", t=T)
        gate2 = at(36, 1024)
        xe = at(20, 256).rearrange("p (k c) -> p k c", k=KD)
        sg = at(21, 512)
        hid = at(23, 512)
        hidT = at(25, 512).rearrange("p (i m) -> p i m", i=4)
        ye = at(27, 1024).rearrange("p (n m) -> p n m", n=2)
        comb = at(31, 256)
        eprob = at(40, 32).rearrange("p (t e) -> p t e", t=T)
        etop = at(41, 256)
        eidx = at(42, 64)
        etop2 = at(43, 256)
        erep = at(44, 256).rearrange("p (a j c) -> p a j c", a=2, j=4)
        ebd = at(45, 512)
        ecol = at(47, 32).rearrange("p (a e) -> p a e", a=2)

        V = at(0, 2048).rearrange("p (t n) -> p t n", t=T)
        U = at(8, 2048).rearrange("p (t n) -> p t n", t=T)
        ws = tmp[:, :].rearrange("p (g j) -> p g j", g=8)
        wsT = at(16, 1024).rearrange("p (g i) -> p g i", g=8)
        lng = at(32, 1024)
        lnb = at(36, 1024)
        grows = [at(kb, 1024) for kb in (28, 28, 16, 28)]
        hidden = [rat(kb, 3072).rearrange("p (b i s) -> p b i s", b=3, i=4) for kb in (0, 12)]
        rl = at(24, 1024)
        sqr = at(32, 1024)
        hR = [rat(kb, 2048).rearrange("p (k s) -> p k s", k=KD) for kb in (0, 8)]
        bp = [at(kb, 1024) for kb in (0, 4, 8, 12)]
        bqT = at(16, 2048).rearrange("p (k s) -> p k s", k=KD)
        bkT = at(24, 2048).rearrange("p (k s) -> p k s", k=KD)
        vR = at(32, 2048).rearrange("p (t n) -> p t n", t=T)
        bpt = [at(40, 1024), at(44, 1024)]
        bias = at(48, 4096).rearrange("p (h m) -> p h m", h=BHEADS)

        psum_full = [sem(f"psum_full{i}") for i in range(4)]
        psum_drained = [sem(f"psum_drained{i}") for i in range(4)]
        slab_in = [sem(f"slab_in{i}") for i in range(R)]
        chunk_high, chunk_low = sem("chunk_high"), sem("chunk_low")
        half_done = sem("half_done")
        high_out = sem("high_out")
        slot_passed = sem("slot_passed")
        slab_done = sem("slab_done")
        consts_in, vrow_in, vrow_in2, x_in, rows_in, wrt_in = (sem(n) for n in ("consts_in", "vrow_in", "vrow_in2", "x_in", "rows_in", "wrt_in"))
        bias1_in, ln_in, ws_in, bias_in, out_written = (
            sem(n) for n in ("bias1_in", "ln_in", "ws_in", "bias_in", "out_written"))
        grow_in = [sem(f"grow_in{i}") for i in range(2)]
        filled = sem("filled")
        norm_ssq, norm_var, norm_std, xn_ready = (sem(n) for n in ("norm_ssq", "norm_var", "norm_std", "xn_ready"))
        x_ready = sem("x_ready")
        crep_ready, c_silu, lb_in, lb_exp, lb_ready, aff_ready = (
            sem(n) for n in ("crep_ready", "c_silu", "lb_in", "lb_exp", "lb_ready", "aff_ready"))
        sig_ready, forget_ready, log_in, log_ready, k_ready, q_ready = (
            sem(n) for n in ("sig_ready", "forget_ready", "log_in", "log_ready", "k_ready", "q_ready"))
        exp_ready, sums_ready, factors_ready = (sem(n) for n in ("exp_ready", "sums_ready", "factors_ready"))
        qk_copied, qk_var, qk_std, qk_rstd, qk_ready = (sem(n) for n in ("qk_copied", "qk_var", "qk_std", "qk_rstd", "qk_ready"))
        row_max, row_exp, prob_ready = (sem(n) for n in ("row_max", "row_exp", "prob_ready"))
        gate_silu, hgate_ready, o_ssq, o_var, o_std, ohg_ready = (
            sem(n) for n in ("gate_silu", "hgate_ready", "o_ssq", "o_var", "o_std", "ohg_ready"))
        merged_ready = sem("merged_ready")
        r_max, r_exp, r_ready, top_ready, pick_ready = (sem(n) for n in ("r_max", "r_exp", "r_ready", "top_ready", "pick_ready"))
        xe_ready, silu_ready, hid_ready, hid_turned, hidT_ready, ye_ready, comb_done = (
            sem(n) for n in ("xe_ready", "silu_ready", "hid_ready", "hid_turned", "hidT_ready", "ye_ready", "comb_done"))
        gelu_ready, ln_var, ln_std, ln_ready, prod_ready = (sem(n) for n in ("gelu_ready", "ln_var", "ln_std", "ln_ready", "prod_ready"))
        post_ssq, post_var, post_std = (sem(n) for n in ("post_ssq", "post_var", "post_std"))
        relu_ready, sqr_ready, sqr_high, hidden_ready, mlp_done = (
            sem(n) for n in ("relu_ready", "sqr_ready", "sqr_high", "hidden_ready", "mlp_done"))
        oatt_high, oatt_low, bd_in, wr_high, wr_ready, wsT_ready = (
            sem(n) for n in ("oatt_high", "oatt_low", "bd_in", "wr_high", "wr_ready", "wsT_ready"))
        dve_step, act_step, pool_step = sem("dve_step"), sem("act_step"), sem("pool_step")
        grow_free, bias_masked = sem("grow_free"), sem("bias_masked")

        X_MIX, X_EXP, X_GM, X_F0, X_AT, X_LAST = 2, 4, 8, 12, 16, 20

        def pair(job):
            return JOB_AT[job] % 4

        def banks(job):
            p = 2 * pair(job)
            return PS[:, p:p + 2, :]

        def bank(job, b):
            return PS[:, 2 * pair(job) + b, :]

        def wait_full(eng, job):
            eng.wait_ge(psum_full[pair(job)], JOB_AT[job] // 4 + 1)

        def wait_drained(eng, job):
            eng.wait_ge(psum_drained[pair(job)], DRAINED[JOB_AT[job]])

        def wait_slab(eng, n):
            eng.wait_ge(slab_in[slot_of(n)], ARRIVED[n])

        def slot(n):
            i = slot_of(n)
            return ring_a[:, i, :] if i < RS else ring_b[:, i - RS, :]

        def kn(n, k=KD):
            return slot(n).rearrange("p (k n) -> p k n", k=k)

        def chunk_shape(c):
            n, how, half, _ = CHUNKS[c]
            if n == SLAB_AT["W5"]:
                return 4, 256
            if how == "k":
                return (2, D) if is_down(n) else (4, NB)
            return (8, 256) if how == "n" else (4, NB)

        def is_down(n):
            return any(a <= n < a + 2 * FJ and FFN_ORDER[n - a][0] == "down" for a in AT_FFN)

        def raw(c):
            n, how, half, _ = CHUNKS[c]
            k, w = chunk_shape(c)
            if how == "k":
                return (kn(n, 4) if is_down(n) else kn(n))[:, half * k:(half + 1) * k, 0:w]
            return kn(n, k)[:, :, half * w:(half + 1) * w]

        def part_of(c, low):
            k, w = chunk_shape(c)
            return parts[:, c % NC, low, 0:k * w].rearrange("p (k n) -> p k n", k=k)

        def wait_used(eng, c):
            job = CHUNKS[c][3]
            if job:
                wait_full(eng, job)
            elif CHUNKS[c][2] == 1:
                eng.wait_ge(slab_done, done_count(CHUNKS[c][0]))
            else:
                eng.wait_ge(half_done, HALF_COUNT[c])

        HALF_COUNT = {}
        for c, (_, how, half, job) in enumerate(CHUNKS):
            if half == 0 and job is None:
                HALF_COUNT[c] = len(HALF_COUNT) + 1

        def high_count(job, b):
            return 2 * SPLIT_JOBS.index(job) + b + 1

        def done_count(n):
            if n < AT_A:
                return n - AT_EXPERT + 1
            if n < AT_B:
                return N_EXPERT + n - AT_FFN[0] + 1
            return N_EXPERT + 2 * FJ + n - AT_FFN[1] + 1

        def split(ap, s):
            v = ap.rearrange("p h s -> p (h s)").rearrange("p (m a s) -> p a m s", a=2, s=s)
            return v[:, 0], v[:, 1]

        def hankel(table):
            v = table[0, :, 129:129 + S]
            return bass.AP(tensor=v.tensor, offset=v.offset, ap=[[1, P], [table.shape[2], BHEADS], [1, S]])

        def by_rows(v):
            return v.rearrange("(k p) -> k p", p=P)

        VECTORS = [(V_AB, by_rows(A["ada_b"][0])), (V_C, by_rows(A["c"][0])), (V_NM, by_rows(A["norm_mix_w"][0])),
                   (V_NF, by_rows(A["norm_ffn_w"][0])), (V_GA0, by_rows(A["norm_g_2"][0, 0])),
                   (V_GA2, by_rows(A["norm_g_2"][0, 2])), (V_GB0, by_rows(A["norm_g_2"][1, 0])),
                   (V_GB2, by_rows(A["norm_g_2"][1, 2])), (V_KV, by_rows(A["kv_norm_g_2"])),
                   (V_BS, A["a_b_s_2"][0]), (V_LB, A["hg_lower_bounds"][0].rearrange("a (h p) -> (a h) p", p=P))]

        block = ctx.enter_context(nc.Block())

        @block.sync
        def _(sp):
            def slab_free(n):
                before = BEFORE[n]
                if AT_EXPERT + RS <= n < AT_EXPERT + R:
                    wait_used(sp, C_A - 1)
                elif before is None:
                    return
                elif before in LAST_CHUNK:
                    sp.wait_ge(chunk_low, LAST_CHUNK[before] + 1)
                elif before < AT_EXPERT:
                    wait_full(sp, FIRST_SLABS[before][1])
                else:
                    sp.wait_ge(slab_done, done_count(before))

            def load(n, src, k=KD, dst=None):
                slab_free(n)
                sp.dma_start(kn(n, k) if dst is None else dst, src).then_inc(slab_in[slot_of(n)], 16)

            def columns(w, n0, width=NB):
                return w[:, n0:n0 + width].rearrange("(k p) n -> p k n", p=P)

            for name, _ in FIRST_SLABS:
                n = SLAB_AT[name]
                if name.startswith("ada"):
                    load(n, columns(A["ada_w"][0], int(name[3:]) * NB))
                elif name == "W5":
                    load(n, columns(A["w_in"][0], W_COLS[name], 256), dst=kn(n)[:, :, 0:256])
                elif name.startswith("W"):
                    load(n, columns(A["w_in"][0], W_COLS[name]))
                elif name == "att":
                    for g in range(2):
                        src = A["w_branch_att"][0, g * 256:(g + 1) * 256, :].rearrange("(i d) n -> d i n", d=AHD)
                        load(n, src, dst=kn(n, 4)[64 * g:64 * g + 64])
                elif name == "hg":
                    load(n, A["w_branch_hg"][0].rearrange("(k p) n -> p k n", p=P), 4)
                else:
                    load(n, columns(A["w_out"][0], int(name[3:]) * NB))

            def expert_slab(e, i):
                if i < 8:
                    w = A["w_exp_gate"] if i < 4 else A["w_exp_up"]
                    return w[0, e, (i % 4) * 256:(i % 4 + 1) * 256, :].rearrange("(k p) n -> p k n", p=P), 2
                rows = A["w_exp_down"][0, e].rearrange("(j i p) n -> i p j n", j=4, p=P)
                return rows[i - 8], 4

            for i in range(R):
                load(AT_EXPERT + i, *expert_slab(0, i))
            with sp.Fori(0, NE - 1) as e:
                for i in range(PER_EXPERT):
                    ahead = R + i
                    sp.wait_ge(slab_done, e * PER_EXPERT + (i + 1))
                    sp.sem_inc(slot_passed, 1)
                    src, k = expert_slab(e + ahead // PER_EXPERT, ahead % PER_EXPERT)
                    sp.dma_start(kn(AT_EXPERT + ahead, k), src).then_inc(slab_in[slot_of(AT_EXPERT + ahead)], 16)
            for i in range(R, PER_EXPERT):
                load(AT_EXPERT + (NE - 1) * PER_EXPERT + i, *expert_slab(NE - 1, i))

            def mlp_slabs(layer):
                up, down = A["w_up_2"][layer], A["w_down_2"][layer]
                for i, (kind, j) in enumerate(FFN_ORDER):
                    if kind == "up":
                        load(AT_FFN[layer] + i, columns(up, j * NB))
                    else:
                        load(AT_FFN[layer] + i,
                             down[j * NB:(j + 1) * NB, :].rearrange("(k p) n -> p k n", p=P), 4)

            for name, _ in A_SLABS:
                w = A["a_w_out_2"] if name.startswith("am") else A["a_w_in_2"]
                load(SLAB_AT[name], columns(w[0], int(name[-1]) * NB + (D if name[0] == "v" else 0)))
            mlp_slabs(0)
            for name, _ in B_SLABS:
                w = {"bk": A["w_k_2"], "bv": A["w_v_2"], "bq": A["b_w_q_2"][0], "bm": A["b_w_o_2"][0]}[name[:2]]
                load(SLAB_AT[name], columns(w, int(name[-1]) * NB))
            mlp_slabs(1)
            sp.wait_ge(x_ready, X_LAST)
            sp.dma_start(out[0].rearrange("(t p) d -> p t d", p=P), x[:, :, :]).then_inc(out_written, 16)
            sp.wait_ge(out_written, 16)


        @block.gpsimd
        def _(pool):
            steps = [0]

            def link(ins):
                steps[0] += 1
                ins.then_inc(pool_step, 1)
                pool.wait_ge(pool_step, steps[0])

            pool.memset(mean32[:, :], 1.0 / 32).then_inc(filled, 1)
            for v, src in VECTORS[6:]:
                pool.dma_start(vrow[v:v + src.shape[0], :], src).then_inc(vrow_in2, 16)
            pool.memset(zrow[:, :], 0.0).then_inc(filled, 1)
            pool.dma_start(wqk[:, 0:64], A["q_norm_w"][0].partition_broadcast(P)).then_inc(rows_in, 16)
            pool.dma_start(wqk[:, 64:128], A["k_norm_w"][0].partition_broadcast(P)).then_inc(rows_in, 16)
            pool.dma_start(hgw[:, :], A["hg_norm_w"][0].partition_broadcast(P)).then_inc(rows_in, 16)

            pool.wait_ge(lb_ready, 1)
            for d, (f, k) in enumerate(((PF, gkf), (PB, gkb))):
                wait_drained(pool, f"W{d + 1}")
                for h in range(HG):
                    c = d * HG + h
                    pool.tensor_scalar(f[:, h, :], f[:, h, :], small[:, 8 + c:9 + c], small[:, c:c + 1],
                                       ALU.mult, ALU.add).then_inc(forget_ready, 1)
                for h in range(HG):
                    c = d * HG + h
                    pool.tensor_scalar(k[:, h, :], k[:, h, :], small[:, 8 + c:9 + c], 0.0,
                                       ALU.mult, ALU.add).then_inc(k_ready, 1)
            pool.memset(XF, 0.0).then_inc(filled, 1)
            pool.memset(XB, 0.0).then_inc(filled, 1)

            pool.wait_ge(rows_in, 48)
            for t in range(T):
                pool.wait_ge(qk_rstd, t + 1)
                q10 = qk[:, t, :].rearrange("p (h d) -> p h d", d=AHD)
                link(pool.tensor_tensor(q10[:, 0:8, :], q10[:, 0:8, :],
                                        wqk[:, 0:64].unsqueeze(1).broadcast_to([P, 8, 64]), ALU.mult))
                link(pool.tensor_tensor(q10[:, 8:10, :], q10[:, 8:10, :],
                                        wqk[:, 64:128].unsqueeze(1).broadcast_to([P, 2, 64]), ALU.mult))
                halves = qk[:, t, :].rearrange("p (h a f i) -> p f h a i", h=10, a=2, f=2)
                x1, x2 = halves[:, 0], halves[:, 1]
                cos = rope[:, t, 0].unsqueeze(1).broadcast_to([P, 10, 2, 16])
                sin = rope[:, t, 1].unsqueeze(1).broadcast_to([P, 10, 2, 16])
                r = [xn[:, 0, i * 320:(i + 1) * 320].rearrange("p (h a i) -> p h a i", h=10, a=2) for i in range(3)]
                r.append(xn[:, 1, 0:320].rearrange("p (h a i) -> p h a i", h=10, a=2))
                pool.tensor_tensor(r[0], x1, cos, ALU.mult)
                pool.tensor_tensor(r[1], x2, sin, ALU.mult)
                pool.tensor_tensor(r[2], x2, cos, ALU.mult)
                link(pool.tensor_tensor(r[3], x1, sin, ALU.mult))
                pool.tensor_tensor(x1, r[0], r[1], ALU.subtract)
                pool.tensor_tensor(x2, r[2], r[3], ALU.add).then_inc(qk_ready, 1)
            wait_drained(pool, "W6")
            for t in range(T):
                g4 = hgate[:, t, :].rearrange("p (h d) -> p h d", h=HG)
                pool.tensor_tensor(g4, g4, hgw[:, :].unsqueeze(1).broadcast_to([P, HG, HGD]), ALU.mult)\
                    .then_inc(hgate_ready, 1)

            wait_full(pool, "lv8")
            pool.dma_start(gate1, A["ada_b"][0, 2 * D:3 * D].partition_broadcast(P)).then_inc(bias1_in, 16)

            wait_full(pool, "og")
            pool.dma_start(gate2, A["ada_b"][0, 5 * D:6 * D].partition_broadcast(P)).then_inc(bias1_in, 16)
            wait_full(pool, "ohgT")
            pool.dma_start(wrt, A["w_router"][0].rearrange("(k p) e -> p k e", p=P)).then_inc(wrt_in, 16)

            wait_full(pool, "yh1")
            pool.dma_start(bias[:, :, :], hankel(A["b_rel_bias_2"])).then_inc(bias_in, 16)
            pool.wait_ge(bias_in, 16)
            pool.memset(bias[0:64, :, 0:64], NEG).then_inc(bias_masked, 1)
            pool.wait_ge(x_ready, X_MIX)
            pool.dma_start(blockdiag, A["blockdiag"]).then_inc(bd_in, 16)
            wait_full(pool, "adr11")
            pool.dma_start(lng, A["a_ln_g_2"][0].partition_broadcast(P)).then_inc(ln_in, 16)
            wait_drained(pool, "nT1b")
            pool.dma_start(ws, A["a_w_s_2"][0].rearrange("g i j -> i g j")).then_inc(ws_in, 16)
            pool.wait_ge(x_ready, X_EXP)
            pool.dma_start(lnb, A["a_ln_b_2"][0].partition_broadcast(P)).then_inc(ln_in, 16)
            for n, row in enumerate((A["norm_g_2"][0, 1], A["norm_g_2"][0, 3],
                                     A["norm_g_2"][1, 1], A["norm_g_2"][1, 3])):
                if n in (1, 3):
                    pool.wait_ge(grow_free, n if n == 1 else 2)
                if n == 2:
                    wait_full(pool, "bs5")
                pool.dma_start(grows[n], row.partition_broadcast(P)).then_inc(grow_in[n % 2], 16)

        @block.scalar
        def _(act):
            act.dma_start(consts[:, :], A["consts"]).then_inc(consts_in, 16)
            for v, src in VECTORS[:6]:
                act.dma_start(vrow[v:v + src.shape[0], :], src).then_inc(vrow_in, 16)
            act.dma_start(x[:, :, :], A["x"][0].rearrange("(t p) d -> p t d", p=P)).then_inc(x_in, 16)

            nexts = [0]

            def split_to(last):
                while nexts[0] <= last:
                    c = nexts[0]
                    nexts[0] += 1
                    wait_slab(act, CHUNKS[c][0])
                    if c >= NC and c != C_A:
                        wait_used(act, c - NC)
                    act.activation(part_of(c, 0), raw(c), ACT.Copy).then_inc(chunk_high, 1)

            def norm(n, ready=0):
                for i in range(4):
                    half, t = divmod(i, 2)
                    if ready:
                        act.wait_ge(x_ready, ready + i + 1)
                    if half:
                        act.wait_ge(norm_ssq, 4 * n + i - 1)
                    act.activation(junk[:, t * NB:(t + 1) * NB], x[:, t, half * NB:(half + 1) * NB], ACT.Square,
                                   accum_out=ssq[:, n, t, half:half + 1]).then_inc(norm_ssq, 1)
                act.wait_ge(norm_var, n + 1)
                act.activation(std[:, n, :], ssq[:, n, :, 0], ACT.Sqrt).then_inc(norm_std, 1)

            def turn_out(jobs, scale=None, shift=None):
                for half, job in enumerate(jobs):
                    wait_full(act, job)
                    for b in range(2):
                        k0 = 4 * half + 2 * b
                        if scale is None:
                            ins = act.activation(hT[0][:, k0:k0 + 2, :].rearrange("p k s -> p (k s)"), bank(job, b), ACT.Copy)
                        for kk in range(2 if scale is not None else 0):
                            k = k0 + kk
                            ins = act.activation(hT[0][:, k, :], bank(job, b)[:, kk * S:(kk + 1) * S], ACT.Identity,
                                                 scale=scale[:, k:k + 1], bias=shift[:, k:k + 1] if shift is not None else 0.0)
                        ins.then_inc(high_out, 1)

            def copy_out(job, dst, b):
                wait_full(act, job)
                act.activation(dst, bank(job, b), ACT.Copy).then_inc(psum_drained[pair(job)], 1)

            wait_full(act, "vecT")
            act.wait_ge(lb_in, 1)
            act.activation(small[:, 24:32], small[:, 16:24], ACT.Exp).then_inc(lb_exp, 1)
            act.activation(csil[:, :], vcol[:, V_C:V_C + 8], ACT.Silu).then_inc(c_silu, 1)
            act.wait_ge(x_in, 16)
            norm(0)
            split_to(1)
            act.wait_ge(aff_ready, 1)
            turn_out(("nT0a", "nT0b"), aff1, modc)
            split_to(3)

            wait_full(act, "W0")
            for b in range(2):
                act.activation(gq[:, 2 * b:2 * b + 2, :], bank("W0", b).rearrange("p (h s) -> p h s", h=2), ACT.Silu)\
                    .then_inc(psum_drained[pair("W0")], 1)
            for job, f, k in (("W1", PF, gkf), ("W2", PB, gkb)):
                split_to(CHUNK_OF[job] + 3)
                wait_full(act, job)
                for b in range(2):
                    src = bank(job, b).rearrange("p (h s) -> p h s", h=2)
                    act.activation(f[:, 2 * b:2 * b + 2, :], src, ACT.Sigmoid)
                    act.activation(k[:, 2 * b:2 * b + 2, :], src, ACT.Sigmoid, scale=-1.0)\
                        .then_inc(psum_drained[pair(job)], 1)
            for d, f in enumerate((PF, PB)):
                act.wait_ge(log_in, d + 1)
                act.activation(f, f, ACT.Ln).then_inc(log_ready, 1)

            def levels(lv):
                s = 1 << (lv - 1)
                act.wait_ge(log_ready if lv == 1 else sums_ready, 2 if lv == 1 else lv - 1)
                if lv == 1:
                    act.wait_ge(filled, 4)
                wait_full(act, f"lv{lv - 1}")
                for dst, left, right in ((EQ, PB, PF), (EK, XF, XB)):
                    act.activation(split(dst, s)[0], split(left, s)[0], ACT.Exp)
                    ins = act.activation(split(dst, s)[1], split(right, s)[1], ACT.Exp)
                ins.then_inc(exp_ready, 1)

            split_to(CHUNK_OF["W4"] + 3)
            levels(1)
            wait_full(act, "W4")
            for t in range(T):
                dst = qk[:, t, 0:512].rearrange("p (i g d) -> p g i d", i=4, g=2)
                act.activation(dst, bank("W4", t).rearrange("p (g i d) -> p g i d", g=2, i=4), ACT.Copy)\
                    .then_inc(psum_drained[pair("W4")], 1)
            split_to(CHUNK_OF["W5"] + 3)
            levels(2)
            wait_full(act, "W5")
            for t in range(T):
                act.activation(qk[:, t, 512:640], bank("W5", t)[:, 0:128], ACT.Copy)
                act.activation(va[:, t, :], bank("W5", t)[:, 128:256], ACT.Copy).then_inc(psum_drained[pair("W5")], 1)
            act.wait_ge(qk_var, 2)
            act.activation(small[:, 80:100], small[:, 60:80], ACT.Sqrt).then_inc(qk_std, 1)
            levels(3)
            split_to(CHUNK_OF["W3"] + 3)
            for t in range(T):
                copy_out("W3", gv[:, t, :], t)
            levels(4)
            copy_out("qT", aqT[:, 2:4, :].rearrange("p i s -> p (i s)"), 1)

            def softmax(n, job, units, width, scale, dst):
                act.wait_ge(row_max, n + 1)
                src = banks(job).rearrange("p b n -> p (b n)").rearrange("p (u w) -> p u w", u=units)
                for u in range(units):
                    ins = act.activation(dst[:, u, :], src[:, u, :], ACT.Exp, scale=scale,
                                         bias=small[:, 100 + 8 * (n % 2) + u:101 + 8 * (n % 2) + u],
                                         accum_out=small[:, 120 + 8 * (n % 2) + u:121 + 8 * (n % 2) + u])
                    if u == units // 2 - 1 or u == units - 1:
                        ins.then_inc(psum_drained[pair(job)], 1)

            def half_of_turned(job):
                copy_out(job, tmp[:, NB:D], 1)

            softmax(0, "sc00", 4, S, 0.125, prob[0])
            softmax(1, "sc01", 4, S, 0.125, prob[1])
            levels(5)
            split_to(CHUNK_OF["W6"] + 3)
            wait_full(act, "W6")
            for t in range(T):
                act.activation(hgate[:, t, :], bank("W6", t), ACT.Silu).then_inc(psum_drained[pair("W6")], 1)
            half_of_turned("PT00")
            wait_full(act, "pv00")
            half_of_turned("PT01")
            levels(6)
            softmax(2, "sc10", 4, S, 0.125, prob[0])
            softmax(3, "sc11", 4, S, 0.125, prob[1])
            levels(7)
            half_of_turned("PT10")
            wait_full(act, "pv10")
            half_of_turned("PT11")
            levels(8)
            copy_out("lv8", AT[:, 1, 0].rearrange("p h s -> p (h s)"), 1)
            wait_full(act, "og")
            for t in range(T):
                for h in range(HG):
                    i = HG * t + h
                    ins = act.activation(junk[:, i * HGD:(i + 1) * HGD], bank("og", t)[:, h * HGD:(h + 1) * HGD], ACT.Square,
                                         accum_out=small[:, 140 + 4 * t + h:141 + 4 * t + h])
            ins.then_inc(o_ssq, 1)
            act.wait_ge(o_var, 1)
            act.activation(small[:, 150:158], small[:, 140:148], ACT.Sqrt).then_inc(o_std, 1)
            for job, b, n in (("W7", 0, 0), ("W8", 0, 1), (None, 0, 0), ("W9", 1, 0), ("W10", 1, 1)):
                if job is None:
                    wait_full(act, "ohgT")
                    for i in range(2):
                        act.activation(ohgR[0][:, 2 * i:2 * i + 2, :].rearrange("p i s -> p (i s)"), bank("ohgT", i),
                                       ACT.Copy).then_inc(high_out, 1)
                    continue
                split_to(CHUNK_OF[job] + 3)
                wait_full(act, job)
                for t in range(T):
                    act.activation(gsig[:, b, t, n * NB:(n + 1) * NB], bank(job, t), ACT.Sigmoid)\
                        .then_inc(psum_drained[pair(job)], 1)
                if job == "W7":
                    for g in ("pv00", "pv01", "pv10", "pv11"):
                        wait_drained(act, g)
                    act.activation(oattR[0].rearrange("p i s -> p (i s)"), oattT, ACT.Copy).then_inc(oatt_high, 1)
            split_to(CHUNK_OF["mo0"] + 2)
            turn_out(("mTa", "mTb"))
            split_to(C_A - 1)

            act.wait_ge(x_ready, X_MIX)
            norm(1)
            act.wait_ge(aff_ready, 2)
            turn_out(("nT1a", "nT1b"), aff2, modc[:, 24:32])
            act.wait_ge(r_max, 1)
            for t in range(T):
                ins = act.activation(eprob[:, t, :], bank("rt", 0)[:, t * NE:(t + 1) * NE], ACT.Exp,
                                     bias=small[:, 160 + t:161 + t], accum_out=small[:, 162 + t:163 + t])
            ins.then_inc(r_exp, 1)
            for q in range(4):
                job = f"ga{q}"
                wait_full(act, job)
                k = 2 * q + 1
                act.activation(xeT[:, k, :], bank(job, 1), ACT.Identity, scale=aff2[:, k:k + 1],
                               bias=modc[:, 24 + k:25 + k]).then_inc(psum_drained[pair(job)], 1)

            copy_out("wsT", wsT[:, 4:8, :].rearrange("p g i -> p (g i)"), 1)

            with act.Fori(0, NE) as e:
                act.wait_ge(slab_done, e * PER_EXPERT + 4)
                act.activation(sg, PS[:, 0, :], ACT.Silu).then_inc(silu_ready, 1)
                act.wait_ge(hid_turned, e + 1)
                act.activation(hidT.rearrange("p i m -> p (i m)"), PS[:, 0, :], ACT.Copy).then_inc(hidT_ready, 1)
                act.wait_ge(slab_done, e * PER_EXPERT + 12)
                act.activation(ye[:, 0, :], PS[:, 2, :], ACT.Copy).then_inc(ye_ready, 1)

            act.wait_ge(x_ready, X_EXP)
            norm(2)
            act.wait_ge(slab_done, N_EXPERT)
            split_to(C_A + 1)
            turn_out(("nT2a", "nT2b"), vcol[:, V_GA0:V_GA0 + 8])
            for job, dst, n in (("v0", V, 0), ("v1", V, 1), ("u0", U, 0), ("u1", U, 1)):
                split_to(CHUNK_OF[job] + 3)
                wait_full(act, job)
                for t in range(T):
                    act.activation(dst[:, t, n * NB:(n + 1) * NB], bank(job, t), ACT.Gelu_apprx_tanh)\
                        .then_inc(psum_drained[pair(job)], 1)
                if job == "v1":
                    act.wait_ge(ln_var, 1)
                    act.activation(small[:, 176:178], small[:, 172:174], ACT.Sqrt).then_inc(ln_std, 1)
            turn_out(("pTa", "pTb"))

            def post_norm(n, bank_of, ready):
                for half in range(2):
                    ready(half)
                    for t in range(T):
                        if half:
                            act.wait_ge(post_ssq, 4 * n + t + 1)
                        act.activation(junk[:, t * NB:(t + 1) * NB], bank_of(half, t), ACT.Square,
                                       accum_out=small[:, 180 + 2 * t + half:181 + 2 * t + half]).then_inc(post_ssq, 1)
                act.wait_ge(post_var, n + 1)
                act.activation(small[:, 188:190], small[:, 186:188], ACT.Sqrt).then_inc(post_std, 1)

            def mlp(layer):
                base = done_count(AT_FFN[layer]) - 1
                done = layer * FJ
                c0, at0 = C_FFN[layer], AT_FFN[layer]
                half0 = HALF_COUNT[c0] - 1

                def high(i, turns=None):
                    c = c0 + i
                    add = (lambda k: 0) if turns is None else (lambda k: turns * k)
                    act.wait_ge(slab_in[slot_of(at0 + i // 2)], add(32) + ARRIVED[at0 + i // 2])
                    if i >= NC and i % 2:
                        act.wait_ge(half_done, add(6) + (half0 + (i - NC) // 2 + 1))
                    elif i >= NC:
                        act.wait_ge(slab_done, add(6) + (base + (i - NC) // 2 + 1))
                    else:
                        wait_used(act, c - NC)
                    act.activation(part_of(c, 0), raw(c), ACT.Copy).then_inc(chunk_high, 1)

                def relu(j, up):
                    act.wait_ge(slab_done, up)
                    act.activation(rl, PS[:, 4:6, :].rearrange("p b n -> p (b n)"), ACT.Relu).then_inc(relu_ready, 1)

                def square_high(j, b):
                    act.wait_ge(sqr_ready, j + (done + 1))
                    act.activation(hidden[0][:, b].rearrange("p i s -> p (i s)"), sqr, ACT.Copy).then_inc(sqr_high, 1)

                high(2)
                high(3)
                relu(0, base + 1)
                square_high(0, 0)
                high(4)
                high(5)
                with act.Fori(0, 2) as it:
                    for jj in range(1, 4):
                        relu(it * 3 + jj, it * 6 + (base + 2 * jj))
                        square_high(it * 3 + jj, jj % 3)
                        for i in range(4 * jj + 2, 4 * jj + 6):
                            high(i, it)
                relu(7, base + 14)
                square_high(7, 1)
                high(30)
                high(31)
                nexts[0] = c0 + 32

            split_to(CHUNK_OF["am0"] + 3)
            split_to(C_FFN[0] + 1)
            post_norm(0, lambda h, t: bank(f"am{h}", t), lambda h: wait_full(act, f"am{h}"))
            norm(3, X_EXP)
            turn_out(("nT3a", "nT3b"), vcol[:, V_GA2:V_GA2 + 8])
            mlp(0)
            split_to(C_B)
            post_norm(1, lambda h, t: PS[:, 2 * t + h, :], lambda h: act.wait_ge(mlp_done, 1))
            norm(4, X_GM)
            for half, job in enumerate(("nT4a", "nT4b")):
                wait_full(act, job)
                for b in range(2):
                    for kk in range(2):
                        k = 4 * half + 2 * b + kk
                        src = bank(job, b)[:, kk * S:(kk + 1) * S]
                        act.activation(hR[0][:, k, ::-1], src, ACT.Identity, scale=vcol[:, V_KV + k:V_KV + k + 1])
                        ins = act.activation(hT[0][:, k, :], src, ACT.Identity, scale=vcol[:, V_GB0 + k:V_GB0 + k + 1])
                    ins.then_inc(high_out, 1)
            for job, dst in (("bk0", bkT[:, 2:4]), ("bk1", bkT[:, 6:8]), ("bq0", bqT[:, 2:4]), ("bq1", bqT[:, 6:8])):
                split_to(CHUNK_OF[job] + 3)
                copy_out(job, dst.rearrange("p k s -> p (k s)"), 1)
            for n in range(2):
                split_to(CHUNK_OF[f"bv{n}"] + 3)
                copy_out(f"bv{n}", vR[:, 1, n * NB:(n + 1) * NB], 1)

            def b_softmax(n):
                units = 8 if n < 2 else 4
                pr = bp[n % 4].rearrange("p (u w) -> p u w", u=units)
                act.wait_ge(row_max, 5 + n)
                for u in range(units):
                    ins = act.activation(pr[:, u, :], pr[:, u, :], ACT.Exp,
                                         bias=small[:, 100 + 8 * (n % 2) + u:101 + 8 * (n % 2) + u],
                                         accum_out=small[:, 120 + 8 * (n % 2) + u:121 + 8 * (n % 2) + u])
                ins.then_inc(row_exp, 1)

            def b_turned(n):
                copy_out(f"bT{n}", bpt[n % 2][:, NB:D], 1)

            b_softmax(0)
            b_softmax(1)
            for n in range(6):
                b_turned(n)
                if n < 4:
                    b_softmax(n + 2)
            split_to(C_FFN[1] + 1)
            post_norm(2, lambda h, t: bank(f"bm{h}", t), lambda h: wait_full(act, f"bm{h}"))
            norm(5, X_F0)
            turn_out(("nT5a", "nT5b"), vcol[:, V_GB2:V_GB2 + 8])
            mlp(1)
            post_norm(3, lambda h, t: PS[:, 2 * t + h, :], lambda h: act.wait_ge(mlp_done, 2))

        @block.vector
        def _(dve):
            steps = [0]

            def link(ins):
                steps[0] += 1
                ins.then_inc(dve_step, 1)
                dve.wait_ge(dve_step, steps[0])

            nexts = [0]

            def split_to(last):
                while nexts[0] <= last:
                    c = nexts[0]
                    nexts[0] += 1
                    dve.wait_ge(chunk_high, c + 1)
                    dve.tensor_tensor(part_of(c, 1), raw(c), part_of(c, 0).bitcast(F32), ALU.subtract)\
                        .then_inc(chunk_low, 1)

            def norm(n):
                dve.wait_ge(norm_ssq, 4 * (n + 1))
                link(dve.tensor_tensor(ssq[:, n, :, 0], ssq[:, n, :, 0], ssq[:, n, :, 1], ALU.add))
                dve.tensor_scalar(ssq[:, n, :, 0], ssq[:, n, :, 0], 1.0 / D, EPS, ALU.mult, ALU.add).then_inc(norm_var, 1)
                dve.wait_ge(norm_std, n + 1)
                link(dve.reciprocal(rstd[:, n, :], std[:, n, :]))
                for t in range(T):
                    dve.tensor_scalar(xn[:, t, :], x[:, t, :], rstd[:, n, t:t + 1], None, ALU.mult)\
                        .then_inc(xn_ready, 1)

            def turn_out(jobs, scale=None, shift=None, dst=hT):
                for half, job in enumerate(jobs):
                    for b in range(2):
                        dve.wait_ge(high_out, high_count(job, b))
                        k0 = 4 * half + 2 * b
                        high = dst[0][:, k0:k0 + 2, :].rearrange("p k s -> p (k s)").bitcast(F32)
                        low = dst[1][:, k0:k0 + 2, :].rearrange("p k s -> p (k s)")
                        if scale is None:
                            ins = dve.tensor_tensor(low, bank(job, b), high, ALU.subtract)
                        elif shift is None:
                            for kk in range(2):
                                c = slice(kk * S, (kk + 1) * S)
                                ins = dve.scalar_tensor_tensor(out=low[:, c], in0=bank(job, b)[:, c],
                                                               scalar=scale[:, k0 + kk:k0 + kk + 1], in1=high[:, c],
                                                               op0=ALU.mult, op1=ALU.subtract)
                        else:
                            for kk in range(2):
                                c = slice(kk * S, (kk + 1) * S)
                                link(dve.tensor_scalar(tmp[:, c], bank(job, b)[:, c], scale[:, k0 + kk:k0 + kk + 1],
                                                       shift[:, k0 + kk:k0 + kk + 1], ALU.mult, ALU.add))
                            ins = dve.tensor_tensor(low, tmp[:, 0:NB], high, ALU.subtract)
                        ins.then_inc(psum_drained[pair(job)], 1)
                        if scale is not None and shift is not None:
                            dve.wait_ge(psum_drained[pair(job)], DRAINED[JOB_AT[job]] - 1 + b)

            def copy_out(job, dst, b):
                wait_full(dve, job)
                dve.tensor_copy(dst, bank(job, b)).then_inc(psum_drained[pair(job)], 1)

            def ada_part(s):
                copy_out(f"ada{s}", part[:, s % 2, :], 0)

            def ada_col(s):
                job = f"adc{s}"
                wait_full(dve, job)
                dve.tensor_tensor(modc[:, 4 * s:4 * s + 4], bank(job, 0)[:, 0:4], vcol[:, V_AB + 4 * s:V_AB + 4 * s + 4],
                                  ALU.add).then_inc(psum_drained[pair(job)], 1)

            def ada_row(s, dst):
                job = f"adr{s}"
                wait_full(dve, job)
                dve.tensor_tensor(dst, dst, bank(job, 0), ALU.add).then_inc(psum_drained[pair(job)], 1)

            wait_full(dve, "vecT")
            link(dve.tensor_copy(vcol[:, :], bank("vecT", 0)[:, 0:P]))
            dve.tensor_tensor(small[:, 16:24], vcol[:, V_LB:V_LB + 8], vcol[:, V_LB:V_LB + 8], ALU.subtract)\
                .then_inc(lb_in, 1)
            dve.sem_inc(psum_drained[pair("vecT")], 1)
            dve.wait_ge(c_silu, 1)
            for k in range(KD):
                ins = dve.tensor_copy(crep[:, k, :], csil[:, k:k + 1].broadcast_to([P, 32]))
            ins.then_inc(crep_ready, 1)
            dve.wait_ge(lb_exp, 1)
            link(dve.reciprocal(small[:, 32:40], small[:, 24:32]))
            link(dve.tensor_tensor(small[:, 32:40], small[:, 24:32], small[:, 32:40], ALU.mult))
            link(dve.tensor_tensor(small[:, 0:8], small[:, 32:40], small[:, 32:40], ALU.subtract))
            dve.tensor_scalar(small[:, 8:16], small[:, 0:8], -1.0, 1.0, ALU.mult, ALU.add).then_inc(lb_ready, 1)
            norm(0)
            ada_part(0)
            ada_part(1)
            ada_col(0)
            ada_part(2)
            ada_col(1)
            ada_part(3)
            ada_col(2)
            ada_col(3)
            wait_drained(dve, "adc3")
            wait_drained(dve, "adc2")
            dve.scalar_tensor_tensor(out=aff1[:, :], in0=modc[:, 8:16], scalar=1.0, in1=vcol[:, V_NM:V_NM + 8],
                                     op0=ALU.add, op1=ALU.mult).then_inc(aff_ready, 1)
            dve.wait_ge(aff_ready, 1)
            split_to(1)
            turn_out(("nT0a", "nT0b"), aff1, modc)
            split_to(3)

            def factors(lv):
                s = 1 << (lv - 1)
                dve.wait_ge(exp_ready, lv)
                if lv == 1:
                    dve.wait_ge(k_ready, 8)
                for src, dst, side in ((gkf, EK, 0), (gkb, EK, 1)):
                    dve.tensor_tensor(split(dst, s)[side], split(dst, s)[side], split(src, s)[side], ALU.mult)
                dve.tensor_tensor(EQ, EQ, gq, ALU.mult).then_inc(factors_ready, 1)
                if lv < LEVELS - 1:
                    (pfl, pfr), (xfl, _) = split(PF, s), split(XF, s)
                    (pbl, pbr), (_, xbr) = split(PB, s), split(XB, s)
                    m = HG * S // (2 * s)
                    wide = [P, m, s]
                    dve.tensor_tensor(xfl, xfl, pfr[:, :, s - 1:s].broadcast_to(wide), ALU.add)
                    link(dve.tensor_tensor(xbr, xbr, pbl[:, :, 0:1].broadcast_to(wide), ALU.add))
                    dve.tensor_tensor(pfr, pfr, pfl[:, :, s - 1:s].broadcast_to(wide), ALU.add)
                    dve.tensor_tensor(pbl, pbl, pbr[:, :, 0:1].broadcast_to(wide), ALU.add).then_inc(sums_ready, 1)

            def scores(lv):
                job = f"lv{lv}"
                wait_full(dve, job)
                for t in range(T):
                    src = bank(job, t).rearrange("p (h s) -> p h s", h=HG)
                    if lv == 0:
                        dve.tensor_copy(AT[:, t, t], src).then_inc(psum_drained[pair(job)], 1)
                    else:
                        m = masks[:, (lv - 1) * P:lv * P].unsqueeze(1).broadcast_to([P, HG, P])
                        dve.copy_predicated(AT[:, t, t], m, src).then_inc(psum_drained[pair(job)], 1)
                    wait_drained(dve, job) if t else None

            for d, (job, f) in enumerate((("W1", PF), ("W2", PB))):
                split_to(CHUNK_OF[job] + 3)
                dve.wait_ge(forget_ready, 4 * d + 4)
                dve.tensor_scalar(f, f, MIN_F, None, ALU.max).then_inc(log_in, 1)
            dve.wait_ge(k_ready, 8)
            wait_drained(dve, "W0")
            dve.tensor_tensor(EK, gkf, gkb, ALU.add)
            dve.tensor_copy(EQ, gq).then_inc(factors_ready, 1)
            scores(0)
            split_to(CHUNK_OF["W4"] + 3)
            factors(1)
            scores(1)
            split_to(CHUNK_OF["W5"] + 3)
            factors(2)

            wait_drained(dve, "W4")
            wait_drained(dve, "W5")
            for t in range(T):
                sq = tmp[:, 0:640]
                link(dve.tensor_tensor(sq, qk[:, t, :], qk[:, t, :], ALU.mult))
                link(dve.tensor_reduce(small[:, 60 + 10 * t:70 + 10 * t], sq.rearrange("p (h d) -> p h d", h=10),
                                       AX, ALU.add))
                dve.tensor_scalar(small[:, 60 + 10 * t:70 + 10 * t], small[:, 60 + 10 * t:70 + 10 * t],
                                  1.0 / AHD, EPS, ALU.mult, ALU.add).then_inc(qk_var, 1)
            dve.wait_ge(qk_std, 1)
            link(dve.reciprocal(small[:, 40:60], small[:, 80:100]))
            for t in range(T):
                v = qk[:, t, :].rearrange("p (h d) -> p h d", h=10)
                dve.tensor_tensor(v, v, small[:, 40 + 10 * t:50 + 10 * t].unsqueeze(2).broadcast_to([P, 10, AHD]),
                                  ALU.mult).then_inc(qk_rstd, 1)
            scores(2)
            factors(3)
            split_to(CHUNK_OF["W3"] + 3)
            scores(3)
            factors(4)
            copy_out("qT", aqT[:, 0:2, :].rearrange("p i s -> p (i s)"), 0)
            wait_full(dve, "kT")
            dve.tensor_copy(akT, bank("kT", 0)[:, 0:S]).then_inc(psum_drained[pair("kT")], 1)

            def maxima(n, job):
                wait_full(dve, job)
                m = small[:, 100 + 8 * (n % 2):104 + 8 * (n % 2)]
                src = banks(job).rearrange("p b n -> p (b n)").rearrange("p (u w) -> p u w", u=4)
                link(dve.tensor_reduce(m, src, AX, ALU.max))
                dve.tensor_scalar(m, m, -0.125, None, ALU.mult).then_inc(row_max, 1)

            def normalise(n, pr, units):
                rs = small[:, 120 + 8 * (n % 2):120 + 8 * (n % 2) + units]
                link(dve.reciprocal(rs, rs))
                shape = [P, units, D // units]
                dve.tensor_tensor(pr, pr, rs.unsqueeze(2).broadcast_to(shape), ALU.mult).then_inc(prob_ready, 1)

            def attended(job, t, g):
                wait_full(dve, job)
                dst = oattT.rearrange("p (i s) -> p i s", i=4)[64 * g:64 * g + 64, :, t * P:(t + 1) * P]
                src = PS[64 * g:64 * g + 64, 2 * pair(job), :].rearrange("p (i s) -> p i s", i=4)
                dve.tensor_copy(dst, src).then_inc(psum_drained[pair(job)], 1)

            maxima(0, "sc00")
            maxima(1, "sc01")
            wait_drained(dve, "sc00")
            normalise(0, prob[0], 4)
            wait_drained(dve, "sc01")
            normalise(1, prob[1], 4)
            scores(4)
            factors(5)
            split_to(CHUNK_OF["W6"] + 3)
            copy_out("PT00", tmp[:, 0:NB], 0)
            attended("pv00", 0, 0)
            copy_out("PT01", tmp[:, 0:NB], 0)
            attended("pv01", 0, 1)
            scores(5)
            factors(6)
            maxima(2, "sc10")
            maxima(3, "sc11")
            wait_drained(dve, "sc10")
            normalise(2, prob[0], 4)
            wait_drained(dve, "sc11")
            normalise(3, prob[1], 4)
            scores(6)
            factors(7)
            copy_out("PT10", tmp[:, 0:NB], 0)
            attended("pv10", 1, 0)
            copy_out("PT11", tmp[:, 0:NB], 0)
            attended("pv11", 1, 1)
            scores(7)
            factors(8)
            copy_out("lv8", AT[:, 0, 1].rearrange("p h s -> p (h s)"), 0)
            ada_part(4)
            ada_part(5)
            dve.wait_ge(o_ssq, 1)
            dve.tensor_scalar(small[:, 140:148], small[:, 140:148], 1.0 / HGD, EPS, ALU.mult, ALU.add).then_inc(o_var, 1)
            dve.wait_ge(o_std, 1)
            link(dve.reciprocal(small[:, 150:158], small[:, 150:158]))
            for t in range(T):
                o4 = ohg[:, t, :].rearrange("p (h d) -> p h d", h=HG)
                dve.tensor_tensor(o4, bank("og", t).rearrange("p (h d) -> p h d", h=HG),
                                  small[:, 150 + 4 * t:154 + 4 * t].unsqueeze(2).broadcast_to([P, HG, HGD]),
                                  ALU.mult).then_inc(psum_drained[pair("og")], 1)
            wait_drained(dve, "og")
            dve.wait_ge(hgate_ready, 2)
            for t in range(T):
                dve.tensor_tensor(ohg[:, t, :], ohg[:, t, :], hgate[:, t, :], ALU.mult).then_inc(ohg_ready, 1)
            dve.wait_ge(bias1_in, 32)
            ada_row(4, gate1[:, 0:NB])
            ada_row(5, gate1[:, NB:D])
            split_to(CHUNK_OF["W7"] + 3)
            dve.wait_ge(oatt_high, 1)
            dve.tensor_tensor(oattR[1].rearrange("p i s -> p (i s)"), oattT,
                              oattR[0].rearrange("p i s -> p (i s)").bitcast(F32), ALU.subtract).then_inc(oatt_low, 1)
            split_to(CHUNK_OF["W8"] + 3)
            for i in range(2):
                dve.wait_ge(high_out, high_count("ohgT", i))
                dve.tensor_tensor(ohgR[1][:, 2 * i:2 * i + 2, :].rearrange("p i s -> p (i s)"), bank("ohgT", i),
                                  ohgR[0][:, 2 * i:2 * i + 2, :].rearrange("p i s -> p (i s)").bitcast(F32),
                                  ALU.subtract).then_inc(psum_drained[pair("ohgT")], 1)
            split_to(CHUNK_OF["W10"] + 3)
            ada_part(6)
            ada_part(7)
            ada_col(6)
            ada_col(7)
            for job in ("W7", "W8"):
                wait_drained(dve, job)
            for n in range(2):
                job = f"ya{n}"
                wait_full(dve, job)
                for t in range(T):
                    dve.tensor_tensor(merged[:, t, n * NB:(n + 1) * NB], bank(job, t),
                                      gsig[:, 0, t, n * NB:(n + 1) * NB], ALU.mult).then_inc(psum_drained[pair(job)], 1)
            split_to(CHUNK_OF["mo0"] + 2)
            for job in ("W9", "W10"):
                wait_drained(dve, job)
            for n in range(2):
                job = f"yh{n}"
                wait_full(dve, job)
                for t in range(T):
                    g = gsig[:, 1, t, n * NB:(n + 1) * NB]
                    dve.tensor_tensor(g, bank(job, t), g, ALU.mult).then_inc(psum_drained[pair(job)], 1)
                wait_drained(dve, job)
                wait_drained(dve, f"ya{n}")
                for t in range(T):
                    m = merged[:, t, n * NB:(n + 1) * NB]
                    dve.tensor_tensor(m, m, gsig[:, 1, t, n * NB:(n + 1) * NB], ALU.add).then_inc(merged_ready, 1)
            ada_part(8)
            ada_part(9)
            ada_col(8)
            ada_col(9)
            wait_drained(dve, "adc9")
            wait_drained(dve, "adc8")
            dve.scalar_tensor_tensor(out=aff2[:, :], in0=modc[:, 32:40], scalar=1.0, in1=vcol[:, V_NF:V_NF + 8],
                                     op0=ALU.add, op1=ALU.mult).then_inc(aff_ready, 1)
            turn_out(("mTa", "mTb"))
            split_to(C_A - 1)
            wait_drained(dve, "adr5")
            wait_drained(dve, "adr4")
            for n in range(2):
                job = f"mo{n}"
                wait_full(dve, job)
                for t in range(T):
                    dve.tensor_tensor(tmp[:, t * NB:(t + 1) * NB], bank(job, t), gate1[:, n * NB:(n + 1) * NB],
                                      ALU.mult).then_inc(psum_drained[pair(job)], 1)
                wait_drained(dve, job)
                for t in range(T):
                    v = x[:, t, n * NB:(n + 1) * NB]
                    link(dve.tensor_tensor(v, v, tmp[:, t * NB:(t + 1) * NB], ALU.add))
            dve.sem_inc(x_ready, T)
            ada_part(10)
            ada_part(11)
            ada_row(10, gate2[:, 0:NB])
            ada_row(11, gate2[:, NB:D])
            dve.wait_ge(wrt_in, 16)
            link(dve.tensor_copy(wr[0][:, :, :], wrt))
            dve.tensor_tensor(wr[1][:, :, :], wrt, wr[0][:, :, :].bitcast(F32), ALU.subtract).then_inc(wr_ready, 1)
            norm(1)
            dve.wait_ge(aff_ready, 2)
            turn_out(("nT1a", "nT1b"), aff2, modc[:, 24:32])

            wait_full(dve, "rt")
            link(dve.tensor_reduce(small[:, 160:162], bank("rt", 0)[:, 0:T * NE].rearrange("p (t e) -> p t e", t=T),
                                   AX, ALU.max))
            dve.tensor_scalar(small[:, 160:162], small[:, 160:162], -1.0, None, ALU.mult).then_inc(r_max, 1)
            dve.wait_ge(r_exp, 1)
            link(dve.reciprocal(small[:, 162:164], small[:, 162:164]))
            dve.tensor_tensor(eprob, eprob, small[:, 162:164].unsqueeze(2).broadcast_to([P, T, NE]), ALU.mult)\
                .then_inc(r_ready, 1)
            dve.sem_inc(psum_drained[pair("rt")], 1)
            wait_full(dve, "aT")
            link(dve.tensor_copy(etop[0:16, :], bank("aT", 0)[0:16, 0:S]))
            dve.sem_inc(psum_drained[pair("aT")], 1)
            cur, other = etop[0:16, :], etop2[0:16, :]
            topw = small[0:16, 208:240]
            for r8 in range(4):
                link(dve.max(topw[:, 8 * r8:8 * r8 + 8], cur))
                link(dve.max_index(eidx[0:16, 8 * r8:8 * r8 + 8].bitcast(U32), topw[:, 8 * r8:8 * r8 + 8], cur))
                if r8 < 3:
                    link(dve.match_replace(other, topw[:, 8 * r8:8 * r8 + 8], cur, -1.0))
                    cur, other = other, cur
            link(dve.tensor_copy(eidx[0:16, 32:64], eidx[0:16, 0:32].bitcast(U32)))
            dve.tensor_copy(erep[0:16, 0], eidx[0:16, 32:64].unsqueeze(1).broadcast_to([16, 4, CAP]))
            dve.tensor_copy(erep[0:16, 1], topw.unsqueeze(1).broadcast_to([16, 4, CAP]))
            dve.wait_ge(bd_in, 16)
            dve.tensor_tensor(ebd[0:16, :].rearrange("p (e c) -> p e c", e=NE), blockdiag.rearrange("p (e c) -> p e c", e=NE),
                              eidx[0:16, 32:64].unsqueeze(1).broadcast_to([16, NE, CAP]), ALU.mult).then_inc(top_ready, 1)
            wait_full(dve, "ic")
            dve.tensor_copy(ecol.rearrange("p a e -> p (a e)"), bank("ic", 0)[:, 0:32]).then_inc(psum_drained[pair("ic")], 1)
            wait_full(dve, "ib")
            for t in range(T):
                ins = dve.tensor_scalar(onehot[:, t, :], bank("ib", 0), consts[:, C_TOK + t:C_TOK + t + 1], None,
                                        ALU.is_equal)
                ins.then_inc(pick_ready if t == 0 else psum_drained[pair("ib")], 1)
            for q in range(4):
                job = f"ga{q}"
                wait_full(dve, job)
                k = 2 * q
                dve.tensor_scalar(xeT[:, k, :], bank(job, 0), aff2[:, k:k + 1], modc[:, 24 + k:25 + k],
                                  ALU.mult, ALU.add).then_inc(psum_drained[pair(job)], 1)
            for q in range(4):
                wait_drained(dve, f"ga{q}")

            copy_out("wsT", wsT[:, 0:4, :].rearrange("p g i -> p (g i)"), 0)
            wait_drained(dve, "wsT")
            dve.memset(wsT[64:128, :, 0:64], 0.0).then_inc(wsT_ready, 1)

            with dve.Fori(0, NE) as e:
                dve.tensor_copy(xe, xeT[:, :, bass.ds(e * CAP, CAP)]).then_inc(xe_ready, 1)
                dve.wait_ge(slab_done, e * PER_EXPERT + 8)
                dve.wait_ge(silu_ready, e + 1)
                dve.tensor_tensor(hid, PS[:, 1, :], sg, ALU.mult).then_inc(hid_ready, 1)
                dve.tensor_scalar(comb, iota, ecol[:, 0, bass.ds(e, 1)], ecol[:, 1, bass.ds(e, 1)],
                                  ALU.is_equal, ALU.mult)
                dve.wait_ge(slab_done, e * PER_EXPERT + 12)
                dve.tensor_copy(ye[:, 1, :], PS[:, 3, :]).then_inc(ye_ready, 1)

            wait_drained(dve, "adr11")
            wait_drained(dve, "adr10")
            dve.wait_ge(comb_done, 1)
            for t in range(T):
                link(dve.tensor_tensor(tmp[:, :], PS[:, 4 + 2 * t:6 + 2 * t, :].rearrange("p b n -> p (b n)"),
                                       gate2[:, :], ALU.mult))
                link(dve.tensor_tensor(x[:, t, :], x[:, t, :], tmp[:, :], ALU.add))
            dve.sem_inc(x_ready, T)

            norm(2)
            split_to(C_A + 1)
            turn_out(("nT2a", "nT2b"), vcol[:, V_GA0:V_GA0 + 8])
            split_to(CHUNK_OF["v1"] + 3)
            stats = small[:, 204:228].rearrange("p (t n) -> p t n", t=T)
            for n in range(2):
                wait_drained(dve, f"v{n}")
                for t in range(T):
                    link(dve.bn_stats(stats[:, t, 6 * n:6 * n + 6], V[:, t, n * NB:(n + 1) * NB]))
            for t in range(T):
                link(dve.bn_aggr(small[:, 168 + 2 * t:170 + 2 * t], stats[:, t, :]))
            mv = small[:, 168:172].rearrange("p (t c) -> p t c", t=T)
            dve.tensor_scalar(small[:, 172:174], mv[:, :, 1], LN_EPS, None, ALU.add).then_inc(ln_var, 1)
            dve.wait_ge(ln_std, 1)
            link(dve.reciprocal(small[:, 174:176], small[:, 176:178]))
            for t in range(T):
                link(dve.tensor_scalar(V[:, t, :], V[:, t, :], mv[:, t, 0:1], small[:, 174 + t:175 + t],
                                       ALU.subtract, ALU.mult))
            dve.wait_ge(ln_in, 32)
            for t in range(T):
                link(dve.tensor_tensor(V[:, t, :], V[:, t, :], lng, ALU.mult))
                dve.tensor_tensor(V[:, t, :], V[:, t, :], lnb, ALU.add).then_inc(ln_ready, 1)
            split_to(CHUNK_OF["u1"] + 3)
            for n in range(2):
                wait_drained(dve, f"u{n}")
            for t in range(T):
                job = f"sv{t}"
                wait_full(dve, job)
                for g in range(8):
                    u = U[:, t, g * P:(g + 1) * P]
                    ins = dve.scalar_tensor_tensor(out=u, in0=bank(job, g // 4)[:, (g % 4) * P:(g % 4 + 1) * P],
                                                   scalar=vcol[:, V_BS + g:V_BS + g + 1], in1=u,
                                                   op0=ALU.add, op1=ALU.mult)
                    if g % 4 == 3:
                        ins.then_inc(psum_drained[pair(job)], 1)
            turn_out(("pTa", "pTb"))

            def post_norm(n, bank_of, drained):
                dve.wait_ge(post_ssq, 4 * (n + 1))
                ss = small[:, 180:184].rearrange("p (t h) -> p t h", t=T)
                link(dve.tensor_reduce(small[:, 184:186], ss, AX, ALU.add))
                dve.tensor_scalar(small[:, 186:188], small[:, 184:186], 1.0 / D, EPS, ALU.mult, ALU.add)\
                    .then_inc(post_var, 1)
                dve.wait_ge(grow_in[n % 2], 16 * (n // 2 + 1))
                for half in range(2):
                    cols = slice(half * NB, (half + 1) * NB)
                    for t in range(T):
                        ins = dve.tensor_tensor(xn[:, t, cols], bank_of(half, t), grows[n][:, cols], ALU.mult)
                        if drained is not None:
                            ins.then_inc(drained(half), 1)
                dve.wait_ge(post_std, n + 1)
                link(dve.reciprocal(small[:, 190:192], small[:, 188:190]))
                dve.sem_inc(grow_free, 1)
                for half in range(2):
                    cols = slice(half * NB, (half + 1) * NB)
                    for t in range(T):
                        dve.scalar_tensor_tensor(out=x[:, t, cols], in0=xn[:, t, cols],
                                                 scalar=small[:, 190 + t:191 + t], in1=x[:, t, cols],
                                                 op0=ALU.mult, op1=ALU.add).then_inc(x_ready, 1)

            def mlp(layer):
                done = layer * FJ
                c0 = C_FFN[layer]

                def low(i, turns=None):
                    c = c0 + i
                    dve.wait_ge(chunk_high, c + 1 if turns is None else turns * 12 + (c + 1))
                    dve.tensor_tensor(part_of(c, 1), raw(c), part_of(c, 0).bitcast(F32), ALU.subtract)\
                        .then_inc(chunk_low, 1)

                def square(j, b):
                    dve.wait_ge(relu_ready, j + (done + 1))
                    if not (isinstance(j, int) and j == 0):
                        dve.wait_ge(hidden_ready, j + done)
                    dve.tensor_tensor(sqr, rl, rl, ALU.mult).then_inc(sqr_ready, 1)
                    dve.wait_ge(sqr_high, j + (done + 1))
                    dve.tensor_tensor(hidden[1][:, b].rearrange("p i s -> p (i s)"), sqr,
                                      hidden[0][:, b].rearrange("p i s -> p (i s)").bitcast(F32), ALU.subtract)\
                        .then_inc(hidden_ready, 1)

                low(2)
                low(3)
                square(0, 0)
                low(4)
                low(5)
                with dve.Fori(0, 2) as it:
                    for jj in range(1, 4):
                        square(it * 3 + jj, jj % 3)
                        for i in range(4 * jj + 2, 4 * jj + 6):
                            low(i, it)
                square(7, 1)
                low(30)
                low(31)
                nexts[0] = c0 + 32

            split_to(C_FFN[0] + 1)
            post_norm(0, lambda h, t: bank(f"am{h}", t), lambda h: psum_drained[pair(f"am{h}")])
            norm(3)
            turn_out(("nT3a", "nT3b"), vcol[:, V_GA2:V_GA2 + 8])
            mlp(0)
            split_to(C_B)
            post_norm(1, lambda h, t: PS[:, 2 * t + h, :], None)
            norm(4)
            for half, job in enumerate(("nT4a", "nT4b")):
                for b in range(2):
                    dve.wait_ge(high_out, high_count(job, b))
                    for kk in range(2):
                        k = 4 * half + 2 * b + kk
                        src = bank(job, b)[:, kk * S:(kk + 1) * S]
                        dve.scalar_tensor_tensor(out=hR[1][:, k, ::-1], in0=src, scalar=vcol[:, V_KV + k:V_KV + k + 1],
                                                 in1=hR[0][:, k, ::-1].bitcast(F32), op0=ALU.mult, op1=ALU.subtract)
                        ins = dve.scalar_tensor_tensor(out=hT[1][:, k, :], in0=src,
                                                       scalar=vcol[:, V_GB0 + k:V_GB0 + k + 1],
                                                       in1=hT[0][:, k, :].bitcast(F32), op0=ALU.mult, op1=ALU.subtract)
                    ins.then_inc(psum_drained[pair(job)], 1)
            for job, dst in (("bk0", bkT[:, 0:2]), ("bk1", bkT[:, 4:6]), ("bq0", bqT[:, 0:2]), ("bq1", bqT[:, 4:6])):
                split_to(CHUNK_OF[job] + 3)
                copy_out(job, dst.rearrange("p k s -> p (k s)"), 0)
            for n in range(2):
                split_to(CHUNK_OF[f"bv{n}"] + 3)
                copy_out(f"bv{n}", vR[:, 0, n * NB:(n + 1) * NB], 0)

            def b_scores(n):
                job = f"bs{n}"
                units, width = (8, P) if n < 2 else (4, S)
                pr = bp[n % 4]
                wait_full(dve, job)
                if n == 0:
                    dve.wait_ge(bias_masked, 1)
                per = units // 2
                b0 = 4 * n if n < 2 else 2 * (n - 2)
                for g in range(2):
                    add = bias.rearrange("p (b g) m -> p g b m", g=2)[:, g, b0:b0 + per, 0:width]
                    dve.scalar_tensor_tensor(out=pr[:, g * NB:(g + 1) * NB].rearrange("p (u w) -> p u w", u=per),
                                             in0=bank(job, g).rearrange("p (u w) -> p u w", u=per), scalar=0.125,
                                             in1=add, op0=ALU.mult, op1=ALU.add).then_inc(psum_drained[pair(job)], 1)
                wait_drained(dve, job)
                m = small[:, 100 + 8 * (n % 2):100 + 8 * (n % 2) + units]
                link(dve.tensor_reduce(m, pr.rearrange("p (u w) -> p u w", u=units), AX, ALU.max))
                dve.tensor_scalar(m, m, -1.0, None, ALU.mult).then_inc(row_max, 1)

            def b_attended(n):
                job = f"bo{n}"
                wait_full(dve, job)
                b0, per, cols = (4 * n, 4, slice(0, P)) if n < 2 else (2 * (n - 2), 2, slice(P, S))
                src = bank(job, 0)[:, 0:per * P].rearrange("p (b s) -> p b s", b=per)
                high, low = (hT[i][:, b0:b0 + per, cols] for i in range(2))
                link(dve.tensor_copy(high, src))
                dve.tensor_tensor(low, src, high.bitcast(F32), ALU.subtract).then_inc(psum_drained[pair(job)], 1)

            def b_probs(n):
                units = 8 if n < 2 else 4
                dve.wait_ge(row_exp, n + 1)
                normalise(4 + n, bp[n % 4].rearrange("p (u w) -> p u w", u=units), units)

            def b_turned(n):
                copy_out(f"bT{n}", bpt[n % 2][:, 0:NB], 0)

            b_scores(0)
            b_scores(1)
            b_probs(0)
            b_scores(2)
            for n in range(6):
                b_turned(n)
                if n < 5:
                    b_probs(n + 1)
                if n < 3:
                    b_scores(n + 3)
                b_attended(n)
            split_to(C_FFN[1] + 1)
            post_norm(2, lambda h, t: bank(f"bm{h}", t), lambda h: psum_drained[pair(f"bm{h}")])
            norm(5)
            turn_out(("nT5a", "nT5b"), vcol[:, V_GB2:V_GB2 + 8])
            mlp(1)
            post_norm(3, lambda h, t: PS[:, 2 * t + h, :], None)

        @block.tensor
        def _(pe):
            mm = nc.tensor.matmul

            def begin(job):
                i = JOB_AT[job]
                if i >= 4:
                    pe.wait_ge(psum_drained[i % 4], DRAINED[i - 4])

            def end(ins, job):
                ins.then_inc(psum_full[pair(job)], 1)

            def turn(job, blocks):
                begin(job)
                for i, src in enumerate(blocks):
                    ins = nc.tensor.transpose(bank(job, i // 4)[:, (i % 4) * P:(i % 4 + 1) * P], src, ident)
                end(ins, job)

            def turn_rows(jobs, src):
                for half, job in enumerate(jobs):
                    turn(job, [src[:, t, k * P:(k + 1) * P] for k in range(4 * half, 4 * half + 4) for t in range(T)])

            def norm(n):
                pe.wait_ge(xn_ready, 2 * n + 2)
                turn_rows((f"nT{n}a", f"nT{n}b"), xn)

            def mm3(out, left, right, start, stop):
                mm(out, left[0], right[0], start=start, stop=False)
                mm(out, left[0], right[1], start=False, stop=False)
                return mm(out, left[1], right[0], start=False, stop=stop)

            def natural(job, act):
                begin(job)
                for half in range(2):
                    c = CHUNK_OF[job] + half
                    pe.wait_ge(chunk_low, c + 1)
                    k, w = chunk_shape(c)
                    for t in range(T):
                        for i in range(k):
                            ins = mm3(bank(job, t)[:, 0:w], [a[:, half * k + i, t * P:(t + 1) * P] for a in act],
                                      [part_of(c, j)[:, i, :] for j in range(2)],
                                      start=half == 0 and i == 0, stop=half == 1 and i == k - 1)
                    if half == 0:
                        ins.then_inc(half_done, 1)
                end(ins, job)

            def branch(job, act):
                begin(job)
                c = CHUNK_OF[job]
                pe.wait_ge(chunk_low, c + 1)
                for t in range(T):
                    for i in range(4):
                        ins = mm3(bank(job, t), [a[:, i, t * P:(t + 1) * P] for a in act],
                                  [part_of(c, j)[:, i, :] for j in range(2)], start=i == 0, stop=i == 3)
                end(ins, job)

            def turned(job, act):
                begin(job)
                for half in range(2):
                    c = CHUNK_OF[job] + half
                    pe.wait_ge(chunk_low, c + 1)
                    for b in range(2):
                        for i in range(KD):
                            ins = mm3(bank(job, half)[:, b * S:(b + 1) * S],
                                      [part_of(c, j)[:, i, b * P:(b + 1) * P] for j in range(2)],
                                      [a[:, i, :] for a in act], start=i == 0, stop=i == KD - 1)
                    if half == 0:
                        ins.then_inc(half_done, 1)
                end(ins, job)

            def ada_part(s):
                job, n = f"ada{s}", SLAB_AT[f"ada{s}"]
                begin(job)
                wait_slab(pe, n)
                for i in range(2):
                    for j in range(4):
                        ins = mm(PS[32 * j:32 * j + 32, 2 * pair(job), :], crep[:, 2 * j + i, :], kn(n)[:, 2 * j + i, :],
                                 start=i == 0, stop=i == 1)
                end(ins, job)

            def ada_col(s):
                job = f"adc{s}"
                begin(job)
                wait_drained(pe, f"ada{s}")
                for i in range(4):
                    ins = mm(bank(job, 0)[:, i:i + 1], part[:, s % 2, i * P:(i + 1) * P], mean32[:, 0:1],
                             start=True, stop=True)
                end(ins, job)

            def ada_row(s):
                job = f"adr{s}"
                begin(job)
                wait_drained(pe, f"ada{s}")
                end(mm(bank(job, 0), mean32[:, :], part[:, s % 2, :], start=True, stop=True), job)

            pe.wait_ge(consts_in, 16)
            pe.wait_ge(vrow_in, 16 * 6)
            pe.wait_ge(vrow_in2, 16 * 5)
            begin("vecT")
            end(nc.tensor.transpose(bank("vecT", 0)[:, 0:P], vrow[:, :], ident), "vecT")
            pe.wait_ge(crep_ready, 1)
            pe.wait_ge(filled, 2)
            ada_part(0)
            ada_part(1)
            ada_col(0)
            ada_part(2)
            ada_col(1)
            ada_part(3)
            ada_col(2)
            ada_col(3)
            norm(0)
            wait_drained(pe, "nT0a")
            wait_drained(pe, "nT0b")

            def W(i):
                job = f"W{i}"
                if i < 3:
                    turned(job, hT)
                else:
                    natural(job, hT)

            def level(lv):
                job = f"lv{lv}"
                begin(job)
                pe.wait_ge(factors_ready, lv + 1)
                for t in range(T):
                    for h in range(HG):
                        key = t if lv < LEVELS - 1 else t
                        qry = t if lv < LEVELS - 1 else 1 - t
                        ins = mm(bank(job, t)[:, h * P:(h + 1) * P], EK[:, h, key * P:(key + 1) * P],
                                 EQ[:, h, qry * P:(qry + 1) * P], start=True, stop=True)
                end(ins, job)

            def a_scores(t, g):
                job = f"sc{t}{g}"
                begin(job)
                rows = slice(64 * g, 64 * g + 64)
                for i in range(4):
                    ins = mm(bank(job, i // 2)[:, (i % 2) * S:(i % 2 + 1) * S], aqT[rows, i, t * P:(t + 1) * P],
                             akT[rows, :], start=True, stop=True)
                end(ins, job)

            def a_values(t, g, n):
                pe.wait_ge(prob_ready, n + 1)
                turn(f"PT{t}{g}", [prob[n % 2][:, i, k * P:(k + 1) * P] for k in range(2) for i in range(4)])
                job = f"pv{t}{g}"
                begin(job)
                wait_drained(pe, f"PT{t}{g}")
                for k in range(2):
                    ins = mm(PS[64 * g:64 * g + 64, 2 * pair(job), :], va[:, k, 64 * g:64 * g + 64],
                             ptr[:, k].rearrange("p i s -> p (i s)"), start=k == 0, stop=k == 1)
                end(ins, job)

            for i in range(3):
                W(i)
            level(0)
            W(4)
            level(1)
            W(5)
            level(2)
            W(3)
            level(3)
            pe.wait_ge(qk_ready, 2)
            turn("qT", [qk[:, t, i * P:(i + 1) * P] for i in range(4) for t in range(T)])
            turn("kT", [qk[:, t, 512:640] for t in range(T)])
            wait_drained(pe, "qT")
            wait_drained(pe, "kT")
            wait_drained(pe, "W5")
            a_scores(0, 0)
            a_scores(0, 1)
            level(4)
            W(6)
            a_values(0, 0, 0)
            a_values(0, 1, 1)
            level(5)
            a_scores(1, 0)
            a_scores(1, 1)
            level(6)
            a_values(1, 0, 2)
            a_values(1, 1, 3)
            level(7)
            level(8)
            ada_part(4)
            ada_part(5)
            begin("og")
            for lv in (7, 8):
                wait_drained(pe, f"lv{lv}")
            for t in range(T):
                for h in range(HG):
                    for j in range(T):
                        ins = mm(bank("og", t)[:, h * HGD:(h + 1) * HGD], AT[:, j, t, h, :],
                                 gv[:, j, h * HGD:(h + 1) * HGD], start=j == 0, stop=j == 1)
            end(ins, "og")
            ada_row(4)
            ada_row(5)
            W(7)
            W(8)
            pe.wait_ge(ohg_ready, 2)
            turn("ohgT", [ohg[:, t, i * P:(i + 1) * P] for i in range(4) for t in range(T)])
            W(9)
            W(10)
            ada_part(6)
            ada_part(7)
            ada_col(6)
            ada_col(7)
            pe.wait_ge(oatt_low, 1)
            wait_drained(pe, "ohgT")
            for n in range(2):
                branch(f"ya{n}", oattR)
            for n in range(2):
                branch(f"yh{n}", ohgR)
            ada_part(8)
            ada_part(9)
            ada_col(8)
            ada_col(9)
            pe.wait_ge(merged_ready, 4)
            turn_rows(("mTa", "mTb"), merged)
            wait_drained(pe, "mTa")
            wait_drained(pe, "mTb")
            for n in range(2):
                natural(f"mo{n}", hT)
            ada_part(10)
            ada_part(11)
            ada_row(10)
            ada_row(11)
            norm(1)
            wait_drained(pe, "nT1a")
            wait_drained(pe, "nT1b")
            pe.wait_ge(wr_ready, 1)
            begin("rt")
            for t in range(T):
                for k in range(KD):
                    ins = mm3(bank("rt", 0)[:, t * NE:(t + 1) * NE], [a[:, k, t * P:(t + 1) * P] for a in hT],
                              [w[:, k, :] for w in wr], start=k == 0, stop=k == KD - 1)
            end(ins, "rt")
            begin("aT")
            pe.wait_ge(r_ready, 1)
            for t in range(T):
                ins = nc.tensor.transpose(bank("aT", 0)[0:16, t * P:(t + 1) * P], eprob[:, t, :], ident)
            end(ins, "aT")
            begin("ic")
            pe.wait_ge(top_ready, 1)
            for a in range(2):
                ins = nc.tensor.transpose(bank("ic", 0)[:, a * NE:(a + 1) * NE],
                                          erep[0:16, a].rearrange("p j c -> p (j c)"), consts[0:16, C_ID:C_ID + 16])
            end(ins, "ic")
            begin("ib")
            end(mm(bank("ib", 0), mean32[0:16, :], ebd[0:16, :], start=True, stop=True), "ib")
            wait_drained(pe, "ib")
            for q in range(4):
                job = f"ga{q}"
                begin(job)
                for b in range(2):
                    k = 2 * q + b
                    for t in range(T):
                        ins = mm(bank(job, b), xn[:, t, k * P:(k + 1) * P], onehot[:, t, :], start=t == 0, stop=t == 1)
                end(ins, job)

            pe.wait_ge(ws_in, 16)
            turn("wsT", [ws[:, g, :] for g in range(8)])

            for q in range(4):
                wait_drained(pe, f"ga{q}")
            wait_drained(pe, "wsT")
            for b in range(4):
                mm(PS[:, 4 + b, :], zrow[0:1, 0:P], zrow[0:1, :], start=True, stop=False)

            with pe.Fori(0, NE) as e:
                def expert_slab(i):
                    n = AT_EXPERT + i
                    pe.wait_ge(slab_in[slot_of(n)], e * (16 * PER_EXPERT // R) + ARRIVED[n])

                pe.wait_ge(xe_ready, e + 1)
                for side in range(2):
                    for q in range(4):
                        i = 4 * side + q
                        expert_slab(i)
                        w = kn(AT_EXPERT + i, 2)
                        for kk in range(2):
                            for j in range(4):
                                ins = mm(PS[32 * j:32 * j + 32, side, :], xe[:, 2 * q + kk, :],
                                         w[:, kk, j * NB:(j + 1) * NB], start=q == 0 and kk == 0, stop=q == 3 and kk == 1)
                        ins.then_inc(slab_done, 1)
                pe.wait_ge(hid_ready, e + 1)
                for i in range(4):
                    ins = nc.tensor.transpose(PS[:, 0, i * P:(i + 1) * P], hid[:, i * P:(i + 1) * P], ident)
                ins.then_inc(hid_turned, 1)
                pe.wait_ge(hidT_ready, e + 1)
                for i in range(4):
                    expert_slab(8 + i)
                    w = kn(AT_EXPERT + 8 + i, 4)
                    for n in range(2):
                        for j in range(4):
                            ins = mm(PS[32 * j:32 * j + 32, 2 + n, :], hidT[:, i, 32 * j:32 * j + 32],
                                     w[:, j, n * NB:(n + 1) * NB], start=i == 0, stop=i == 3)
                    ins.then_inc(slab_done, 1)
                pe.wait_ge(ye_ready, 2 * e + 2)
                for t in range(T):
                    for n in range(2):
                        mm(PS[:, 4 + 2 * t + n, :], comb[:, t * P:(t + 1) * P], ye[:, n, :], start=False, stop=False)
            for b in range(4):
                ins = mm(PS[:, 4 + b, :], zrow[0:1, 0:P], zrow[0:1, :], start=False, stop=True)
            ins.then_inc(comb_done, 1)

            pe.wait_ge(x_ready, X_EXP)
            norm(2)
            wait_drained(pe, "nT2a")
            wait_drained(pe, "nT2b")
            for j in ("v0", "v1", "u0", "u1"):
                natural(j, hT)
            pe.wait_ge(ln_ready, 2)
            pe.wait_ge(wsT_ready, 1)
            for t in range(T):
                job = f"sv{t}"
                begin(job)
                for g in range(8):
                    ins = mm(bank(job, g // 4)[:, (g % 4) * P:(g % 4 + 1) * P], wsT[:, g, :],
                             V[:, t, g * P:(g + 1) * P], start=True, stop=True)
                end(ins, job)
            wait_drained(pe, "sv0")
            wait_drained(pe, "sv1")
            turn_rows(("pTa", "pTb"), U)
            wait_drained(pe, "pTa")
            wait_drained(pe, "pTb")
            for n in range(2):
                natural(f"am{n}", hT)

            def mlp(layer):
                squares = layer * FJ
                for b in range(4):
                    mm(PS[:, b, :], zrow[0:1, 0:P], zrow[0:1, :], start=True, stop=False)

                c0 = C_FFN[layer]

                def chunk(i, turns):
                    c = c0 + i
                    pe.wait_ge(chunk_low, c + 1 if turns is None else turns * 12 + (c + 1))
                    return [part_of(c, j) for j in range(2)]

                def up(j, i, turns=None):
                    for half in range(2):
                        w = chunk(2 * i + half, turns)
                        if half == 0 and not (isinstance(j, int) and j == 0):
                            pe.wait_ge(relu_ready, j + squares)
                        for b in range(2):
                            for k in range(KD):
                                ins = mm3(PS[:, 4 + half, b * S:(b + 1) * S], [v[:, k, b * P:(b + 1) * P] for v in w],
                                          [a[:, k, :] for a in hT], start=k == 0, stop=k == KD - 1)
                        ins.then_inc(slab_done if half else half_done, 1)

                def down(j, i, b, turns=None):
                    pe.wait_ge(hidden_ready, j + (squares + 1))
                    for half in range(2):
                        w = chunk(2 * i + half, turns)
                        for t in range(T):
                            for h in range(2):
                                for k in range(2):
                                    ins = mm3(PS[:, 2 * t + h, :],
                                              [a[:, b, 2 * half + k, t * P:(t + 1) * P] for a in hidden],
                                              [v[:, k, h * NB:(h + 1) * NB] for v in w], start=False, stop=False)
                        ins.then_inc(slab_done if half else half_done, 1)

                up(0, 0)
                with pe.Fori(0, 2) as it:
                    for jj in range(1, 4):
                        up(it * 3 + jj, 2 * jj - 1, it)
                        down(it * 3 + (jj - 1), 2 * jj, (jj - 1) % 3, it)
                up(7, 13)
                down(6, 14, 0)
                down(7, 15, 1)
                for b in range(4):
                    ins = mm(PS[:, b, :], zrow[0:1, 0:P], zrow[0:1, :], start=False, stop=True)
                ins.then_inc(mlp_done, 1)

            norm(3)
            wait_drained(pe, "nT3a")
            wait_drained(pe, "nT3b")
            mlp(0)
            norm(4)
            wait_drained(pe, "nT4a")
            wait_drained(pe, "nT4b")
            for j in ("bk0", "bk1"):
                turned(j, hR)
            for j in ("bq0", "bq1"):
                turned(j, hT)
            for j in ("bv0", "bv1"):
                natural(j, hR)

            def b_scores(n):
                job = f"bs{n}"
                begin(job)
                t, per, k0 = (0, 4, P) if n < 2 else (1, 2, 0)
                b0 = 4 * n if n < 2 else 2 * (n - 2)
                w = S - k0
                for g in range(2):
                    rows = slice(64 * g, 64 * g + 64)
                    for i in range(per):
                        ins = mm(bank(job, g)[:, i * w:(i + 1) * w], bqT[rows, b0 + i, t * P:(t + 1) * P],
                                 bkT[rows, b0 + i, k0:S], start=True, stop=True)
                end(ins, job)

            def b_turn(n):
                pe.wait_ge(prob_ready, 5 + n)
                turn(f"bT{n}", [bp[n % 4][:, i * P:(i + 1) * P] for i in range(8)])

            def b_values(n):
                job = f"bo{n}"
                begin(job)
                wait_drained(pe, f"bT{n}")
                per = 4 if n < 2 else 2
                b0 = 4 * n if n < 2 else 2 * (n - 2)
                for g in range(2):
                    for i in range(per):
                        h = 2 * (b0 + i) + g
                        for kb in ((1,) if n < 2 else (0, 1)):
                            blk = g * 4 + (i if n < 2 else 2 * i + kb)
                            ins = mm(PS[64 * g:64 * g + 64, 2 * pair(job), i * P:(i + 1) * P],
                                     vR[:, kb, h * BHD:(h + 1) * BHD], bpt[n % 2][:, blk * P:(blk + 1) * P],
                                     start=n < 2 or kb == 0, stop=n < 2 or kb == 1)
                end(ins, job)

            for j in ("bk0", "bk1", "bq0", "bq1"):
                wait_drained(pe, j)
            b_scores(0)
            b_scores(1)
            wait_drained(pe, "bv0")
            wait_drained(pe, "bv1")
            b_scores(2)
            for n in range(6):
                b_turn(n)
                if n < 3:
                    b_scores(n + 3)
                b_values(n)
            for n in range(6):
                wait_drained(pe, f"bo{n}")
            for n in range(2):
                natural(f"bm{n}", hT)
            norm(5)
            wait_drained(pe, "nT5a")
            wait_drained(pe, "nT5b")
            mlp(1)


_INS = ["x", "c", "ada_w", "ada_b", "norm_mix_w", "norm_ffn_w", "w_in", "q_norm_w", "k_norm_w", "hg_lower_bounds",
        "hg_norm_w", "w_branch_att", "w_branch_hg", "w_out", "w_router", "w_exp_gate", "w_exp_up", "w_exp_down",
        "norm_g_2", "a_w_in_2", "a_ln_g_2", "a_ln_b_2", "a_w_s_2", "a_b_s_2", "a_w_out_2", "kv_norm_g_2", "w_k_2",
        "w_v_2", "b_w_q_2", "b_rel_bias_2", "b_w_o_2", "w_up_2", "w_down_2"]


def constants():
    import numpy as np

    c = np.zeros((P, C_END), np.float32)
    i = np.arange(P)
    c[:, C_ID:C_ID + P] = np.eye(P)
    parted = i[:, None] ^ i[None, :]
    masks = np.concatenate([(parted >> lv) == 1 for lv in range(7)], axis=1).astype(np.int16)
    c[:, C_MASK:C_MASK + 7 * P // 2] = masks.view(np.float32)
    c[:, C_IOTA:C_IOTA + S] = np.arange(S)[None, :]
    for t in range(T):
        tok = t * P + i
        c[:, C_TOK + t] = tok
        inv = np.float32(10000.0) ** (-np.arange(0, 32, 2, dtype=np.float32) / np.float32(32))
        pos = np.stack([(tok // 64), (tok % 64)], axis=1).astype(np.float32)
        ang = (pos[:, :, None] * inv.astype(np.float32)).reshape(P, 32)
        c[:, C_ROPE + 64 * t:C_ROPE + 64 * t + 32] = np.cos(ang)
        c[:, C_ROPE + 64 * t + 32:C_ROPE + 64 * t + 64] = np.sin(ang)
    return c, np.repeat(np.eye(NE, dtype=np.float32) * 32, CAP, axis=1)


def kernel(**inputs):
    import numpy as _np
    import concourse.bacc as _bacc
    from concourse.bass_utils import run_bass_kernel_spmd as _run

    nc = _bacc.Bacc("TRN2", target_bir_lowering=False, num_devices=1)
    arrays, aps = {}, {}
    consts, blockdiag = constants()
    own = {"consts": consts, "blockdiag": blockdiag}
    for name in _INS + list(own):
        a = own[name] if name in own else _np.ascontiguousarray(inputs[name])
        arrays[f"in_{name}_dram"] = a
        aps[name] = nc.dram_tensor(f"in_{name}_dram", a.shape, mybir.dt.from_np(a.dtype), kind="ExternalInput").ap()
    out = nc.dram_tensor("out_0_dram", (1, S, D), F32, kind="ExternalOutput").ap()
    build(nc, aps, out)
    r = _run(nc, [arrays], core_ids=[0])
    return r.results[0]["out_0_dram"]
```

```python
from contextlib import ExitStack

import concourse.bass as bass
from concourse import mybir

F32 = mybir.dt.float32
F32R = mybir.dt.float32r
BF16 = mybir.dt.bfloat16
U32 = mybir.dt.uint32
I16 = mybir.dt.int16
ALU = mybir.AluOpType
ACT = mybir.ActivationFunctionType
AX = mybir.AxisListType.X

P = 128
S = 256
T = S // P
D = 1024
KD = D // P
NB = 512
SLOT = KD * NB
R = 6
RS = 3
NC = 3
CHUNK = SLOT // 2

AH, AHD = 8, 64
HG, HGD = 4, 128
LEVELS = 9
NE, CAP, FF = 16, 32, 2048
PER_EXPERT = 12
FFH = 4096
FJ = FFH // NB
BHEADS, BHD = 16, 64
EPS, LN_EPS, MIN_F = 1e-6, 1e-5, 1e-6
NEG = -1e30

C_ID, C_MASK, C_IOTA, C_TOK, C_ROPE = 0, 128, 576, 832, 834
C_SUM = 962
C_END = 978
V_C, V_NM, V_NF, V_GA0, V_GA2, V_GB0, V_GB2, V_KV, V_BS, V_LB, V_AB = (8 * i for i in range(11))

JOBS = (
    [("vecT", 1)]
    + [(j, 1) for j in ("ada0", "ada1", "adc0", "ada2", "adc1", "ada3", "adc2", "adc3")]
    + [("nT0a", 2), ("nT0b", 2)]
    + [("W1", 2), ("W2", 2), ("W0", 2), ("lv0", 2), ("W4", 2), ("lv1", 2), ("W5", 2), ("lv2", 2), ("W3", 2)]
    + [("lv3", 2), ("ada6", 1), ("adc6", 1), ("qT", 2), ("kT", 1), ("sc00", 2), ("sc01", 2), ("lv4", 2), ("W6", 2)]
    + [("PT00", 2), ("pv00", 1), ("PT01", 2), ("pv01", 1), ("lv5", 2), ("sc10", 2), ("sc11", 2), ("ada7", 1)]
    + [("lv6", 2), ("adc7", 1), ("PT10", 2), ("ada8", 1), ("pv10", 1), ("PT11", 2), ("adc8", 1), ("pv11", 1)]
    + [("lv7", 2), ("ada9", 1), ("W7", 2), ("lv8", 2), ("adc9", 1), ("ada4", 1), ("og", 2), ("ada5", 1), ("W8", 2)]
    + [("adr4", 1), ("adr5", 1), ("ohgT", 2), ("W9", 2), ("W10", 2), ("ya0", 2), ("ya1", 2), ("yh0", 2), ("yh1", 2)]
    + [("ada10", 1), ("mTa", 2), ("mTb", 2), ("mo0", 2), ("adr10", 1), ("ada11", 1), ("mo1", 2), ("adr11", 1)]
    + [("nT1a", 2), ("nT1b", 2), ("rt", 1), ("rl", 1), ("aT", 1), ("ic", 1), ("ib", 1)]
    + [("ga0", 2), ("ga1", 2), ("ga2", 2), ("ga3", 2), ("wsT", 2)]
    + [("nT2a", 2), ("nT2b", 2), ("v0", 2), ("v1", 2), ("u0", 2), ("u1", 2)]
    + [("sv0", 2), ("sv1", 2), ("pTa", 2), ("pTb", 2), ("am0", 2), ("am1", 2), ("nT3a", 2), ("nT3b", 2)]
    + [("nT4a", 2), ("nT4b", 2), ("bk0", 2), ("bk1", 2), ("bq0", 2), ("bq1", 2), ("bv0", 2), ("bv1", 2)]
    + [("bs0", 2), ("bs1", 2), ("bs2", 2), ("bT0", 2), ("bs3", 2), ("bo0", 1), ("bT1", 2), ("bs4", 2), ("bo1", 1)]
    + [("bT2", 2), ("bs5", 2), ("bo2", 1), ("bT3", 2), ("bo3", 1), ("bT4", 2), ("bo4", 1), ("bT5", 2), ("bo5", 1)]
    + [("bm0", 2), ("bm1", 2), ("nT5a", 2), ("nT5b", 2)]
)
JOB_AT = {name: i for i, (name, _) in enumerate(JOBS)}
DRAINED = [sum(n for j, (_, n) in enumerate(JOBS) if j % 4 == i % 4 and j <= i) for i in range(len(JOBS))]

FIRST_SLABS = (
    [(f"ada{i}", f"ada{i}") for i in range(4)]
    + [(n, n) for n in ("W1", "W2", "W0", "W4", "W5", "W3", "ada6", "W6", "ada7", "ada8", "ada9", "W7", "W8")]
    + [("ada4", "ada4"), ("ada5", "ada5"), ("W9", "W9"), ("W10", "W10"), ("att", "ya1"), ("hg", "yh1")]
    + [("ada10", "ada10"), ("out0", "mo0"), ("ada11", "ada11"), ("out1", "mo1")]
)
A_SLABS = [("v0", "v0"), ("v1", "v1"), ("u0", "u0"), ("u1", "u1"), ("am0", "am0"), ("am1", "am1")]
B_SLABS = [(j, j) for j in ("bk0", "bk1", "bq0", "bq1", "bv0", "bv1", "bm0", "bm1")]
N_FIRST = len(FIRST_SLABS)
N_EXPERT = NE * PER_EXPERT
AT_EXPERT = N_FIRST
AT_A = AT_EXPERT + N_EXPERT
AT_FFN = [AT_A + len(A_SLABS), AT_A + len(A_SLABS) + 2 * FJ + len(B_SLABS)]
AT_B = AT_FFN[0] + 2 * FJ
SLAB_AT = {name: i for i, (name, _) in enumerate(FIRST_SLABS)}
SLAB_AT |= {name: AT_A + i for i, (name, _) in enumerate(A_SLABS)}
SLAB_AT |= {name: AT_B + i for i, (name, _) in enumerate(B_SLABS)}

def cut_of(name):
    if name in ("W0", "W1", "W2", "bk0", "bk1", "bq0", "bq1"):
        return "n", (None, name)
    if name in ("att", "hg"):
        job = {"att": "ya", "hg": "yh"}[name]
        return "n4", (f"{job}0", f"{job}1")
    return "k", (None, {"out0": "mo0", "out1": "mo1"}.get(name, name))


CHUNKS = []
CHUNK_OF = {}


def add_chunks(slabs, at):
    for i, (name, _) in enumerate(slabs):
        if not name.startswith("ada"):
            how, jobs = cut_of(name)
            for half, job in enumerate(jobs):
                CHUNK_OF[job or jobs[1]] = min(CHUNK_OF.get(job or jobs[1], len(CHUNKS)), len(CHUNKS))
                CHUNKS.append((at + i, how, half, job))


def add_mlp_chunks(layer):
    for i, (kind, _) in enumerate(FFN_ORDER):
        CHUNKS.extend((AT_FFN[layer] + i, "n" if kind == "up" else "k", half, None) for half in range(2))


FFN_ORDER = [("up", 0)] + [x for j in range(1, FJ) for x in (("up", j), ("down", j - 1))] + [("down", FJ - 1)]
add_chunks(FIRST_SLABS, 0)
C_A = len(CHUNKS)
add_chunks(A_SLABS, AT_A)
C_FFN = [len(CHUNKS)]
add_mlp_chunks(0)
C_B = len(CHUNKS)
add_chunks(B_SLABS, AT_B)
C_FFN.append(len(CHUNKS))
add_mlp_chunks(1)


def slot_of(n):
    if n < AT_EXPERT:
        return n % RS
    return (n - AT_EXPERT) % R if n < AT_A else (n - AT_A) % RS


ARRIVED, BEFORE, _count, _last = [], [], [0] * R, [None] * R
for _n in range(AT_FFN[1] + 2 * FJ):
    _s = slot_of(_n)
    _count[_s] += 32 if _n == SLAB_AT["att"] else 16
    ARRIVED.append(_count[_s])
    BEFORE.append(_last[_s])
    _last[_s] = _n
LAST_CHUNK = {n: c for c, (n, _, _, _) in enumerate(CHUNKS)}
SPLIT_JOBS = ["nT0a", "nT0b", "ohgT", "mTa", "mTb", "nT1a", "nT1b", "nT2a", "nT2b", "pTa", "pTb", "nT3a", "nT3b",
              "nT4a", "nT4b", "nT5a", "nT5b"]
W_COLS = {"W0": 768, "W1": 1280, "W2": 1792, "W3": 2304, "W4": 0, "W5": 512, "W6": 2816,
          "W7": 3328, "W8": 3840, "W9": 4352, "W10": 4864}


def build(nc, A, out):
    with ExitStack() as ctx:
        def sb(name, shape, dt=F32):
            return ctx.enter_context(nc.sbuf_tensor(name, shape, dt))

        def sem(name):
            return ctx.enter_context(nc.semaphore(name))

        PS = ctx.enter_context(nc.psum_tensor("PS", [P, 8, NB], F32))

        ring_a = sb("ring_a", [P, RS, SLOT])
        with nc.sbuf_tensor("ring_b", [P, R - RS, SLOT], F32) as ring_b:
            pass
        parts = sb("parts", [P, NC, 2, CHUNK], F32R)
        x = sb("x", [P, T, D])
        xn = sb("xn", [P, T, D])
        hT = [sb(f"hT{i}", [P, KD, S], F32R) for i in range(2)]
        consts = sb("consts", [P, C_END])
        vcol = sb("vcol", [P, P])
        modc = sb("modc", [P, 48])
        aff1 = sb("aff1", [P, KD])
        aff2 = sb("aff2", [P, KD])
        crep = sb("crep", [P, KD, 32])
        csil = sb("csil", [P, KD])
        wr = sb("wr", [P, KD, 32])
        mean32 = sb("mean32", [P, P])
        zrow = sb("zrow", [1, NB], BF16)
        junk = sb("junk", [P, D], BF16)
        tmp = sb("tmp", [P, D])
        vrow = tmp[:, 0:P]
        ssq = sb("ssq", [P, 6, T, 2])
        std = sb("std", [P, 6, T])
        rstd = sb("rstd", [P, 6, T])
        small = sb("small", [P, 256])
        with nc.sbuf_tensor("arena", [P, 16 * 1024], F32) as arena:
            pass
        rounded = sb("rounded", [P, 16 * 1024], F32R)

        def at(kb, cols):
            return arena[:, kb * 256:kb * 256 + cols]

        def rat(kb, cols):
            return rounded[:, kb * 256:kb * 256 + cols]

        ident = consts[:, C_ID:C_ID + P]
        masks = consts[:, C_MASK:C_MASK + 7 * P // 2].bitcast(I16)
        iota = consts[:, C_IOTA:C_IOTA + S]
        rope = consts[:, C_ROPE:C_ROPE + 128].rearrange("p (t f a i) -> p t f a i", t=T, f=2, a=2)
        blockdiag = at(24, 512)[0:16, :]

        part = at(32, 2 * NB).rearrange("p (b n) -> p b n", b=2)
        part2 = junk[:, :].bitcast(F32)
        gq = at(0, 1024).rearrange("p (h s) -> p h s", h=HG)
        gkf = at(4, 1024).rearrange("p (h s) -> p h s", h=HG)
        gkb = at(8, 1024).rearrange("p (h s) -> p h s", h=HG)
        PF = at(12, 1024).rearrange("p (h s) -> p h s", h=HG)
        XF = at(16, 1024).rearrange("p (h s) -> p h s", h=HG)
        PB = at(20, 1024).rearrange("p (h s) -> p h s", h=HG)
        XB = at(24, 1024).rearrange("p (h s) -> p h s", h=HG)
        EK = at(28, 1024).rearrange("p (h s) -> p h s", h=HG)
        EQ = at(32, 1024).rearrange("p (h s) -> p h s", h=HG)
        AT = at(36, 2048).rearrange("p (j i h s) -> p j i h s", j=T, i=T, h=HG)
        gv = at(44, 1024).rearrange("p (t n) -> p t n", t=T)
        hgate = at(48, 1024).rearrange("p (t n) -> p t n", t=T)
        qk = at(52, 1280).rearrange("p (t n) -> p t n", t=T)
        va = at(57, 256).rearrange("p (t n) -> p t n", t=T)
        aqT = at(58, 1024).rearrange("p (i s) -> p i s", i=4)
        akT = at(62, 256)
        wqk = at(63, 128)
        hgw = at(63, 256)[:, P:2 * P]
        oattT = at(52, 1024)
        oattR = [rat(kb, 1024).rearrange("p (i s) -> p i s", i=4) for kb in (56, 60)]
        prob = [xn[:, b, :].rearrange("p (i s) -> p i s", i=4) for b in range(2)]
        ptr = tmp[:, :].rearrange("p (k i s) -> p k i s", k=2, i=4)
        ohg = at(0, 1024).rearrange("p (t n) -> p t n", t=T)
        ohgR = [rat(kb, 1024).rearrange("p (i s) -> p i s", i=4) for kb in (4, 28)]
        gate1 = at(8, 1024)
        gsig = at(12, 4096).rearrange("p (b t n) -> p b t n", b=2, t=T)
        merged = xn

        xeT = at(0, 4096).rearrange("p (k c) -> p k c", k=KD)
        onehot = rat(16, 1024).rearrange("p (t c) -> p t c", t=T)
        gate2 = at(36, 1024)
        xe = at(20, 256).rearrange("p (k c) -> p k c", k=KD)
        sg = at(21, 512)
        logits = at(21, 256)
        hid = at(23, 512)
        hidT = at(25, 512).rearrange("p (i m) -> p i m", i=4)
        ye = at(27, 1024).rearrange("p (n m) -> p n m", n=2)
        comb = at(31, 256)
        eprob = at(40, 32).rearrange("p (t e) -> p t e", t=T)
        etop = at(41, 256)
        eidx = at(42, 64)
        etop2 = at(43, 256)
        erep = at(44, 256).rearrange("p (a j c) -> p a j c", a=2, j=4)
        ebd = at(45, 512)
        ecol = at(47, 32).rearrange("p (a e) -> p a e", a=2)

        xn_parts = [h[:, :, :].rearrange("p k s -> p (k s)") for h in hT]

        V = at(0, 2048).rearrange("p (t n) -> p t n", t=T)
        U = at(8, 2048).rearrange("p (t n) -> p t n", t=T)
        ws = tmp[:, :].rearrange("p (g j) -> p g j", g=8)
        wsT = at(16, 1024).rearrange("p (g i) -> p g i", g=8)
        lng = at(32, 1024)
        lnb = at(36, 1024)
        grows = [at(kb, 1024) for kb in (28, 28, 16, 28)]
        hidden = [rat(kb, 3072).rearrange("p (b i s) -> p b i s", b=3, i=4) for kb in (0, 12)]
        rl = at(24, 1024)
        sqr = at(32, 1024)
        hR = [rat(kb, 2048).rearrange("p (k s) -> p k s", k=KD) for kb in (0, 8)]
        bp = [at(kb, 1024) for kb in (0, 4, 8, 12)]
        bqT = at(16, 2048).rearrange("p (k s) -> p k s", k=KD)
        bkT = at(24, 2048).rearrange("p (k s) -> p k s", k=KD)
        vR = at(32, 2048).rearrange("p (t n) -> p t n", t=T)
        bpt = [at(40, 1024), at(44, 1024)]
        bias = at(48, 4096).rearrange("p (h m) -> p h m", h=BHEADS)

        psum_full = [sem(f"psum_full{i}") for i in range(4)]
        psum_drained = [sem(f"psum_drained{i}") for i in range(4)]
        slab_in = [sem(f"slab_in{i}") for i in range(R)]
        chunk_high, chunk_low = sem("chunk_high"), sem("chunk_low")
        half_done = sem("half_done")
        high_out = sem("high_out")
        slot_passed = sem("slot_passed")
        slab_done = sem("slab_done")
        consts_in, x_in, rows_in, wr_in = (sem(n) for n in ("consts_in", "x_in", "rows_in", "wr_in"))
        vrow_in, vrow_in2 = sem("vrow_in"), sem("vrow_in2")
        bias1_in, ln_in, ws_in, bias_in, out_written = (
            sem(n) for n in ("bias1_in", "ln_in", "ws_in", "bias_in", "out_written"))
        grow_in = [sem(f"grow_in{i}") for i in range(2)]
        filled = sem("filled")
        norm_ssq, norm_var, norm_std, norm_rstd = (sem(n) for n in ("norm_ssq", "norm_var", "norm_std", "norm_rstd"))
        xn_ready = [sem(f"xn_ready{h}") for h in range(2)]
        tile_full = sem("tile_full")
        x_ready = sem("x_ready")
        crep_ready, c_silu, lb_in, lb_exp, lb_ready, aff_ready = (
            sem(n) for n in ("crep_ready", "c_silu", "lb_in", "lb_exp", "lb_ready", "aff_ready"))
        forget_ready, log_in, log_ready, k_ready = (sem(n) for n in ("forget_ready", "log_in", "log_ready", "k_ready"))
        exp_ready, sums_ready, factors_ready = (sem(n) for n in ("exp_ready", "sums_ready", "factors_ready"))
        qk_var, qk_std, qk_rstd = (sem(n) for n in ("qk_var", "qk_std", "qk_rstd"))
        qk_ready = [sem(f"qk_ready{t}") for t in range(T)]
        row_max, row_exp, prob_ready = (sem(n) for n in ("row_max", "row_exp", "prob_ready"))
        hgate_ready, o_ssq, o_var, o_std, ohg_ready = (
            sem(n) for n in ("hgate_ready", "o_ssq", "o_var", "o_std", "ohg_ready"))
        merged_ready = sem("merged_ready")
        r_max, r_exp, r_ready, top_ready = (sem(n) for n in ("r_max", "r_exp", "r_ready", "top_ready"))
        xe_ready, silu_ready, hid_ready, hid_turned, hidT_ready, ye_ready, comb_done = (
            sem(n) for n in ("xe_ready", "silu_ready", "hid_ready", "hid_turned", "hidT_ready", "ye_ready", "comb_done"))
        ln_var, ln_std, ln_ready = (sem(n) for n in ("ln_var", "ln_std", "ln_ready"))
        post_ssq, post_var, post_std = (sem(n) for n in ("post_ssq", "post_var", "post_std"))
        relu_ready, sqr_ready, sqr_high, hidden_ready = (
            sem(n) for n in ("relu_ready", "sqr_ready", "sqr_high", "hidden_ready"))
        low_out = sem("low_out")
        kv_low, q_high = sem("kv_low"), sem("q_high")
        oatt_high, oatt_low, bd_in, rows_high, rows_low, wsT_ready = (
            sem(n) for n in ("oatt_high", "oatt_low", "bd_in", "rows_high", "rows_low", "wsT_ready"))
        dve_step, pool_step = sem("dve_step"), sem("pool_step")
        grow_free, bias_masked = sem("grow_free"), sem("bias_masked")

        X_MIX, X_EXP, X_GM, X_F0, X_AT = (4 * i for i in range(1, 6))

        def pair(job):
            return JOB_AT[job] % 4

        def banks(job):
            p = 2 * pair(job)
            return PS[:, p:p + 2, :]

        def bank(job, b):
            return PS[:, 2 * pair(job) + b, :]

        def wait_full(eng, job):
            eng.wait_ge(psum_full[pair(job)], JOB_AT[job] // 4 + 1)

        def wait_drained(eng, job):
            eng.wait_ge(psum_drained[pair(job)], DRAINED[JOB_AT[job]])

        def wait_slab(eng, n):
            eng.wait_ge(slab_in[slot_of(n)], ARRIVED[n])

        def slot(n):
            i = slot_of(n)
            return ring_a[:, i, :] if i < RS else ring_b[:, i - RS, :]

        def kn(n, k=KD):
            return slot(n).rearrange("p (k n) -> p k n", k=k)

        def chunk_shape(c):
            n, how, half, _ = CHUNKS[c]
            if n == SLAB_AT["W5"]:
                return 4, 256
            if how == "k":
                return (2, D) if is_down(n) else (4, NB)
            return (8, 256) if how == "n" else (4, NB)

        def is_down(n):
            return any(a <= n < a + 2 * FJ and FFN_ORDER[n - a][0] == "down" for a in AT_FFN)

        def raw(c):
            n, how, half, _ = CHUNKS[c]
            k, w = chunk_shape(c)
            if how == "k":
                return (kn(n, 4) if is_down(n) else kn(n))[:, half * k:(half + 1) * k, 0:w]
            return kn(n, k)[:, :, half * w:(half + 1) * w]

        def part_of(c, low):
            k, w = chunk_shape(c)
            return parts[:, c % NC, low, 0:k * w].rearrange("p (k n) -> p k n", k=k)

        def wait_used(eng, c):
            job = CHUNKS[c][3]
            if job:
                wait_full(eng, job)
            elif CHUNKS[c][2] == 1:
                eng.wait_ge(slab_done, done_count(CHUNKS[c][0]))
            else:
                eng.wait_ge(half_done, HALF_COUNT[c])

        HALF_COUNT = {}
        for c, (_, how, half, job) in enumerate(CHUNKS):
            if half == 0 and job is None:
                HALF_COUNT[c] = len(HALF_COUNT) + 1

        def high_count(job, b):
            return 2 * SPLIT_JOBS.index(job) + b + 1

        def done_count(n):
            if n < AT_A:
                return n - AT_EXPERT + 1
            if n < AT_B:
                return N_EXPERT + n - AT_FFN[0] + 1
            return N_EXPERT + 2 * FJ + n - AT_FFN[1] + 1

        def split(ap, s):
            v = ap.rearrange("p h s -> p (h s)").rearrange("p (m a s) -> p a m s", a=2, s=s)
            return v[:, 0], v[:, 1]

        def hankel(table):
            v = table[0, :, 129:129 + S]
            return bass.AP(tensor=v.tensor, offset=v.offset, ap=[[1, P], [table.shape[2], BHEADS], [1, S]])

        def by_rows(v):
            return v.rearrange("(k p) -> k p", p=P)

        VECTORS = [(V_AB, by_rows(A["ada_b"][0])), (V_C, by_rows(A["c"][0])), (V_NM, by_rows(A["norm_mix_w"][0])),
                   (V_NF, by_rows(A["norm_ffn_w"][0])), (V_GA0, by_rows(A["norm_g_2"][0, 0])),
                   (V_GA2, by_rows(A["norm_g_2"][0, 2])), (V_GB0, by_rows(A["norm_g_2"][1, 0])),
                   (V_GB2, by_rows(A["norm_g_2"][1, 2])), (V_KV, by_rows(A["kv_norm_g_2"])),
                   (V_BS, A["a_b_s_2"][0]), (V_LB, A["hg_lower_bounds"][0].rearrange("a (h p) -> (a h) p", p=P))]

        def rotate(eng, link, t, scratch):
            q10 = qk[:, t, :].rearrange("p (h d) -> p h d", d=AHD)
            eng.tensor_tensor(q10[:, 0:8, :], q10[:, 0:8, :], wqk[:, 0:64].unsqueeze(1).broadcast_to([P, 8, 64]), ALU.mult)
            link(eng.tensor_tensor(q10[:, 8:10, :], q10[:, 8:10, :],
                                   wqk[:, 64:128].unsqueeze(1).broadcast_to([P, 2, 64]), ALU.mult))
            halves = qk[:, t, :].rearrange("p (h a f i) -> p f h a i", h=10, a=2, f=2)
            x1, x2 = halves[:, 0], halves[:, 1]
            cos = rope[:, t, 0].unsqueeze(1).broadcast_to([P, 10, 2, 16])
            sin = rope[:, t, 1].unsqueeze(1).broadcast_to([P, 10, 2, 16])
            r = [v.rearrange("p (h a i) -> p h a i", h=10, a=2) for v in scratch]
            eng.tensor_tensor(r[0], x1, cos, ALU.mult)
            eng.tensor_tensor(r[1], x2, sin, ALU.mult)
            eng.tensor_tensor(r[2], x2, cos, ALU.mult)
            link(eng.tensor_tensor(r[3], x1, sin, ALU.mult))
            eng.tensor_tensor(x1, r[0], r[1], ALU.subtract)
            eng.tensor_tensor(x2, r[2], r[3], ALU.add).then_inc(qk_ready[t], 1)

        block = ctx.enter_context(nc.Block())

        @block.sync
        def _(sp):
            def slab_free(n):
                before = BEFORE[n]
                if AT_EXPERT + RS <= n < AT_EXPERT + R:
                    wait_used(sp, C_A - 1)
                elif before is None:
                    return
                elif before in LAST_CHUNK:
                    sp.wait_ge(chunk_low, LAST_CHUNK[before] + 1)
                elif before < AT_EXPERT:
                    wait_full(sp, FIRST_SLABS[before][1])
                else:
                    sp.wait_ge(slab_done, done_count(before))

            def load(n, src, k=KD, dst=None):
                slab_free(n)
                sp.dma_start(kn(n, k) if dst is None else dst, src).then_inc(slab_in[slot_of(n)], 16)

            def columns(w, n0, width=NB):
                return w[:, n0:n0 + width].rearrange("(k p) n -> p k n", p=P)

            for v, src in VECTORS[:4]:
                sp.dma_start(vrow[v:v + src.shape[0], :], src).then_inc(vrow_in, 16)
            for name, _ in FIRST_SLABS:
                n = SLAB_AT[name]
                if n == 1:
                    sp.wait_ge(vrow_in, 16 * 8)
                    sp.wait_ge(vrow_in2, 16 * 3)
                if name.startswith("ada"):
                    load(n, columns(A["ada_w"][0], int(name[3:]) * NB))
                elif name == "W5":
                    load(n, columns(A["w_in"][0], W_COLS[name], 256), dst=kn(n)[:, :, 0:256])
                elif name.startswith("W"):
                    load(n, columns(A["w_in"][0], W_COLS[name]))
                elif name == "att":
                    for g in range(2):
                        src = A["w_branch_att"][0, g * 256:(g + 1) * 256, :].rearrange("(i d) n -> d i n", d=AHD)
                        load(n, src, dst=kn(n, 4)[64 * g:64 * g + 64])
                elif name == "hg":
                    load(n, A["w_branch_hg"][0].rearrange("(k p) n -> p k n", p=P), 4)
                else:
                    load(n, columns(A["w_out"][0], int(name[3:]) * NB))

            def expert_slab(e, i):
                if i < 8:
                    w = A["w_exp_gate"] if i < 4 else A["w_exp_up"]
                    return w[0, e, (i % 4) * 256:(i % 4 + 1) * 256, :].rearrange("(k p) n -> p k n", p=P), 2
                rows = A["w_exp_down"][0, e].rearrange("(j i p) n -> i p j n", j=4, p=P)
                return rows[i - 8], 4

            for i in range(R):
                load(AT_EXPERT + i, *expert_slab(0, i))
            with sp.Fori(0, NE - 1) as e:
                for i in range(PER_EXPERT):
                    ahead = R + i
                    sp.wait_ge(slab_done, e * PER_EXPERT + (i + 1))
                    sp.sem_inc(slot_passed, 1)
                    src, k = expert_slab(e + ahead // PER_EXPERT, ahead % PER_EXPERT)
                    sp.dma_start(kn(AT_EXPERT + ahead, k), src).then_inc(slab_in[slot_of(AT_EXPERT + ahead)], 16)
            for i in range(R, PER_EXPERT):
                load(AT_EXPERT + (NE - 1) * PER_EXPERT + i, *expert_slab(NE - 1, i))

            def mlp_slabs(layer):
                up, down = A["w_up_2"][layer], A["w_down_2"][layer]
                for i, (kind, j) in enumerate(FFN_ORDER):
                    if kind == "up":
                        load(AT_FFN[layer] + i, columns(up, j * NB))
                    else:
                        load(AT_FFN[layer] + i,
                             down[j * NB:(j + 1) * NB, :].rearrange("(k p) n -> p k n", p=P), 4)

            for name, _ in A_SLABS:
                w = A["a_w_out_2"] if name.startswith("am") else A["a_w_in_2"]
                load(SLAB_AT[name], columns(w[0], int(name[-1]) * NB + (D if name[0] == "v" else 0)))
            mlp_slabs(0)
            for name, _ in B_SLABS:
                w = {"bk": A["w_k_2"], "bv": A["w_v_2"], "bq": A["b_w_q_2"][0], "bm": A["b_w_o_2"][0]}[name[:2]]
                load(SLAB_AT[name], columns(w, int(name[-1]) * NB))
            mlp_slabs(1)
            for t in range(T):
                sp.wait_ge(x_ready, X_AT + 2 * t + 2)
                sp.dma_start(out[0, t * P:(t + 1) * P, :], x[:, t, :]).then_inc(out_written, 16)
            sp.wait_ge(out_written, 32)


        @block.gpsimd
        def _(pool):
            steps = [0]

            def link(ins):
                steps[0] += 1
                ins.then_inc(pool_step, 1)
                pool.wait_ge(pool_step, steps[0])

            pool.memset(mean32[:, :], 1.0 / 32).then_inc(filled, 1)
            for v, src in VECTORS[8:]:
                pool.dma_start(vrow[v:v + src.shape[0], :], src).then_inc(vrow_in2, 16)
            pool.memset(zrow[:, :], 0.0).then_inc(filled, 1)
            link(pool.memset(wr[:, :, :], 0.0))
            pool.dma_start(wr[:, :, 0:NE], A["w_router"][0].rearrange("(k p) e -> p k e", p=P)).then_inc(wr_in, 16)
            pool.dma_start(wqk[:, 0:64], A["q_norm_w"][0].partition_broadcast(P)).then_inc(rows_in, 16)
            pool.dma_start(wqk[:, 64:128], A["k_norm_w"][0].partition_broadcast(P)).then_inc(rows_in, 16)
            pool.dma_start(hgw[:, :], A["hg_norm_w"][0].partition_broadcast(P)).then_inc(rows_in, 16)

            def low_parts(jobs):
                for half, job in enumerate(jobs):
                    for b in range(2):
                        k0 = 4 * half + 2 * b
                        high, low = (h[:, k0:k0 + 2, :].rearrange("p k s -> p (k s)") for h in hT)
                        pool.wait_ge(psum_drained[pair(job)], DRAINED[JOB_AT[job]] - 1 + b)
                        pool.tensor_tensor(low, tmp[:, b * NB:(b + 1) * NB], high.bitcast(F32), ALU.subtract)\
                            .then_inc(low_out, 1)

            low_parts(("nT0a", "nT0b"))
            pool.wait_ge(lb_ready, 1)
            for d, (f, k) in enumerate(((PF, gkf), (PB, gkb))):
                wait_drained(pool, f"W{d + 1}")
                for h in range(HG):
                    c = d * HG + h
                    pool.tensor_scalar(f[:, h, :], f[:, h, :], small[:, 8 + c:9 + c], small[:, c:c + 1],
                                       ALU.mult, ALU.add).then_inc(forget_ready, 1)
                for h in range(HG):
                    c = d * HG + h
                    pool.tensor_scalar(k[:, h, :], k[:, h, :], small[:, 8 + c:9 + c], 0.0,
                                       ALU.mult, ALU.add).then_inc(k_ready, 1)
            pool.memset(XF, 0.0).then_inc(filled, 1)
            pool.memset(XB, 0.0).then_inc(filled, 1)

            def sums(lv):
                s = 1 << (lv - 1)
                pool.wait_ge(exp_ready, lv)
                (pfl, pfr), (xfl, _) = split(PF, s), split(XF, s)
                (pbl, pbr), (_, xbr) = split(PB, s), split(XB, s)
                wide = [P, HG * S // (2 * s), s]
                pool.tensor_tensor(xfl, xfl, pfr[:, :, s - 1:s].broadcast_to(wide), ALU.add)
                link(pool.tensor_tensor(xbr, xbr, pbl[:, :, 0:1].broadcast_to(wide), ALU.add))
                pool.tensor_tensor(pfr, pfr, pfl[:, :, s - 1:s].broadcast_to(wide), ALU.add)
                pool.tensor_tensor(pbl, pbl, pbr[:, :, 0:1].broadcast_to(wide), ALU.add).then_inc(sums_ready, 1)

            for lv in range(1, 4):
                sums(lv)

            pool.wait_ge(rows_in, 48)
            pool.wait_ge(qk_rstd, 1)
            rotate(pool, link, 0, [xn[:, 0, i * 320:(i + 1) * 320] for i in range(3)] + [xn[:, 1, 0:320]])
            for lv in range(4, LEVELS - 1):
                sums(lv)
            wait_drained(pool, "W6")
            for t in range(T):
                g4 = hgate[:, t, :].rearrange("p (h d) -> p h d", h=HG)
                pool.tensor_tensor(g4, g4, hgw[:, :].unsqueeze(1).broadcast_to([P, HG, HGD]), ALU.mult)\
                    .then_inc(hgate_ready, 1)

            wait_full(pool, "lv8")
            pool.dma_start(gate1, A["ada_b"][0, 2 * D:3 * D].partition_broadcast(P)).then_inc(bias1_in, 16)

            wait_full(pool, "og")
            pool.dma_start(gate2, A["ada_b"][0, 5 * D:6 * D].partition_broadcast(P)).then_inc(bias1_in, 16)

            wait_full(pool, "yh1")
            pool.dma_start(bias[:, :, :], hankel(A["b_rel_bias_2"])).then_inc(bias_in, 16)
            pool.wait_ge(bias_in, 16)
            pool.memset(bias[0:64, :, 0:64], NEG).then_inc(bias_masked, 1)
            pool.wait_ge(x_ready, X_MIX)
            pool.dma_start(blockdiag, A["blockdiag"]).then_inc(bd_in, 16)
            wait_full(pool, "adr11")
            pool.dma_start(lng, A["a_ln_g_2"][0].partition_broadcast(P)).then_inc(ln_in, 16)
            low_parts(("nT1a", "nT1b"))
            pool.wait_ge(low_out, 8)
            pool.dma_start(ws, A["a_w_s_2"][0].rearrange("g i j -> i g j")).then_inc(ws_in, 16)
            pool.wait_ge(rows_high, 1)
            pool.tensor_tensor(xn_parts[1], xn[:, :, :].rearrange("p t d -> p (t d)"), xn_parts[0].bitcast(F32),
                               ALU.subtract).then_inc(rows_low, 1)
            wait_drained(pool, "wsT")
            pool.memset(wsT[64:128, :, 0:64], 0.0).then_inc(wsT_ready, 1)
            pool.wait_ge(x_ready, X_EXP)
            pool.dma_start(lnb, A["a_ln_b_2"][0].partition_broadcast(P)).then_inc(ln_in, 16)
            for n, row in enumerate((A["norm_g_2"][0, 1], A["norm_g_2"][0, 3],
                                     A["norm_g_2"][1, 1], A["norm_g_2"][1, 3])):
                if n in (1, 3):
                    pool.wait_ge(grow_free, n if n == 1 else 2)
                if n == 2:
                    wait_full(pool, "bs5")
                pool.dma_start(grows[n], row.partition_broadcast(P)).then_inc(grow_in[n % 2], 16)

        @block.scalar
        def _(act):
            act.dma_start(consts[:, :], A["consts"]).then_inc(consts_in, 16)
            for v, src in VECTORS[4:8]:
                act.dma_start(vrow[v:v + src.shape[0], :], src).then_inc(vrow_in, 16)
            act.dma_start(x[:, :, :], A["x"][0].rearrange("(t p) d -> p t d", p=P)).then_inc(x_in, 16)

            nexts = [0]

            def split_to(last):
                while nexts[0] <= last:
                    c = nexts[0]
                    nexts[0] += 1
                    wait_slab(act, CHUNKS[c][0])
                    if c >= NC and c != C_A:
                        wait_used(act, c - NC)
                    act.activation(part_of(c, 0), raw(c), ACT.Copy).then_inc(chunk_high, 1)

            def squares(n, t, counts=None):
                for half in range(2):
                    if counts:
                        act.wait_ge(x_ready, counts[half])
                    i = 4 * n + 2 * t + half
                    if i:
                        act.wait_ge(norm_ssq, i)
                    act.activation(junk[:, NB:D], x[:, t, half * NB:(half + 1) * NB], ACT.Square,
                                   accum_out=ssq[:, n, t, half:half + 1]).then_inc(norm_ssq, 1)

            def root(n, t):
                act.wait_ge(norm_var, 2 * n + t + 1)
                act.activation(std[:, n, t:t + 1], ssq[:, n, t, 0:1], ACT.Sqrt).then_inc(norm_std, 1)
                act.wait_ge(norm_rstd, 2 * n + t + 1)
                act.activation(xn[:, t, NB:D], x[:, t, NB:D], ACT.Copy, scale=rstd[:, n, t:t + 1])\
                    .then_inc(xn_ready[1], 1)

            def norm(n, t, counts=None):
                squares(n, t, counts)
                root(n, t)

            def by_tile(before, t):
                return [before + 2 * t + 1, before + 2 * t + 2]

            def turn_out(jobs, scale=None, shift=None):
                for half, job in enumerate(jobs):
                    wait_full(act, job)
                    for b in range(2):
                        k0 = 4 * half + 2 * b
                        if scale is None:
                            ins = act.activation(hT[0][:, k0:k0 + 2, :].rearrange("p k s -> p (k s)"), bank(job, b), ACT.Copy)
                        for kk in range(2 if scale is not None else 0):
                            k = k0 + kk
                            ins = act.activation(hT[0][:, k, :], bank(job, b)[:, kk * S:(kk + 1) * S], ACT.Identity,
                                                 scale=scale[:, k:k + 1], bias=shift[:, k:k + 1] if shift is not None else 0.0)
                        ins.then_inc(high_out, 1)

            def copy_out(job, dst, b):
                wait_full(act, job)
                act.activation(dst, bank(job, b), ACT.Copy).then_inc(psum_drained[pair(job)], 1)

            wait_full(act, "vecT")
            act.wait_ge(lb_in, 1)
            act.activation(small[:, 24:32], small[:, 16:24], ACT.Exp).then_inc(lb_exp, 1)
            act.activation(csil[:, :], vcol[:, V_C:V_C + 8], ACT.Silu).then_inc(c_silu, 1)
            act.wait_ge(x_in, 16)
            for t in range(T):
                squares(0, t)
            for t in range(T):
                root(0, t)
            split_to(0)
            act.wait_ge(aff_ready, 1)
            turn_out(("nT0a", "nT0b"), aff1, modc)
            split_to(3)

            for job, f, k in (("W1", PF, gkf), ("W2", PB, gkb)):
                wait_full(act, job)
                for b in range(2):
                    src = bank(job, b).rearrange("p (h s) -> p h s", h=2)
                    act.activation(k[:, 2 * b:2 * b + 2, :], src, ACT.Sigmoid, scale=-1.0)
                    act.activation(f[:, 2 * b:2 * b + 2, :], src, ACT.Sigmoid).then_inc(psum_drained[pair(job)], 1)
                split_to(CHUNK_OF["W2" if job == "W1" else "W0"] + 3)
            for d, f in enumerate((PF, PB)):
                act.wait_ge(log_in, d + 1)
                act.activation(f, f, ACT.Ln).then_inc(log_ready, 1)
            wait_full(act, "W0")
            for b in range(2):
                act.activation(gq[:, 2 * b:2 * b + 2, :], bank("W0", b).rearrange("p (h s) -> p h s", h=2), ACT.Silu)\
                    .then_inc(psum_drained[pair("W0")], 1)

            def levels(lv):
                s = 1 << (lv - 1)
                act.wait_ge(log_ready if lv == 1 else sums_ready, 2 if lv == 1 else lv - 1)
                if lv == 1:
                    act.wait_ge(filled, 4)
                wait_full(act, f"lv{lv - 1}")
                for dst, left, right in ((EQ, PB, PF), (EK, XF, XB)):
                    act.activation(split(dst, s)[0], split(left, s)[0], ACT.Exp)
                    ins = act.activation(split(dst, s)[1], split(right, s)[1], ACT.Exp)
                ins.then_inc(exp_ready, 1)

            split_to(CHUNK_OF["W4"] + 3)
            levels(1)
            wait_full(act, "W4")
            for t in range(T):
                dst = qk[:, t, 0:512].rearrange("p (i g d) -> p g i d", i=4, g=2)
                act.activation(dst, bank("W4", t).rearrange("p (g i d) -> p g i d", g=2, i=4), ACT.Copy)\
                    .then_inc(psum_drained[pair("W4")], 1)
            split_to(CHUNK_OF["W5"] + 3)
            levels(2)
            wait_full(act, "W5")
            for t in range(T):
                act.activation(qk[:, t, 512:640], bank("W5", t)[:, 0:128], ACT.Copy)
                act.activation(va[:, t, :], bank("W5", t)[:, 128:256], ACT.Copy).then_inc(psum_drained[pair("W5")], 1)
            act.wait_ge(qk_var, 2)
            act.activation(small[:, 80:100], small[:, 60:80], ACT.Sqrt).then_inc(qk_std, 1)
            levels(3)
            split_to(CHUNK_OF["W3"] + 3)
            for t in range(T):
                copy_out("W3", gv[:, t, :], t)
            levels(4)
            copy_out("qT", aqT[:, 2:4, :].rearrange("p i s -> p (i s)"), 1)

            def softmax(n, job, units, width, scale, dst):
                act.wait_ge(row_max, n + 1)
                src = banks(job).rearrange("p b n -> p (b n)").rearrange("p (u w) -> p u w", u=units)
                for u in range(units):
                    ins = act.activation(dst[:, u, :], src[:, u, :], ACT.Exp, scale=scale,
                                         bias=small[:, 100 + 8 * (n % 2) + u:101 + 8 * (n % 2) + u],
                                         accum_out=small[:, 120 + 8 * (n % 2) + u:121 + 8 * (n % 2) + u])
                    if u == units // 2 - 1 or u == units - 1:
                        ins.then_inc(psum_drained[pair(job)], 1)

            def half_of_turned(job):
                copy_out(job, tmp[:, NB:D], 1)

            softmax(0, "sc00", 4, S, 0.125, prob[0])
            softmax(1, "sc01", 4, S, 0.125, prob[1])
            levels(5)
            split_to(CHUNK_OF["W6"] + 1)
            wait_full(act, "W6")
            for t in range(T):
                act.activation(hgate[:, t, :], bank("W6", t), ACT.Silu).then_inc(psum_drained[pair("W6")], 1)
            half_of_turned("PT00")
            wait_full(act, "pv00")
            half_of_turned("PT01")
            levels(6)
            softmax(2, "sc10", 4, S, 0.125, prob[0])
            softmax(3, "sc11", 4, S, 0.125, prob[1])
            levels(7)
            half_of_turned("PT10")
            wait_full(act, "pv10")
            half_of_turned("PT11")
            split_to(CHUNK_OF["W7"] + 1)
            levels(8)
            split_to(CHUNK_OF["W8"])
            copy_out("lv8", AT[:, 1, 0].rearrange("p h s -> p (h s)"), 1)
            split_to(CHUNK_OF["W8"] + 1)

            def branch_gate(job, b, n):
                wait_full(act, job)
                for t in range(T):
                    act.activation(gsig[:, b, t, n * NB:(n + 1) * NB], bank(job, t), ACT.Sigmoid)\
                        .then_inc(psum_drained[pair(job)], 1)

            branch_gate("W7", 0, 0)
            for g in ("pv00", "pv01", "pv10", "pv11"):
                wait_drained(act, g)
            act.activation(oattR[0].rearrange("p i s -> p (i s)"), oattT, ACT.Copy).then_inc(oatt_high, 1)
            wait_full(act, "og")
            for t in range(T):
                for h in range(HG):
                    i = HG * t + h
                    ins = act.activation(junk[:, i * HGD:(i + 1) * HGD], bank("og", t)[:, h * HGD:(h + 1) * HGD], ACT.Square,
                                         accum_out=small[:, 140 + 4 * t + h:141 + 4 * t + h])
            ins.then_inc(o_ssq, 1)
            act.wait_ge(o_var, 1)
            act.activation(small[:, 150:158], small[:, 140:148], ACT.Sqrt).then_inc(o_std, 1)
            split_to(CHUNK_OF["W9"] + 1)
            branch_gate("W8", 0, 1)
            split_to(CHUNK_OF["W10"])
            wait_full(act, "ohgT")
            for i in range(2):
                act.activation(ohgR[0][:, 2 * i:2 * i + 2, :].rearrange("p i s -> p (i s)"), bank("ohgT", i),
                               ACT.Copy).then_inc(high_out, 1)
            split_to(CHUNK_OF["W10"] + 1)
            branch_gate("W9", 1, 0)
            split_to(CHUNK_OF["ya1"])
            branch_gate("W10", 1, 1)
            split_to(CHUNK_OF["mo0"] + 1)
            turn_out(("mTa", "mTb"))
            split_to(C_A - 1)

            for t in range(T):
                norm(1, t, [t + 1, t + 3])
            act.wait_ge(aff_ready, 2)
            turn_out(("nT1a", "nT1b"), aff2, modc[:, 24:32])
            act.wait_ge(r_max, 1)
            for t in range(T):
                ins = act.activation(eprob[:, t, :], bank("rl", 0)[:, t * NE:(t + 1) * NE], ACT.Exp,
                                     bias=small[:, 160 + t:161 + t], accum_out=small[:, 162 + t:163 + t])
            ins.then_inc(r_exp, 1)
            act.activation(xn_parts[0], xn[:, :, :].rearrange("p t d -> p (t d)"), ACT.Copy).then_inc(rows_high, 1)
            for q in range(4):
                job = f"ga{q}"
                wait_full(act, job)
                k = 2 * q + 1
                act.activation(xeT[:, k, :], bank(job, 1), ACT.Identity, scale=aff2[:, k:k + 1],
                               bias=modc[:, 24 + k:25 + k]).then_inc(psum_drained[pair(job)], 1)

            for b in range(2):
                copy_out("wsT", wsT[:, 4 * b:4 * b + 4, :].rearrange("p g i -> p (g i)"), b)

            with act.Fori(0, NE) as e:
                act.wait_ge(slab_done, e * PER_EXPERT + 4)
                act.activation(sg, PS[:, 0, :], ACT.Silu).then_inc(silu_ready, 1)
                act.wait_ge(hid_turned, e + 1)
                act.activation(hidT.rearrange("p i m -> p (i m)"), PS[:, 0, :], ACT.Copy).then_inc(hidT_ready, 1)
                act.wait_ge(slab_done, e * PER_EXPERT + 12)
                act.activation(ye[:, 0, :], PS[:, 2, :], ACT.Copy).then_inc(ye_ready, 1)

            split_to(C_A + 1)
            for t in range(T):
                squares(2, t, by_tile(X_MIX, t))
            for t in range(T):
                root(2, t)
            turn_out(("nT2a", "nT2b"), vcol[:, V_GA0:V_GA0 + 8])
            for job, dst, n in (("v0", V, 0), ("v1", V, 1), ("u0", U, 0), ("u1", U, 1)):
                split_to(CHUNK_OF[job] + 3)
                wait_full(act, job)
                for t in range(T):
                    act.activation(dst[:, t, n * NB:(n + 1) * NB], bank(job, t), ACT.Gelu_apprx_tanh)\
                        .then_inc(psum_drained[pair(job)], 1)
                if job == "v1":
                    act.wait_ge(ln_var, 1)
                    act.activation(small[:, 176:178], small[:, 172:174], ACT.Sqrt).then_inc(ln_std, 1)
            turn_out(("pTa", "pTb"))

            def post_norm(n, t, bank_of, halves=(0, 1)):
                for half in halves:
                    i = 4 * n + (2 * half + t if len(halves) == 1 else 2 * t + half)
                    if i:
                        act.wait_ge(post_ssq, i)
                    act.activation(junk[:, 0:NB], bank_of(half, t), ACT.Square,
                                   accum_out=small[:, 180 + 2 * t + half:181 + 2 * t + half]).then_inc(post_ssq, 1)
                if 1 in halves:
                    act.wait_ge(post_var, 2 * n + t + 1)
                    act.activation(small[:, 188 + t:189 + t], small[:, 186 + t:187 + t], ACT.Sqrt).then_inc(post_std, 1)

            def after_product(n, name, before):
                def bank_of(half, t):
                    return bank(f"{name}{half}", t)

                wait_full(act, f"{name}0")
                for t in range(T):
                    post_norm(n, t, bank_of, (0,))
                for t in range(T):
                    if t == 0:
                        act.wait_ge(tile_full, n + 2)
                    else:
                        wait_full(act, f"{name}1")
                    post_norm(n, t, bank_of, (1,))
                    norm(n + 3, t, by_tile(before, t))

            def after_mlp(n, layer, before=None):
                for t in range(T):
                    if t == 0:
                        act.wait_ge(tile_full, n + 2)
                    else:
                        act.wait_ge(slab_done, done_count(AT_FFN[layer] + 2 * FJ - 1))
                    post_norm(n, t, lambda h, t: PS[:, 2 * t + h, :])
                    if before is not None:
                        norm(n + 3, t, by_tile(before, t))

            def mlp(layer):
                base = done_count(AT_FFN[layer]) - 1
                done = layer * FJ
                c0, at0 = C_FFN[layer], AT_FFN[layer]
                half0 = HALF_COUNT[c0] - 1

                def high(i, turns=None):
                    c = c0 + i
                    add = (lambda k: 0) if turns is None else (lambda k: turns * k)
                    act.wait_ge(slab_in[slot_of(at0 + i // 2)], add(32) + ARRIVED[at0 + i // 2])
                    if i >= NC and i % 2:
                        act.wait_ge(half_done, add(6) + (half0 + (i - NC) // 2 + 1))
                    elif i >= NC:
                        act.wait_ge(slab_done, add(6) + (base + (i - NC) // 2 + 1))
                    else:
                        wait_used(act, c - NC)
                    act.activation(part_of(c, 0), raw(c), ACT.Copy).then_inc(chunk_high, 1)

                def relu(j, up):
                    act.wait_ge(slab_done, up)
                    act.activation(rl, PS[:, 4:6, :].rearrange("p b n -> p (b n)"), ACT.Relu).then_inc(relu_ready, 1)

                def square_high(j, b):
                    act.wait_ge(sqr_ready, j + (done + 1))
                    act.activation(hidden[0][:, b].rearrange("p i s -> p (i s)"), sqr, ACT.Copy).then_inc(sqr_high, 1)

                high(2)
                high(3)
                relu(0, base + 1)
                square_high(0, 0)
                high(4)
                high(5)
                with act.Fori(0, 2) as it:
                    for jj in range(1, 4):
                        relu(it * 3 + jj, it * 6 + (base + 2 * jj))
                        square_high(it * 3 + jj, jj % 3)
                        for i in range(4 * jj + 2, 4 * jj + 6):
                            high(i, it)
                relu(7, base + 14)
                square_high(7, 1)
                high(30)
                high(31)
                nexts[0] = c0 + 32

            split_to(CHUNK_OF["am0"] + 3)
            split_to(C_FFN[0])
            after_product(0, "am", X_EXP)
            turn_out(("nT3a", "nT3b"), vcol[:, V_GA2:V_GA2 + 8])
            split_to(C_FFN[0] + 1)
            mlp(0)
            split_to(C_B)
            after_mlp(1, 0, X_GM)
            quarters = [(job, half, b) for half, job in enumerate(("nT4a", "nT4b")) for b in range(2)]
            for job, half, b in quarters:
                wait_full(act, job)
                for kk in range(2):
                    k = 4 * half + 2 * b + kk
                    ins = act.activation(hR[0][:, k, ::-1], bank(job, b)[:, kk * S:(kk + 1) * S], ACT.Identity,
                                         scale=vcol[:, V_KV + k:V_KV + k + 1])
                ins.then_inc(high_out, 1)
            for i, (job, half, b) in enumerate(quarters):
                act.wait_ge(kv_low, i + 1)
                for kk in range(2):
                    k = 4 * half + 2 * b + kk
                    ins = act.activation(hT[0][:, k, :], bank(job, b)[:, kk * S:(kk + 1) * S], ACT.Identity,
                                         scale=vcol[:, V_GB0 + k:V_GB0 + k + 1])
                ins.then_inc(q_high, 1)
            for job, dst in (("bk0", bkT[:, 2:4]), ("bk1", bkT[:, 6:8]), ("bq0", bqT[:, 2:4]), ("bq1", bqT[:, 6:8])):
                split_to(CHUNK_OF[job] + 3)
                copy_out(job, dst.rearrange("p k s -> p (k s)"), 1)
            for n in range(2):
                split_to(CHUNK_OF[f"bv{n}"] + 3)
                copy_out(f"bv{n}", vR[:, 1, n * NB:(n + 1) * NB], 1)

            def b_softmax(n):
                units = 8 if n < 2 else 4
                pr = bp[n % 4].rearrange("p (u w) -> p u w", u=units)
                act.wait_ge(row_max, 5 + n)
                for u in range(units):
                    ins = act.activation(pr[:, u, :], pr[:, u, :], ACT.Exp,
                                         bias=small[:, 100 + 8 * (n % 2) + u:101 + 8 * (n % 2) + u],
                                         accum_out=small[:, 120 + 8 * (n % 2) + u:121 + 8 * (n % 2) + u])
                ins.then_inc(row_exp, 1)

            def b_turned(n):
                copy_out(f"bT{n}", bpt[n % 2][:, NB:D], 1)

            b_softmax(0)
            b_softmax(1)
            for n in range(6):
                b_turned(n)
                if n < 4:
                    b_softmax(n + 2)
            split_to(C_FFN[1])
            after_product(2, "bm", X_F0)
            turn_out(("nT5a", "nT5b"), vcol[:, V_GB2:V_GB2 + 8])
            split_to(C_FFN[1] + 1)
            mlp(1)
            after_mlp(3, 1)

        @block.vector
        def _(dve):
            steps = [0]

            def link(ins):
                steps[0] += 1
                ins.then_inc(dve_step, 1)
                dve.wait_ge(dve_step, steps[0])

            nexts = [0]

            def split_to(last):
                while nexts[0] <= last:
                    c = nexts[0]
                    nexts[0] += 1
                    dve.wait_ge(chunk_high, c + 1)
                    dve.tensor_tensor(part_of(c, 1), raw(c), part_of(c, 0).bitcast(F32), ALU.subtract)\
                        .then_inc(chunk_low, 1)

            def mean_square(n, t):
                dve.wait_ge(norm_ssq, 4 * n + 2 * t + 2)
                s0 = ssq[:, n, t, 0:1]
                link(dve.tensor_tensor(s0, s0, ssq[:, n, t, 1:2], ALU.add))
                dve.tensor_scalar(s0, s0, 1.0 / D, EPS, ALU.mult, ALU.add).then_inc(norm_var, 1)

            def rescale(n, t):
                dve.wait_ge(norm_std, 2 * n + t + 1)
                dve.reciprocal(rstd[:, n, t:t + 1], std[:, n, t:t + 1]).then_inc(norm_rstd, 1)
                dve.wait_ge(norm_rstd, 2 * n + t + 1)
                dve.tensor_scalar(xn[:, t, 0:NB], x[:, t, 0:NB], rstd[:, n, t:t + 1], None, ALU.mult)\
                    .then_inc(xn_ready[0], 1)

            def norm(n, t):
                mean_square(n, t)
                rescale(n, t)

            def turn_out(jobs, scale=None, shift=None, dst=hT):
                for half, job in enumerate(jobs):
                    for b in range(2):
                        dve.wait_ge(high_out, high_count(job, b))
                        k0 = 4 * half + 2 * b
                        high = dst[0][:, k0:k0 + 2, :].rearrange("p k s -> p (k s)").bitcast(F32)
                        low = dst[1][:, k0:k0 + 2, :].rearrange("p k s -> p (k s)")
                        if scale is None:
                            ins = dve.tensor_tensor(low, bank(job, b), high, ALU.subtract)
                        elif shift is None:
                            for kk in range(2):
                                c = slice(kk * S, (kk + 1) * S)
                                ins = dve.scalar_tensor_tensor(out=low[:, c], in0=bank(job, b)[:, c],
                                                               scalar=scale[:, k0 + kk:k0 + kk + 1], in1=high[:, c],
                                                               op0=ALU.mult, op1=ALU.subtract)
                        else:
                            if half:
                                dve.wait_ge(low_out, (0 if job == "nT0b" else 4) + b + 1)
                            for kk in range(2):
                                c = slice(kk * S, (kk + 1) * S)
                                ins = dve.tensor_scalar(tmp[:, b * NB + kk * S:b * NB + (kk + 1) * S], bank(job, b)[:, c],
                                                        scale[:, k0 + kk:k0 + kk + 1], shift[:, k0 + kk:k0 + kk + 1],
                                                        ALU.mult, ALU.add)
                        ins.then_inc(psum_drained[pair(job)], 1)

            def copy_out(job, dst, b):
                wait_full(dve, job)
                dve.tensor_copy(dst, bank(job, b)).then_inc(psum_drained[pair(job)], 1)

            def ada_part(s):
                copy_out(f"ada{s}", part2 if 6 <= s < 10 else part[:, s % 2, :], 0)

            def ada_col(s):
                job = f"adc{s}"
                wait_full(dve, job)
                dve.tensor_tensor(modc[:, 4 * s:4 * s + 4], bank(job, 0)[:, 0:4], vcol[:, V_AB + 4 * s:V_AB + 4 * s + 4],
                                  ALU.add).then_inc(psum_drained[pair(job)], 1)

            def ada_row(s, dst):
                job = f"adr{s}"
                wait_full(dve, job)
                dve.tensor_tensor(dst, dst, bank(job, 0), ALU.add).then_inc(psum_drained[pair(job)], 1)

            wait_full(dve, "vecT")
            link(dve.tensor_copy(vcol[:, :], bank("vecT", 0)[:, 0:P]))
            dve.tensor_tensor(small[:, 16:24], vcol[:, V_LB:V_LB + 8], vcol[:, V_LB:V_LB + 8], ALU.subtract)\
                .then_inc(lb_in, 1)
            dve.sem_inc(psum_drained[pair("vecT")], 1)
            dve.wait_ge(c_silu, 1)
            for k in range(KD):
                ins = dve.tensor_copy(crep[:, k, :], csil[:, k:k + 1].broadcast_to([P, 32]))
            ins.then_inc(crep_ready, 1)
            dve.wait_ge(lb_exp, 1)
            link(dve.reciprocal(small[:, 32:40], small[:, 24:32]))
            link(dve.tensor_tensor(small[:, 32:40], small[:, 24:32], small[:, 32:40], ALU.mult))
            link(dve.tensor_tensor(small[:, 0:8], small[:, 32:40], small[:, 32:40], ALU.subtract))
            dve.tensor_scalar(small[:, 8:16], small[:, 0:8], -1.0, 1.0, ALU.mult, ALU.add).then_inc(lb_ready, 1)
            for t in range(T):
                mean_square(0, t)
            for t in range(T):
                rescale(0, t)
            ada_part(0)
            ada_part(1)
            ada_col(0)
            ada_part(2)
            ada_col(1)
            ada_part(3)
            ada_col(2)
            ada_col(3)
            wait_drained(dve, "adc3")
            wait_drained(dve, "adc2")
            dve.scalar_tensor_tensor(out=aff1[:, :], in0=modc[:, 8:16], scalar=1.0, in1=vcol[:, V_NM:V_NM + 8],
                                     op0=ALU.add, op1=ALU.mult).then_inc(aff_ready, 1)
            dve.wait_ge(aff_ready, 1)
            split_to(0)
            turn_out(("nT0a", "nT0b"), aff1, modc)
            split_to(3)

            def factors(lv):
                s = 1 << (lv - 1)
                dve.wait_ge(exp_ready, lv)
                if lv == 1:
                    dve.wait_ge(k_ready, 8)
                for src, dst, side in ((gkf, EK, 0), (gkb, EK, 1)):
                    dve.tensor_tensor(split(dst, s)[side], split(dst, s)[side], split(src, s)[side], ALU.mult)
                dve.tensor_tensor(EQ, EQ, gq, ALU.mult).then_inc(factors_ready, 1)

            def scores(lv):
                job = f"lv{lv}"
                wait_full(dve, job)
                for t in range(T):
                    src = bank(job, t).rearrange("p (h s) -> p h s", h=HG)
                    if lv == 0:
                        dve.tensor_copy(AT[:, t, t], src).then_inc(psum_drained[pair(job)], 1)
                    else:
                        m = masks[:, (lv - 1) * P:lv * P].unsqueeze(1).broadcast_to([P, HG, P])
                        dve.copy_predicated(AT[:, t, t], m, src).then_inc(psum_drained[pair(job)], 1)
                wait_drained(dve, job)

            for d, (job, f) in enumerate((("W1", PF), ("W2", PB))):
                dve.wait_ge(forget_ready, 4 * d + 4)
                dve.tensor_scalar(f, f, MIN_F, None, ALU.max).then_inc(log_in, 1)
                split_to(CHUNK_OF["W2" if job == "W1" else "W0"] + 3)
            dve.wait_ge(k_ready, 8)
            dve.tensor_tensor(EK, gkf, gkb, ALU.add).then_inc(factors_ready, 1)
            scores(0)
            split_to(CHUNK_OF["W4"] + 3)
            factors(1)
            scores(1)
            split_to(CHUNK_OF["W5"] + 3)
            factors(2)

            wait_drained(dve, "W4")
            wait_drained(dve, "W5")
            for t in range(T):
                sq = tmp[:, 0:640]
                link(dve.tensor_tensor(sq, qk[:, t, :], qk[:, t, :], ALU.mult))
                link(dve.tensor_reduce(small[:, 60 + 10 * t:70 + 10 * t], sq.rearrange("p (h d) -> p h d", h=10),
                                       AX, ALU.add))
                dve.tensor_scalar(small[:, 60 + 10 * t:70 + 10 * t], small[:, 60 + 10 * t:70 + 10 * t],
                                  1.0 / AHD, EPS, ALU.mult, ALU.add).then_inc(qk_var, 1)
            dve.wait_ge(qk_std, 1)
            link(dve.reciprocal(small[:, 40:60], small[:, 80:100]))
            for t in range(T):
                v = qk[:, t, :].rearrange("p (h d) -> p h d", h=10)
                dve.tensor_tensor(v, v, small[:, 40 + 10 * t:50 + 10 * t].unsqueeze(2).broadcast_to([P, 10, AHD]),
                                  ALU.mult).then_inc(qk_rstd, 1)
            dve.wait_ge(qk_rstd, 2)
            dve.wait_ge(rows_in, 48)
            rotate(dve, link, 1, [xn[:, 1, 320:640], xn[:, 1, 640:960], tmp[:, 0:320], tmp[:, 320:640]])
            scores(2)
            factors(3)
            split_to(CHUNK_OF["W3"] + 3)
            scores(3)
            factors(4)
            ada_part(6)
            ada_col(6)
            copy_out("qT", aqT[:, 0:2, :].rearrange("p i s -> p (i s)"), 0)
            wait_full(dve, "kT")
            dve.tensor_copy(akT, bank("kT", 0)[:, 0:S]).then_inc(psum_drained[pair("kT")], 1)

            def maxima(n, job):
                wait_full(dve, job)
                m = small[:, 100 + 8 * (n % 2):104 + 8 * (n % 2)]
                src = banks(job).rearrange("p b n -> p (b n)").rearrange("p (u w) -> p u w", u=4)
                link(dve.tensor_reduce(m, src, AX, ALU.max))
                dve.tensor_scalar(m, m, -0.125, None, ALU.mult).then_inc(row_max, 1)

            def normalise(n, pr, units):
                rs = small[:, 120 + 8 * (n % 2):120 + 8 * (n % 2) + units]
                link(dve.reciprocal(rs, rs))
                shape = [P, units, D // units]
                dve.tensor_tensor(pr, pr, rs.unsqueeze(2).broadcast_to(shape), ALU.mult).then_inc(prob_ready, 1)

            def attended(job, t, g):
                wait_full(dve, job)
                dst = oattT.rearrange("p (i s) -> p i s", i=4)[64 * g:64 * g + 64, :, t * P:(t + 1) * P]
                src = PS[64 * g:64 * g + 64, 2 * pair(job), :].rearrange("p (i s) -> p i s", i=4)
                dve.tensor_copy(dst, src).then_inc(psum_drained[pair(job)], 1)

            maxima(0, "sc00")
            maxima(1, "sc01")
            wait_drained(dve, "sc00")
            normalise(0, prob[0], 4)
            wait_drained(dve, "sc01")
            normalise(1, prob[1], 4)
            scores(4)
            factors(5)
            split_to(CHUNK_OF["W6"] + 1)
            copy_out("PT00", tmp[:, 0:NB], 0)
            attended("pv00", 0, 0)
            copy_out("PT01", tmp[:, 0:NB], 0)
            attended("pv01", 0, 1)
            scores(5)
            factors(6)
            maxima(2, "sc10")
            maxima(3, "sc11")
            wait_drained(dve, "sc10")
            normalise(2, prob[0], 4)
            wait_drained(dve, "sc11")
            normalise(3, prob[1], 4)
            ada_part(7)
            scores(6)
            ada_col(7)
            copy_out("PT10", tmp[:, 0:NB], 0)
            factors(7)
            ada_part(8)
            attended("pv10", 1, 0)
            copy_out("PT11", tmp[:, 0:NB], 0)
            ada_col(8)
            attended("pv11", 1, 1)
            split_to(CHUNK_OF["W7"] + 1)
            scores(7)
            ada_part(9)
            factors(8)
            split_to(CHUNK_OF["W8"])
            copy_out("lv8", AT[:, 0, 1].rearrange("p h s -> p (h s)"), 0)
            ada_col(9)
            split_to(CHUNK_OF["W8"] + 1)
            ada_part(4)
            dve.wait_ge(o_ssq, 1)
            dve.tensor_scalar(small[:, 140:148], small[:, 140:148], 1.0 / HGD, EPS, ALU.mult, ALU.add).then_inc(o_var, 1)
            dve.wait_ge(o_std, 1)
            link(dve.reciprocal(small[:, 150:158], small[:, 150:158]))
            for t in range(T):
                o4 = ohg[:, t, :].rearrange("p (h d) -> p h d", h=HG)
                dve.tensor_tensor(o4, bank("og", t).rearrange("p (h d) -> p h d", h=HG),
                                  small[:, 150 + 4 * t:154 + 4 * t].unsqueeze(2).broadcast_to([P, HG, HGD]),
                                  ALU.mult).then_inc(psum_drained[pair("og")], 1)
            wait_drained(dve, "og")
            dve.wait_ge(hgate_ready, 2)
            for t in range(T):
                dve.tensor_tensor(ohg[:, t, :], ohg[:, t, :], hgate[:, t, :], ALU.mult).then_inc(ohg_ready, 1)
            ada_part(5)
            split_to(CHUNK_OF["W9"])
            dve.wait_ge(oatt_high, 1)
            dve.tensor_tensor(oattR[1].rearrange("p i s -> p (i s)"), oattT,
                              oattR[0].rearrange("p i s -> p (i s)").bitcast(F32), ALU.subtract).then_inc(oatt_low, 1)
            split_to(CHUNK_OF["W9"] + 1)
            dve.wait_ge(bias1_in, 32)
            ada_row(4, gate1[:, 0:NB])
            ada_row(5, gate1[:, NB:D])
            split_to(CHUNK_OF["W10"])
            for i in range(2):
                dve.wait_ge(high_out, high_count("ohgT", i))
                dve.tensor_tensor(ohgR[1][:, 2 * i:2 * i + 2, :].rearrange("p i s -> p (i s)"), bank("ohgT", i),
                                  ohgR[0][:, 2 * i:2 * i + 2, :].rearrange("p i s -> p (i s)").bitcast(F32),
                                  ALU.subtract).then_inc(psum_drained[pair("ohgT")], 1)
            split_to(CHUNK_OF["yh0"])
            for job in ("W7", "W8"):
                wait_drained(dve, job)
            for n in range(2):
                job = f"ya{n}"
                wait_full(dve, job)
                for t in range(T):
                    dve.tensor_tensor(merged[:, t, n * NB:(n + 1) * NB], bank(job, t),
                                      gsig[:, 0, t, n * NB:(n + 1) * NB], ALU.mult).then_inc(psum_drained[pair(job)], 1)
                split_to(CHUNK_OF["yh1"] + n)
            for job in ("W9", "W10"):
                wait_drained(dve, job)
            for n in range(2):
                job = f"yh{n}"
                wait_full(dve, job)
                for t in range(T):
                    g = gsig[:, 1, t, n * NB:(n + 1) * NB]
                    dve.tensor_tensor(g, bank(job, t), g, ALU.mult).then_inc(psum_drained[pair(job)], 1)
                wait_drained(dve, job)
                wait_drained(dve, f"ya{n}")
                for t in range(T):
                    m = merged[:, t, n * NB:(n + 1) * NB]
                    dve.tensor_tensor(m, m, gsig[:, 1, t, n * NB:(n + 1) * NB], ALU.add).then_inc(merged_ready, 1)
                if n == 0:
                    split_to(CHUNK_OF["mo0"] + 1)
            ada_part(10)
            wait_drained(dve, "adc9")
            wait_drained(dve, "adc8")
            dve.scalar_tensor_tensor(out=aff2[:, :], in0=modc[:, 32:40], scalar=1.0, in1=vcol[:, V_NF:V_NF + 8],
                                     op0=ALU.add, op1=ALU.mult).then_inc(aff_ready, 1)
            turn_out(("mTa", "mTb"))
            split_to(C_A - 1)
            wait_drained(dve, "adr5")
            wait_drained(dve, "adr4")
            wait_full(dve, "mo0")
            for t in range(T):
                dve.tensor_tensor(tmp[:, t * NB:(t + 1) * NB], bank("mo0", t), gate1[:, 0:NB],
                                  ALU.mult).then_inc(psum_drained[pair("mo0")], 1)
            wait_drained(dve, "mo0")
            for t in range(T):
                dve.tensor_tensor(x[:, t, 0:NB], x[:, t, 0:NB], tmp[:, t * NB:(t + 1) * NB], ALU.add)\
                    .then_inc(x_ready, 1)
            ada_row(10, gate2[:, 0:NB])
            ada_part(11)
            dve.wait_ge(x_ready, 2)
            for t in range(T):
                if t == 0:
                    dve.wait_ge(tile_full, 1)
                else:
                    wait_full(dve, "mo1")
                c = slice(t * NB, (t + 1) * NB)
                dve.tensor_tensor(tmp[:, c], bank("mo1", t), gate1[:, NB:D], ALU.mult).then_inc(psum_drained[pair("mo1")], 1)
                dve.wait_ge(psum_drained[pair("mo1")], DRAINED[JOB_AT["mo1"]] - 1 + t)
                dve.tensor_tensor(x[:, t, NB:D], x[:, t, NB:D], tmp[:, c], ALU.add).then_inc(x_ready, 1)
                norm(1, t)
            ada_row(11, gate2[:, NB:D])
            dve.wait_ge(aff_ready, 2)
            turn_out(("nT1a", "nT1b"), aff2, modc[:, 24:32])

            wait_full(dve, "rt")
            dve.tensor_copy(logits, bank("rt", 0)[:, 0:S]).then_inc(psum_drained[pair("rt")], 1)
            wait_full(dve, "rl")
            link(dve.tensor_reduce(small[:, 160:162], bank("rl", 0)[:, 0:T * NE].rearrange("p (t e) -> p t e", t=T),
                                   AX, ALU.max))
            dve.tensor_scalar(small[:, 160:162], small[:, 160:162], -1.0, None, ALU.mult).then_inc(r_max, 1)
            dve.wait_ge(r_exp, 1)
            link(dve.reciprocal(small[:, 162:164], small[:, 162:164]))
            dve.tensor_tensor(eprob, eprob, small[:, 162:164].unsqueeze(2).broadcast_to([P, T, NE]), ALU.mult)\
                .then_inc(r_ready, 1)
            dve.sem_inc(psum_drained[pair("rl")], 1)
            wait_full(dve, "aT")
            link(dve.tensor_copy(etop[0:16, :], bank("aT", 0)[0:16, 0:S]))
            dve.sem_inc(psum_drained[pair("aT")], 1)
            cur, other = etop[0:16, :], etop2[0:16, :]
            topw = small[0:16, 208:240]
            for r8 in range(4):
                link(dve.max(topw[:, 8 * r8:8 * r8 + 8], cur))
                link(dve.max_index(eidx[0:16, 8 * r8:8 * r8 + 8].bitcast(U32), topw[:, 8 * r8:8 * r8 + 8], cur))
                if r8 < 3:
                    link(dve.match_replace(other, topw[:, 8 * r8:8 * r8 + 8], cur, -1.0))
                    cur, other = other, cur
            link(dve.tensor_copy(eidx[0:16, 32:64], eidx[0:16, 0:32].bitcast(U32)))
            dve.tensor_copy(erep[0:16, 0], eidx[0:16, 32:64].unsqueeze(1).broadcast_to([16, 4, CAP]))
            dve.tensor_copy(erep[0:16, 1], topw.unsqueeze(1).broadcast_to([16, 4, CAP]))
            dve.wait_ge(bd_in, 16)
            dve.tensor_tensor(ebd[0:16, :].rearrange("p (e c) -> p e c", e=NE), blockdiag.rearrange("p (e c) -> p e c", e=NE),
                              eidx[0:16, 32:64].unsqueeze(1).broadcast_to([16, NE, CAP]), ALU.mult).then_inc(top_ready, 1)
            wait_full(dve, "ic")
            dve.tensor_copy(ecol.rearrange("p a e -> p (a e)"), bank("ic", 0)[:, 0:32]).then_inc(psum_drained[pair("ic")], 1)
            wait_full(dve, "ib")
            for t in range(T):
                ins = dve.tensor_scalar(onehot[:, t, :], bank("ib", 0), consts[:, C_TOK + t:C_TOK + t + 1], None,
                                        ALU.is_equal)
            ins.then_inc(psum_drained[pair("ib")], 1)
            for q in range(4):
                job = f"ga{q}"
                wait_full(dve, job)
                k = 2 * q
                dve.tensor_scalar(xeT[:, k, :], bank(job, 0), aff2[:, k:k + 1], modc[:, 24 + k:25 + k],
                                  ALU.mult, ALU.add).then_inc(psum_drained[pair(job)], 1)
            for q in range(4):
                wait_drained(dve, f"ga{q}")


            with dve.Fori(0, NE) as e:
                dve.tensor_copy(xe, xeT[:, :, bass.ds(e * CAP, CAP)]).then_inc(xe_ready, 1)
                dve.wait_ge(slab_done, e * PER_EXPERT + 8)
                dve.wait_ge(silu_ready, e + 1)
                dve.tensor_tensor(hid, PS[:, 1, :], sg, ALU.mult).then_inc(hid_ready, 1)
                dve.tensor_scalar(comb, iota, ecol[:, 0, bass.ds(e, 1)], ecol[:, 1, bass.ds(e, 1)],
                                  ALU.is_equal, ALU.mult)
                dve.wait_ge(slab_done, e * PER_EXPERT + 12)
                dve.tensor_copy(ye[:, 1, :], PS[:, 3, :]).then_inc(ye_ready, 1)

            wait_drained(dve, "adr11")
            wait_drained(dve, "adr10")
            dve.wait_ge(comb_done, 1)
            for t in range(T):
                for half in range(2):
                    cols = slice(half * NB, (half + 1) * NB)
                    ins = dve.tensor_tensor(tmp[:, cols], PS[:, 4 + 2 * t + half, :], gate2[:, cols], ALU.mult)
                link(ins)
                for half in range(2):
                    cols = slice(half * NB, (half + 1) * NB)
                    dve.tensor_tensor(x[:, t, cols], x[:, t, cols], tmp[:, cols], ALU.add).then_inc(x_ready, 1)
                dve.wait_ge(x_ready, X_MIX + 2 * t + 2)
            for t in range(T):
                mean_square(2, t)
            for t in range(T):
                rescale(2, t)

            split_to(C_A)
            turn_out(("nT2a", "nT2b"), vcol[:, V_GA0:V_GA0 + 8])
            split_to(CHUNK_OF["v1"] + 3)
            stats = small[:, 204:228].rearrange("p (t n) -> p t n", t=T)
            for n in range(2):
                wait_drained(dve, f"v{n}")
                for t in range(T):
                    link(dve.bn_stats(stats[:, t, 6 * n:6 * n + 6], V[:, t, n * NB:(n + 1) * NB]))
            for t in range(T):
                link(dve.bn_aggr(small[:, 168 + 2 * t:170 + 2 * t], stats[:, t, :]))
            mv = small[:, 168:172].rearrange("p (t c) -> p t c", t=T)
            dve.tensor_scalar(small[:, 172:174], mv[:, :, 1], LN_EPS, None, ALU.add).then_inc(ln_var, 1)
            dve.wait_ge(ln_std, 1)
            link(dve.reciprocal(small[:, 174:176], small[:, 176:178]))
            for t in range(T):
                link(dve.tensor_scalar(V[:, t, :], V[:, t, :], mv[:, t, 0:1], small[:, 174 + t:175 + t],
                                       ALU.subtract, ALU.mult))
            split_to(CHUNK_OF["u1"])
            dve.wait_ge(ln_in, 32)
            for t in range(T):
                link(dve.tensor_tensor(V[:, t, :], V[:, t, :], lng, ALU.mult))
                dve.tensor_tensor(V[:, t, :], V[:, t, :], lnb, ALU.add).then_inc(ln_ready, 1)
                split_to(CHUNK_OF["u1"] + 1 + t)
            split_to(CHUNK_OF["u1"] + 3)
            for n in range(2):
                wait_drained(dve, f"u{n}")
            for t in range(T):
                job = f"sv{t}"
                wait_full(dve, job)
                for g in range(8):
                    u = U[:, t, g * P:(g + 1) * P]
                    ins = dve.scalar_tensor_tensor(out=u, in0=bank(job, g // 4)[:, (g % 4) * P:(g % 4 + 1) * P],
                                                   scalar=vcol[:, V_BS + g:V_BS + g + 1], in1=u,
                                                   op0=ALU.add, op1=ALU.mult)
                    if g % 4 == 3:
                        ins.then_inc(psum_drained[pair(job)], 1)
            turn_out(("pTa", "pTb"))

            def times_gain(n, half, t, src):
                cols = slice(half * NB, (half + 1) * NB)
                return dve.tensor_tensor(xn[:, t, cols], src, grows[n][:, cols], ALU.mult)

            def post_norm(n, t, counts, products):
                dve.wait_ge(post_ssq, counts)
                link(dve.tensor_reduce(small[:, 184 + t:185 + t], small[:, 180 + 2 * t:182 + 2 * t], AX, ALU.add))
                dve.tensor_scalar(small[:, 186 + t:187 + t], small[:, 184 + t:185 + t], 1.0 / D, EPS, ALU.mult, ALU.add)\
                    .then_inc(post_var, 1)
                products()
                dve.wait_ge(post_std, 2 * n + t + 1)
                link(dve.reciprocal(small[:, 190 + t:191 + t], small[:, 188 + t:189 + t]))
                if t == 1:
                    dve.sem_inc(grow_free, 1)
                for half in range(2):
                    cols = slice(half * NB, (half + 1) * NB)
                    dve.scalar_tensor_tensor(out=x[:, t, cols], in0=xn[:, t, cols],
                                             scalar=small[:, 190 + t:191 + t], in1=x[:, t, cols],
                                             op0=ALU.mult, op1=ALU.add).then_inc(x_ready, 1)

            def after_product(n, name):
                def product(half, t):
                    job = f"{name}{half}"
                    times_gain(n, half, t, bank(job, t)).then_inc(psum_drained[pair(job)], 1)

                dve.wait_ge(grow_in[n % 2], 16 * (n // 2 + 1))
                dve.wait_ge(post_ssq, 4 * n + 2)
                for t in range(T):
                    product(0, t)
                for t in range(T):
                    post_norm(n, t, 4 * n + 3 + t, lambda: product(1, t))
                    norm(n + 3, t)

            def after_mlp(n):
                dve.wait_ge(grow_in[n % 2], 16 * (n // 2 + 1))
                for t in range(T):
                    post_norm(n, t, 4 * n + 2 * t + 2,
                              lambda: [times_gain(n, half, t, PS[:, 2 * t + half, :]) for half in range(2)])
                    if n == 1:
                        norm(n + 3, t)

            def mlp(layer):
                done = layer * FJ
                c0 = C_FFN[layer]

                def low(i, turns=None):
                    c = c0 + i
                    dve.wait_ge(chunk_high, c + 1 if turns is None else turns * 12 + (c + 1))
                    dve.tensor_tensor(part_of(c, 1), raw(c), part_of(c, 0).bitcast(F32), ALU.subtract)\
                        .then_inc(chunk_low, 1)

                def square(j, b):
                    dve.wait_ge(relu_ready, j + (done + 1))
                    if not (isinstance(j, int) and j == 0):
                        dve.wait_ge(hidden_ready, j + done)
                    dve.tensor_tensor(sqr, rl, rl, ALU.mult).then_inc(sqr_ready, 1)
                    dve.wait_ge(sqr_high, j + (done + 1))
                    dve.tensor_tensor(hidden[1][:, b].rearrange("p i s -> p (i s)"), sqr,
                                      hidden[0][:, b].rearrange("p i s -> p (i s)").bitcast(F32), ALU.subtract)\
                        .then_inc(hidden_ready, 1)

                low(2)
                low(3)
                square(0, 0)
                low(4)
                low(5)
                with dve.Fori(0, 2) as it:
                    for jj in range(1, 4):
                        square(it * 3 + jj, jj % 3)
                        for i in range(4 * jj + 2, 4 * jj + 6):
                            low(i, it)
                square(7, 1)
                low(30)
                low(31)
                nexts[0] = c0 + 32

            split_to(C_FFN[0])
            after_product(0, "am")
            turn_out(("nT3a", "nT3b"), vcol[:, V_GA2:V_GA2 + 8])
            split_to(C_FFN[0] + 1)
            mlp(0)
            split_to(C_B)
            after_mlp(1)
            quarters = [(job, half, b) for half, job in enumerate(("nT4a", "nT4b")) for b in range(2)]
            for job, half, b in quarters:
                dve.wait_ge(high_out, high_count(job, b))
                for kk in range(2):
                    k = 4 * half + 2 * b + kk
                    ins = dve.scalar_tensor_tensor(out=hR[1][:, k, ::-1], in0=bank(job, b)[:, kk * S:(kk + 1) * S],
                                                   scalar=vcol[:, V_KV + k:V_KV + k + 1],
                                                   in1=hR[0][:, k, ::-1].bitcast(F32), op0=ALU.mult, op1=ALU.subtract)
                ins.then_inc(kv_low, 1)
            for i, (job, half, b) in enumerate(quarters):
                dve.wait_ge(q_high, i + 1)
                for kk in range(2):
                    k = 4 * half + 2 * b + kk
                    ins = dve.scalar_tensor_tensor(out=hT[1][:, k, :], in0=bank(job, b)[:, kk * S:(kk + 1) * S],
                                                   scalar=vcol[:, V_GB0 + k:V_GB0 + k + 1],
                                                   in1=hT[0][:, k, :].bitcast(F32), op0=ALU.mult, op1=ALU.subtract)
                ins.then_inc(psum_drained[pair(job)], 1)
            for job, dst in (("bk0", bkT[:, 0:2]), ("bk1", bkT[:, 4:6]), ("bq0", bqT[:, 0:2]), ("bq1", bqT[:, 4:6])):
                split_to(CHUNK_OF[job] + 3)
                copy_out(job, dst.rearrange("p k s -> p (k s)"), 0)
            for n in range(2):
                split_to(CHUNK_OF[f"bv{n}"] + 3)
                copy_out(f"bv{n}", vR[:, 0, n * NB:(n + 1) * NB], 0)

            def b_scores(n):
                job = f"bs{n}"
                units, width = (8, P) if n < 2 else (4, S)
                pr = bp[n % 4]
                wait_full(dve, job)
                if n == 0:
                    dve.wait_ge(bias_masked, 1)
                per = units // 2
                b0 = 4 * n if n < 2 else 2 * (n - 2)
                for g in range(2):
                    add = bias.rearrange("p (b g) m -> p g b m", g=2)[:, g, b0:b0 + per, 0:width]
                    dve.scalar_tensor_tensor(out=pr[:, g * NB:(g + 1) * NB].rearrange("p (u w) -> p u w", u=per),
                                             in0=bank(job, g).rearrange("p (u w) -> p u w", u=per), scalar=0.125,
                                             in1=add, op0=ALU.mult, op1=ALU.add).then_inc(psum_drained[pair(job)], 1)
                wait_drained(dve, job)
                m = small[:, 100 + 8 * (n % 2):100 + 8 * (n % 2) + units]
                link(dve.tensor_reduce(m, pr.rearrange("p (u w) -> p u w", u=units), AX, ALU.max))
                dve.tensor_scalar(m, m, -1.0, None, ALU.mult).then_inc(row_max, 1)

            def b_attended(n):
                job = f"bo{n}"
                wait_full(dve, job)
                b0, per, cols = (4 * n, 4, slice(0, P)) if n < 2 else (2 * (n - 2), 2, slice(P, S))
                src = bank(job, 0)[:, 0:per * P].rearrange("p (b s) -> p b s", b=per)
                high, low = (hT[i][:, b0:b0 + per, cols] for i in range(2))
                link(dve.tensor_copy(high, src))
                dve.tensor_tensor(low, src, high.bitcast(F32), ALU.subtract).then_inc(psum_drained[pair(job)], 1)

            def b_probs(n):
                units = 8 if n < 2 else 4
                dve.wait_ge(row_exp, n + 1)
                normalise(4 + n, bp[n % 4].rearrange("p (u w) -> p u w", u=units), units)

            def b_turned(n):
                copy_out(f"bT{n}", bpt[n % 2][:, 0:NB], 0)

            b_scores(0)
            b_scores(1)
            b_probs(0)
            b_scores(2)
            for n in range(6):
                b_turned(n)
                if n < 5:
                    b_probs(n + 1)
                if n < 3:
                    b_scores(n + 3)
                b_attended(n)
            split_to(C_FFN[1])
            after_product(2, "bm")
            turn_out(("nT5a", "nT5b"), vcol[:, V_GB2:V_GB2 + 8])
            split_to(C_FFN[1] + 1)
            mlp(1)
            after_mlp(3)

        @block.tensor
        def _(pe):
            mm = nc.tensor.matmul

            def begin(job):
                i = JOB_AT[job]
                if i >= 4:
                    pe.wait_ge(psum_drained[i % 4], DRAINED[i - 4])

            def end(ins, job):
                ins.then_inc(psum_full[pair(job)], 1)

            def turn(job, blocks):
                begin(job)
                for i, src in enumerate(blocks):
                    ins = nc.tensor.transpose(bank(job, i // 4)[:, (i % 4) * P:(i % 4 + 1) * P], src, ident)
                end(ins, job)

            def turn_rows(jobs, src):
                for half, job in enumerate(jobs):
                    turn(job, [src[:, t, k * P:(k + 1) * P] for k in range(4 * half, 4 * half + 4) for t in range(T)])

            def norm(n):
                for half, job in enumerate((f"nT{n}a", f"nT{n}b")):
                    pe.wait_ge(xn_ready[half], 2 * n + 2)
                    turn(job, [xn[:, t, k * P:(k + 1) * P] for k in range(4 * half, 4 * half + 4) for t in range(T)])

            def mm3(out, left, right, start, stop):
                mm(out, left[0], right[0], start=start, stop=False)
                mm(out, left[0], right[1], start=False, stop=False)
                return mm(out, left[1], right[0], start=False, stop=stop)

            def natural(job, act):
                begin(job)
                for half in range(2):
                    c = CHUNK_OF[job] + half
                    pe.wait_ge(chunk_low, c + 1)
                    k, w = chunk_shape(c)
                    for t in range(T):
                        for i in range(k):
                            ins = mm3(bank(job, t)[:, 0:w], [a[:, half * k + i, t * P:(t + 1) * P] for a in act],
                                      [part_of(c, j)[:, i, :] for j in range(2)],
                                      start=half == 0 and i == 0, stop=half == 1 and i == k - 1)
                    if half == 0:
                        ins.then_inc(half_done, 1)
                end(ins, job)

            def natural_by_tile(job, act):
                begin(job)
                c = CHUNK_OF[job]
                pe.wait_ge(chunk_low, c + 2)
                k, w = chunk_shape(c)
                for t in range(T):
                    for half in range(2):
                        for i in range(k):
                            ins = mm3(bank(job, t)[:, 0:w], [a[:, half * k + i, t * P:(t + 1) * P] for a in act],
                                      [part_of(c + half, j)[:, i, :] for j in range(2)],
                                      start=half == 0 and i == 0, stop=half == 1 and i == k - 1)
                        if half == 0 and t == 1:
                            ins.then_inc(half_done, 1)
                    if t == 0:
                        ins.then_inc(tile_full, 1)
                end(ins, job)

            def branch(job, act):
                begin(job)
                c = CHUNK_OF[job]
                pe.wait_ge(chunk_low, c + 1)
                for t in range(T):
                    for i in range(4):
                        ins = mm3(bank(job, t), [a[:, i, t * P:(t + 1) * P] for a in act],
                                  [part_of(c, j)[:, i, :] for j in range(2)], start=i == 0, stop=i == 3)
                end(ins, job)

            def turned(job, act):
                begin(job)
                for half in range(2):
                    c = CHUNK_OF[job] + half
                    pe.wait_ge(chunk_low, c + 1)
                    for b in range(2):
                        for i in range(KD):
                            ins = mm3(bank(job, half)[:, b * S:(b + 1) * S],
                                      [part_of(c, j)[:, i, b * P:(b + 1) * P] for j in range(2)],
                                      [a[:, i, :] for a in act], start=i == 0, stop=i == KD - 1)
                    if half == 0:
                        ins.then_inc(half_done, 1)
                end(ins, job)

            def ada_part(s):
                job, n = f"ada{s}", SLAB_AT[f"ada{s}"]
                begin(job)
                wait_slab(pe, n)
                for i in range(2):
                    for j in range(4):
                        ins = mm(PS[32 * j:32 * j + 32, 2 * pair(job), :], crep[:, 2 * j + i, :], kn(n)[:, 2 * j + i, :],
                                 start=i == 0, stop=i == 1)
                end(ins, job)

            def ada_col(s):
                job = f"adc{s}"
                begin(job)
                wait_drained(pe, f"ada{s}")
                for i in range(4):
                    ins = mm(bank(job, 0)[:, i:i + 1], (part2 if s >= 6 else part[:, s % 2, :])[:, i * P:(i + 1) * P],
                             mean32[:, 0:1],
                             start=True, stop=True)
                end(ins, job)

            def ada_row(s):
                job = f"adr{s}"
                begin(job)
                wait_drained(pe, f"ada{s}")
                end(mm(bank(job, 0), mean32[:, :], part[:, s % 2, :], start=True, stop=True), job)

            pe.wait_ge(consts_in, 16)
            pe.wait_ge(vrow_in, 16 * 8)
            pe.wait_ge(vrow_in2, 16 * 3)
            begin("vecT")
            end(nc.tensor.transpose(bank("vecT", 0)[:, 0:P], vrow[:, :], ident), "vecT")
            pe.wait_ge(crep_ready, 1)
            pe.wait_ge(filled, 2)
            ada_part(0)
            ada_part(1)
            ada_col(0)
            ada_part(2)
            ada_col(1)
            ada_part(3)
            ada_col(2)
            ada_col(3)
            norm(0)
            pe.wait_ge(low_out, 4)

            def W(i):
                job = f"W{i}"
                if i < 3:
                    turned(job, hT)
                else:
                    natural(job, hT)

            def level(lv):
                job = f"lv{lv}"
                begin(job)
                pe.wait_ge(factors_ready, lv + 1)
                queries = EQ if lv else gq
                if lv == 0:
                    wait_drained(pe, "W0")
                for t in range(T):
                    for h in range(HG):
                        qry = t if lv < LEVELS - 1 else 1 - t
                        ins = mm(bank(job, t)[:, h * P:(h + 1) * P], EK[:, h, t * P:(t + 1) * P],
                                 queries[:, h, qry * P:(qry + 1) * P], start=True, stop=True)
                end(ins, job)

            def a_scores(t, g):
                job = f"sc{t}{g}"
                begin(job)
                rows = slice(64 * g, 64 * g + 64)
                for i in range(4):
                    ins = mm(bank(job, i // 2)[:, (i % 2) * S:(i % 2 + 1) * S], aqT[rows, i, t * P:(t + 1) * P],
                             akT[rows, :], start=True, stop=True)
                end(ins, job)

            def a_values(t, g, n, between=lambda: None):
                pe.wait_ge(prob_ready, n + 1)
                turn(f"PT{t}{g}", [prob[n % 2][:, i, k * P:(k + 1) * P] for k in range(2) for i in range(4)])
                between()
                job = f"pv{t}{g}"
                begin(job)
                wait_drained(pe, f"PT{t}{g}")
                for k in range(2):
                    ins = mm(PS[64 * g:64 * g + 64, 2 * pair(job), :], va[:, k, 64 * g:64 * g + 64],
                             ptr[:, k].rearrange("p i s -> p (i s)"), start=k == 0, stop=k == 1)
                end(ins, job)

            W(1)
            W(2)
            W(0)
            level(0)
            W(4)
            level(1)
            W(5)
            level(2)
            W(3)
            level(3)
            ada_part(6)
            ada_col(6)
            pe.wait_ge(qk_ready[0], 1)
            pe.wait_ge(qk_ready[1], 1)
            turn("qT", [qk[:, t, i * P:(i + 1) * P] for i in range(4) for t in range(T)])
            turn("kT", [qk[:, t, 512:640] for t in range(T)])
            wait_drained(pe, "qT")
            wait_drained(pe, "kT")
            wait_drained(pe, "W5")
            a_scores(0, 0)
            a_scores(0, 1)
            level(4)
            W(6)
            a_values(0, 0, 0)
            a_values(0, 1, 1)
            level(5)
            a_scores(1, 0)
            a_scores(1, 1)
            ada_part(7)
            level(6)
            ada_col(7)
            a_values(1, 0, 2, lambda: ada_part(8))
            a_values(1, 1, 3, lambda: ada_col(8))
            level(7)
            ada_part(9)
            W(7)
            level(8)
            ada_col(9)
            ada_part(4)
            begin("og")
            for lv in (7, 8):
                wait_drained(pe, f"lv{lv}")
            for t in range(T):
                for h in range(HG):
                    for j in range(T):
                        ins = mm(bank("og", t)[:, h * HGD:(h + 1) * HGD], AT[:, j, t, h, :],
                                 gv[:, j, h * HGD:(h + 1) * HGD], start=j == 0, stop=j == 1)
            end(ins, "og")
            ada_part(5)
            W(8)
            ada_row(4)
            ada_row(5)
            pe.wait_ge(ohg_ready, 2)
            turn("ohgT", [ohg[:, t, i * P:(i + 1) * P] for i in range(4) for t in range(T)])
            W(9)
            W(10)
            pe.wait_ge(oatt_low, 1)
            for n in range(2):
                branch(f"ya{n}", oattR)
            wait_drained(pe, "ohgT")
            for n in range(2):
                branch(f"yh{n}", ohgR)
            ada_part(10)
            pe.wait_ge(merged_ready, 4)
            turn_rows(("mTa", "mTb"), merged)
            wait_drained(pe, "mTa")
            wait_drained(pe, "mTb")
            natural("mo0", hT)
            ada_row(10)
            ada_part(11)
            natural_by_tile("mo1", hT)
            ada_row(11)
            norm(1)
            pe.wait_ge(low_out, 8)
            pe.wait_ge(wr_in, 16)
            begin("rt")
            for i in range(4):
                for j in range(4):
                    k = 2 * j + i // 2
                    ins = mm(PS[32 * j:32 * j + 32, 2 * pair("rt"), 0:S], wr[:, k, :], hT[i % 2][:, k, :].bitcast(F32),
                             start=i == 0, stop=i == 3)
            end(ins, "rt")
            begin("rl")
            wait_drained(pe, "rt")
            for t in range(T):
                ins = mm(bank("rl", 0)[:, t * NE:(t + 1) * NE], logits[:, t * P:(t + 1) * P],
                         consts[:, C_SUM:C_SUM + NE], start=True, stop=True)
            end(ins, "rl")
            begin("aT")
            pe.wait_ge(r_ready, 1)
            for t in range(T):
                ins = nc.tensor.transpose(bank("aT", 0)[0:16, t * P:(t + 1) * P], eprob[:, t, :], ident)
            end(ins, "aT")
            begin("ic")
            pe.wait_ge(top_ready, 1)
            for a in range(2):
                ins = nc.tensor.transpose(bank("ic", 0)[:, a * NE:(a + 1) * NE],
                                          erep[0:16, a].rearrange("p j c -> p (j c)"), consts[0:16, C_ID:C_ID + 16])
            end(ins, "ic")
            begin("ib")
            end(mm(bank("ib", 0), mean32[0:16, :], ebd[0:16, :], start=True, stop=True), "ib")
            wait_drained(pe, "ib")
            pe.wait_ge(rows_low, 1)
            for q in range(4):
                job = f"ga{q}"
                begin(job)
                for b in range(2):
                    k = 2 * q + b
                    for t in range(T):
                        for i in range(2):
                            ins = mm(bank(job, b), xn_parts[i][:, t * D + k * P:t * D + (k + 1) * P], onehot[:, t, :],
                                     start=t == 0 and i == 0, stop=t == 1 and i == 1)
                end(ins, job)

            pe.wait_ge(ws_in, 16)
            turn("wsT", [ws[:, g, :] for g in range(8)])

            for q in range(4):
                wait_drained(pe, f"ga{q}")
            wait_drained(pe, "wsT")
            for b in range(4):
                mm(PS[:, 4 + b, :], zrow[0:1, 0:P], zrow[0:1, :], start=True, stop=False)

            with pe.Fori(0, NE) as e:
                def expert_slab(i):
                    n = AT_EXPERT + i
                    pe.wait_ge(slab_in[slot_of(n)], e * (16 * PER_EXPERT // R) + ARRIVED[n])

                pe.wait_ge(xe_ready, e + 1)
                for side in range(2):
                    for q in range(4):
                        i = 4 * side + q
                        expert_slab(i)
                        w = kn(AT_EXPERT + i, 2)
                        for kk in range(2):
                            for j in range(4):
                                ins = mm(PS[32 * j:32 * j + 32, side, :], xe[:, 2 * q + kk, :],
                                         w[:, kk, j * NB:(j + 1) * NB], start=q == 0 and kk == 0, stop=q == 3 and kk == 1)
                        ins.then_inc(slab_done, 1)
                pe.wait_ge(hid_ready, e + 1)
                for i in range(4):
                    ins = nc.tensor.transpose(PS[:, 0, i * P:(i + 1) * P], hid[:, i * P:(i + 1) * P], ident)
                ins.then_inc(hid_turned, 1)
                pe.wait_ge(hidT_ready, e + 1)
                for i in range(4):
                    expert_slab(8 + i)
                    w = kn(AT_EXPERT + 8 + i, 4)
                    for n in range(2):
                        for j in range(4):
                            ins = mm(PS[32 * j:32 * j + 32, 2 + n, :], hidT[:, i, 32 * j:32 * j + 32],
                                     w[:, j, n * NB:(n + 1) * NB], start=i == 0, stop=i == 3)
                    ins.then_inc(slab_done, 1)
                pe.wait_ge(ye_ready, 2 * e + 2)
                for t in range(T):
                    for n in range(2):
                        mm(PS[:, 4 + 2 * t + n, :], comb[:, t * P:(t + 1) * P], ye[:, n, :], start=False, stop=False)
            for b in range(4):
                ins = mm(PS[:, 4 + b, :], zrow[0:1, 0:P], zrow[0:1, :], start=False, stop=True)
            ins.then_inc(comb_done, 1)

            pe.wait_ge(x_ready, X_EXP)
            norm(2)
            wait_drained(pe, "nT2a")
            wait_drained(pe, "nT2b")
            for j in ("v0", "v1", "u0", "u1"):
                natural(j, hT)
            pe.wait_ge(ln_ready, 2)
            pe.wait_ge(wsT_ready, 1)
            for t in range(T):
                job = f"sv{t}"
                begin(job)
                for g in range(8):
                    ins = mm(bank(job, g // 4)[:, (g % 4) * P:(g % 4 + 1) * P], wsT[:, g, :],
                             V[:, t, g * P:(g + 1) * P], start=True, stop=True)
                end(ins, job)
            wait_drained(pe, "sv0")
            wait_drained(pe, "sv1")
            turn_rows(("pTa", "pTb"), U)
            wait_drained(pe, "pTa")
            wait_drained(pe, "pTb")
            natural("am0", hT)
            natural_by_tile("am1", hT)

            def mlp(layer):
                squares = layer * FJ
                for b in range(4):
                    mm(PS[:, b, :], zrow[0:1, 0:P], zrow[0:1, :], start=True, stop=False)

                c0 = C_FFN[layer]

                def chunk(i, turns):
                    c = c0 + i
                    pe.wait_ge(chunk_low, c + 1 if turns is None else turns * 12 + (c + 1))
                    return [part_of(c, j) for j in range(2)]

                def up(j, i, turns=None):
                    for half in range(2):
                        w = chunk(2 * i + half, turns)
                        if half == 0 and not (isinstance(j, int) and j == 0):
                            pe.wait_ge(relu_ready, j + squares)
                        for b in range(2):
                            for k in range(KD):
                                ins = mm3(PS[:, 4 + half, b * S:(b + 1) * S], [v[:, k, b * P:(b + 1) * P] for v in w],
                                          [a[:, k, :] for a in hT], start=k == 0, stop=k == KD - 1)
                        ins.then_inc(slab_done if half else half_done, 1)

                def down(j, i, b, turns=None):
                    pe.wait_ge(hidden_ready, j + (squares + 1))
                    for half in range(2):
                        w = chunk(2 * i + half, turns)
                        for t in range(T):
                            for h in range(2):
                                for k in range(2):
                                    ins = mm3(PS[:, 2 * t + h, :],
                                              [a[:, b, 2 * half + k, t * P:(t + 1) * P] for a in hidden],
                                              [v[:, k, h * NB:(h + 1) * NB] for v in w], start=False, stop=False)
                        ins.then_inc(slab_done if half else half_done, 1)

                up(0, 0)
                with pe.Fori(0, 2) as it:
                    for jj in range(1, 4):
                        up(it * 3 + jj, 2 * jj - 1, it)
                        down(it * 3 + (jj - 1), 2 * jj, (jj - 1) % 3, it)
                up(7, 13)
                down(6, 14, 0)
                pe.wait_ge(hidden_ready, squares + FJ)
                w = [chunk(30 + half, None) for half in range(2)]
                for t in range(T):
                    for half in range(2):
                        for h in range(2):
                            for k in range(2):
                                ins = mm3(PS[:, 2 * t + h, :],
                                          [a[:, 1, 2 * half + k, t * P:(t + 1) * P] for a in hidden],
                                          [v[:, k, h * NB:(h + 1) * NB] for v in w[half]],
                                          start=False, stop=half == 1 and k == 1)
                        if half == 0 and t == 1:
                            ins.then_inc(half_done, 1)
                    if t == 0:
                        ins.then_inc(tile_full, 1)
                ins.then_inc(slab_done, 1)

            norm(3)
            wait_drained(pe, "nT3a")
            wait_drained(pe, "nT3b")
            mlp(0)
            norm(4)
            pe.wait_ge(kv_low, 4)
            for j in ("bk0", "bk1"):
                turned(j, hR)
            wait_drained(pe, "nT4a")
            wait_drained(pe, "nT4b")
            for j in ("bq0", "bq1"):
                turned(j, hT)
            for j in ("bv0", "bv1"):
                natural(j, hR)

            def b_scores(n):
                job = f"bs{n}"
                begin(job)
                t, per, k0 = (0, 4, P) if n < 2 else (1, 2, 0)
                b0 = 4 * n if n < 2 else 2 * (n - 2)
                w = S - k0
                for g in range(2):
                    rows = slice(64 * g, 64 * g + 64)
                    for i in range(per):
                        ins = mm(bank(job, g)[:, i * w:(i + 1) * w], bqT[rows, b0 + i, t * P:(t + 1) * P],
                                 bkT[rows, b0 + i, k0:S], start=True, stop=True)
                end(ins, job)

            def b_turn(n):
                pe.wait_ge(prob_ready, 5 + n)
                turn(f"bT{n}", [bp[n % 4][:, i * P:(i + 1) * P] for i in range(8)])

            def b_values(n):
                job = f"bo{n}"
                begin(job)
                wait_drained(pe, f"bT{n}")
                per = 4 if n < 2 else 2
                b0 = 4 * n if n < 2 else 2 * (n - 2)
                for g in range(2):
                    for i in range(per):
                        h = 2 * (b0 + i) + g
                        for kb in ((1,) if n < 2 else (0, 1)):
                            blk = g * 4 + (i if n < 2 else 2 * i + kb)
                            ins = mm(PS[64 * g:64 * g + 64, 2 * pair(job), i * P:(i + 1) * P],
                                     vR[:, kb, h * BHD:(h + 1) * BHD], bpt[n % 2][:, blk * P:(blk + 1) * P],
                                     start=n < 2 or kb == 0, stop=n < 2 or kb == 1)
                end(ins, job)

            for j in ("bk0", "bk1", "bq0", "bq1"):
                wait_drained(pe, j)
            b_scores(0)
            b_scores(1)
            wait_drained(pe, "bv0")
            wait_drained(pe, "bv1")
            b_scores(2)
            for n in range(6):
                b_turn(n)
                if n < 3:
                    b_scores(n + 3)
                b_values(n)
            for n in range(6):
                wait_drained(pe, f"bo{n}")
            natural("bm0", hT)
            natural_by_tile("bm1", hT)
            norm(5)
            wait_drained(pe, "nT5a")
            wait_drained(pe, "nT5b")
            mlp(1)


_INS = ["x", "c", "ada_w", "ada_b", "norm_mix_w", "norm_ffn_w", "w_in", "q_norm_w", "k_norm_w", "hg_lower_bounds",
        "hg_norm_w", "w_branch_att", "w_branch_hg", "w_out", "w_router", "w_exp_gate", "w_exp_up", "w_exp_down",
        "norm_g_2", "a_w_in_2", "a_ln_g_2", "a_ln_b_2", "a_w_s_2", "a_b_s_2", "a_w_out_2", "kv_norm_g_2", "w_k_2",
        "w_v_2", "b_w_q_2", "b_rel_bias_2", "b_w_o_2", "w_up_2", "w_down_2"]


def constants():
    import numpy as np

    c = np.zeros((P, C_END), np.float32)
    i = np.arange(P)
    c[:, C_ID:C_ID + P] = np.eye(P)
    parted = i[:, None] ^ i[None, :]
    masks = np.concatenate([(parted >> lv) == 1 for lv in range(7)], axis=1).astype(np.int16)
    c[:, C_MASK:C_MASK + 7 * P // 2] = masks.view(np.float32)
    c[:, C_IOTA:C_IOTA + S] = np.arange(S)[None, :]
    for t in range(T):
        tok = t * P + i
        c[:, C_TOK + t] = tok
        inv = np.float32(10000.0) ** (-np.arange(0, 32, 2, dtype=np.float32) / np.float32(32))
        pos = np.stack([(tok // 64), (tok % 64)], axis=1).astype(np.float32)
        ang = (pos[:, :, None] * inv.astype(np.float32)).reshape(P, 32)
        c[:, C_ROPE + 64 * t:C_ROPE + 64 * t + 32] = np.cos(ang)
        c[:, C_ROPE + 64 * t + 32:C_ROPE + 64 * t + 64] = np.sin(ang)
    c[:, C_SUM:C_SUM + NE] = np.arange(P)[:, None] % 32 == np.arange(NE)[None, :]
    return c, np.repeat(np.eye(NE, dtype=np.float32) * 32, CAP, axis=1)


def kernel(**inputs):
    import numpy as _np
    import concourse.bacc as _bacc
    from concourse.bass_utils import run_bass_kernel_spmd as _run

    nc = _bacc.Bacc("TRN2", target_bir_lowering=False, num_devices=1)
    arrays, aps = {}, {}
    consts, blockdiag = constants()
    own = {"consts": consts, "blockdiag": blockdiag}
    for name in _INS + list(own):
        a = own[name] if name in own else _np.ascontiguousarray(inputs[name])
        arrays[f"in_{name}_dram"] = a
        aps[name] = nc.dram_tensor(f"in_{name}_dram", a.shape, mybir.dt.from_np(a.dtype), kind="ExternalInput").ap()
    out = nc.dram_tensor("out_0_dram", (1, S, D), F32, kind="ExternalOutput").ap()
    build(nc, aps, out)
    r = _run(nc, [arrays], core_ids=[0])
    return r.results[0]["out_0_dram"]
```
